# Optimizing a Trainium2 kernel written in Bass

```python
import jax, jax.numpy as jnp
from jax import lax
import numpy as np

D_MODEL = 1024
BATCH = 1
SEQ = 1024
DEPTH = 2
DEC_BATCH = 8
DEC_SEQ = 1
PAST_LEN = 2048
PAGE_SIZE = 128

N_EVEN = (DEPTH + 1) // 2
N_ODD = DEPTH // 2
C_CONV = D_MODEL // 2
CONV_W = 3
H_FOX = 8
HD_FOX = (D_MODEL // 2) // H_FOX
D_FOX = H_FOX * HD_FOX
H_GLA = 4
DK_GLA = (D_MODEL // 2) // H_GLA
DV_GLA = D_MODEL // H_GLA
GATE_RANK = 16
GLA_TAU = 16.0
GLA_CHUNK = 64
D_FF = 4 * D_MODEL
Q_BLOCK = 128
EPS = 1e-6

kernel_name = "hybrid_conv_fox_gla_decoder_step"

def rms_norm(x, gain):
    xf = x.astype(jnp.float32)
    y = xf * lax.rsqrt(jnp.mean(xf * xf, axis=-1, keepdims=True) + EPS)
    return (y * gain.astype(jnp.float32)).astype(x.dtype)

def adaln(c, w_ada, b_ada):
    mod = jax.nn.silu(c) @ w_ada + b_ada
    return jnp.split(mod[:, None, :], 6, axis=-1)

def modulate(h, shift, scale):
    return h * (1 + scale) + shift

def short_conv(u, prev, w_conv):
    L = u.shape[1]
    full = jnp.concatenate([prev.astype(u.dtype), u], axis=1)
    out = sum(full[:, j:j + L] * w_conv[j] for j in range(CONV_W))
    return out, full[:, -(CONV_W - 1):]

def fox_attend(q, k, v, f_q, f_k, q_pos, k_pos):
    s = jnp.einsum('bqhd,bkhd->bhqk', q, k, preferred_element_type=jnp.float32)
    s = s + jnp.swapaxes(f_q, 1, 2)[..., :, None] - jnp.swapaxes(f_k, 1, 2)[..., None, :]
    s = jnp.where(k_pos[None, :] <= q_pos[:, None], s, -1e30)
    p = jax.nn.softmax(s, axis=-1)
    return jnp.einsum('bhqk,bkhd->bqhd', p.astype(v.dtype), v)

def fox_prompt(q, k, v, f):
    B, L, H, Dh = q.shape
    nb = L // Q_BLOCK
    qb = q.reshape(B, nb, Q_BLOCK, H, Dh).transpose(1, 0, 2, 3, 4)
    fb = f.reshape(B, nb, Q_BLOCK, H).transpose(1, 0, 2, 3)
    k_pos = jnp.arange(L)

    def block(args):
        i, q_i, f_i = args
        q_pos = i * Q_BLOCK + jnp.arange(Q_BLOCK)
        return fox_attend(q_i, k, v, f_i, f, q_pos, k_pos)

    out = lax.map(block, (jnp.arange(nb), qb, fb))
    return out.transpose(1, 0, 2, 3, 4).reshape(B, L, H, Dh)

def even_mixer(h, w_in, b_f, g_q, g_k, w_conv, w_out, conv_prev, past):
    B, L, _ = h.shape
    idx = [C_CONV, 2 * C_CONV, 3 * C_CONV, 3 * C_CONV + D_FOX, 3 * C_CONV + 2 * D_FOX, 3 * C_CONV + 3 * D_FOX]
    gb, gc, xin, q, k, v, fz = jnp.split(h @ w_in, idx, axis=-1)
    conv_out, conv_new = short_conv(gc * xin, conv_prev, w_conv)
    y_a = gb * conv_out
    q = rms_norm(q.reshape(B, L, H_FOX, HD_FOX), g_q) * (HD_FOX ** -0.5)
    k = rms_norm(k.reshape(B, L, H_FOX, HD_FOX), g_k)
    v = v.reshape(B, L, H_FOX, HD_FOX)
    logf = jax.nn.log_sigmoid((fz + b_f).astype(jnp.float32))
    if past is None:
        o = fox_prompt(q, k, v, jnp.cumsum(logf, axis=1))
    else:
        k_past, v_past, lf_past = past
        P = k_past.shape[1]
        k_all = jnp.concatenate([k_past.astype(k.dtype), k], axis=1)
        v_all = jnp.concatenate([v_past.astype(v.dtype), v], axis=1)
        f_all = jnp.cumsum(jnp.concatenate([lf_past.astype(jnp.float32), logf], axis=1), axis=1)
        o = fox_attend(q, k_all, v_all, f_all[:, P:], f_all, P + jnp.arange(L), jnp.arange(P + L))
    y = jnp.concatenate([y_a, o.reshape(B, L, D_FOX)], axis=-1) @ w_out
    return y, conv_new, k, v, logf.astype(h.dtype)

def gla_recurrence(q, k, v, g, s0):
    B, L, H, _ = q.shape
    DV = v.shape[-1]
    C = GLA_CHUNK
    n = -(-L // C)
    padw = ((0, 0), (0, n * C - L), (0, 0), (0, 0))
    q, k, v, g = [jnp.pad(a, padw).reshape(B, n, C, H, a.shape[-1]) for a in (q, k, v, g)]
    b = jnp.cumsum(g, axis=2)
    b_last = b[:, :, -1:]
    q_e = q * jnp.exp(b)
    k_e = k * jnp.exp(-b)
    k_d = k * jnp.exp(b_last - b)
    causal = jnp.tril(jnp.ones((C, C), bool))
    a = jnp.where(causal, jnp.einsum('bnihk,bnjhk->bnhij', q_e, k_e), 0.0)
    o_intra = jnp.einsum('bnhij,bnjhv->bnihv', a, v)
    decay = jnp.exp(b_last[:, :, 0])

    def step(s, xs):
        q_c, k_c, v_c, d_c = xs
        o_c = jnp.einsum('bihk,bhkv->bihv', q_c, s)
        s = d_c[..., None] * s + jnp.einsum('bjhk,bjhv->bhkv', k_c, v_c)
        return s, o_c

    mv = lambda a: jnp.moveaxis(a, 1, 0)
    s_fin, o_inter = lax.scan(step, s0, (mv(q_e), mv(k_d), mv(v), mv(decay)))
    o = o_intra + jnp.moveaxis(o_inter, 0, 1)
    return o.reshape(B, n * C, H, DV)[:, :L], s_fin

def odd_mixer(h, w_in, w_gk, b_gk, g_o, w_out, s0):
    B, L, _ = h.shape
    QK = H_GLA * DK_GLA
    VV = H_GLA * DV_GLA
    q, k, v, r, gd = jnp.split(h @ w_in, [QK, 2 * QK, 2 * QK + VV, 2 * QK + 2 * VV], axis=-1)
    q = q.reshape(B, L, H_GLA, DK_GLA).astype(jnp.float32) * (DK_GLA ** -0.5)
    k = k.reshape(B, L, H_GLA, DK_GLA).astype(jnp.float32)
    v = v.reshape(B, L, H_GLA, DV_GLA).astype(jnp.float32)
    g = jax.nn.log_sigmoid((gd @ w_gk + b_gk).astype(jnp.float32)) / GLA_TAU
    g = g.reshape(B, L, H_GLA, DK_GLA)
    o, s_fin = gla_recurrence(q, k, v, g, s0.astype(jnp.float32))
    o = rms_norm(o, g_o).astype(h.dtype) * jax.nn.silu(r).reshape(B, L, H_GLA, DV_GLA)
    return o.reshape(B, L, VV) @ w_out, s_fin.astype(h.dtype)

def sq_relu_mlp(h, w1, w2):
    return jnp.square(jax.nn.relu(h @ w1)) @ w2

def setup_inputs(seed: int = 0) -> dict:
    key = jax.random.key(seed)
    ks = iter(jax.random.split(key, 32))
    nrm = lambda shape, s: jax.random.normal(next(ks), shape, jnp.float32) * s
    n_pages = PAST_LEN // PAGE_SIZE
    pool = (DEC_BATCH * n_pages * 5) // 4
    e_in = 3 * C_CONV + 3 * D_FOX + H_FOX
    o_in = 2 * H_GLA * DK_GLA + 2 * H_GLA * DV_GLA + GATE_RANK
    x_prompt = nrm((BATCH, SEQ, D_MODEL), 1.0)
    x_sample = nrm((DEC_BATCH, DEC_SEQ, D_MODEL), 1.0)
    c_prompt = nrm((BATCH, D_MODEL), 1.0)
    c_sample = nrm((DEC_BATCH, D_MODEL), 1.0)
    cache_k = nrm((pool, N_EVEN, PAGE_SIZE, H_FOX, HD_FOX), 1.0)
    cache_v = nrm((pool, N_EVEN, PAGE_SIZE, H_FOX, HD_FOX), 1.0)
    cache_logf = jax.nn.log_sigmoid(3.0 + nrm((pool, N_EVEN, PAGE_SIZE, H_FOX), 1.0))
    page_table = jax.random.permutation(next(ks), pool)[:DEC_BATCH * n_pages].reshape(DEC_BATCH, n_pages).astype(jnp.int32)
    state_conv = nrm((DEC_BATCH, N_EVEN, CONV_W - 1, C_CONV), 1.0)
    state_gla = nrm((DEC_BATCH, N_ODD, H_GLA, DK_GLA, DV_GLA), 1.0)
    g_mix = 1.0 + nrm((DEPTH, D_MODEL), 0.05)
    g_ffn = 1.0 + nrm((DEPTH, D_MODEL), 0.05)
    w_ada = nrm((DEPTH, D_MODEL, 6 * D_MODEL), 0.5 * D_MODEL ** -0.5)
    b_ada = nrm((DEPTH, 6 * D_MODEL), 0.01)
    w_in_even = nrm((N_EVEN, D_MODEL, e_in), D_MODEL ** -0.5)
    b_f = 1.0 + 4.0 * jax.random.uniform(next(ks), (N_EVEN, H_FOX), jnp.float32)
    g_q = 1.0 + nrm((N_EVEN, HD_FOX), 0.05)
    g_k = 1.0 + nrm((N_EVEN, HD_FOX), 0.05)
    w_conv = nrm((N_EVEN, CONV_W, C_CONV), CONV_W ** -0.5)
    w_out_even = nrm((N_EVEN, C_CONV + D_FOX, D_MODEL), (C_CONV + D_FOX) ** -0.5)
    w_in_odd = nrm((N_ODD, D_MODEL, o_in), D_MODEL ** -0.5)
    w_gk = nrm((N_ODD, GATE_RANK, H_GLA * DK_GLA), GATE_RANK ** -0.5)
    b_gk = nrm((N_ODD, H_GLA * DK_GLA), 0.01)
    g_o = 1.0 + nrm((N_ODD, DV_GLA), 0.05)
    w_out_odd = nrm((N_ODD, H_GLA * DV_GLA, D_MODEL), (H_GLA * DV_GLA) ** -0.5)
    w_ff1 = nrm((DEPTH, D_MODEL, D_FF), D_MODEL ** -0.5)
    w_ff2 = nrm((DEPTH, D_FF, D_MODEL), D_FF ** -0.5)
    return {"x_prompt": x_prompt, "x_sample": x_sample, "c_prompt": c_prompt, "c_sample": c_sample,
            "cache_k": cache_k, "cache_v": cache_v, "cache_logf": cache_logf, "page_table": page_table,
            "state_conv": state_conv, "state_gla": state_gla, "g_mix": g_mix, "g_ffn": g_ffn,
            "w_ada": w_ada, "b_ada": b_ada, "w_in_even": w_in_even, "b_f": b_f, "g_q": g_q, "g_k": g_k,
            "w_conv": w_conv, "w_out_even": w_out_even, "w_in_odd": w_in_odd, "w_gk": w_gk, "b_gk": b_gk,
            "g_o": g_o, "w_out_odd": w_out_odd, "w_ff1": w_ff1, "w_ff2": w_ff2}

def reference(x_prompt, x_sample, c_prompt, c_sample, cache_k, cache_v, cache_logf, page_table,
              state_conv, state_gla, g_mix, g_ffn, w_ada, b_ada, w_in_even, b_f, g_q, g_k,
              w_conv, w_out_even, w_in_odd, w_gk, b_gk, g_o, w_out_odd, w_ff1, w_ff2):
    n_seq, n_pages = page_table.shape
    past_len = n_pages * cache_k.shape[2]

    def gather(cache, e):
        rows = cache[page_table, e]
        return rows.reshape((n_seq, past_len) + rows.shape[3:])

    def run_group(x, c, conv_prev, gla_prev, fox_past):
        fox_rows, conv_new, gla_new = [], [], []
        for li in range(DEPTH):
            sh_m, sc_m, gt_m, sh_f, sc_f, gt_f = adaln(c, w_ada[li], b_ada[li])
            h = modulate(rms_norm(x, g_mix[li]), sh_m, sc_m)
            if li % 2 == 0:
                e = li // 2
                m, buf, k_rows, v_rows, lf_rows = even_mixer(
                    h, w_in_even[e], b_f[e], g_q[e], g_k[e], w_conv[e], w_out_even[e],
                    conv_prev(e), fox_past(e))
                fox_rows.append((k_rows, v_rows, lf_rows))
                conv_new.append(buf)
            else:
                o = li // 2
                m, s_fin = odd_mixer(h, w_in_odd[o], w_gk[o], b_gk[o], g_o[o], w_out_odd[o], gla_prev(o))
                gla_new.append(s_fin)
            x = x + gt_m * m
            h = modulate(rms_norm(x, g_ffn[li]), sh_f, sc_f)
            x = x + gt_f * sq_relu_mlp(h, w_ff1[li], w_ff2[li])
        k_new = jnp.stack([r[0] for r in fox_rows], axis=1)
        v_new = jnp.stack([r[1] for r in fox_rows], axis=1)
        lf_new = jnp.stack([r[2] for r in fox_rows], axis=1)
        return x, k_new, v_new, lf_new, jnp.stack(conv_new, axis=1), jnp.stack(gla_new, axis=1)

    bp = x_prompt.shape[0]
    y_p, k_p, v_p, lf_p, conv_p, gla_p = run_group(
        x_prompt, c_prompt,
        lambda e: jnp.zeros((bp, CONV_W - 1, C_CONV), x_prompt.dtype),
        lambda o: jnp.zeros((bp, H_GLA, DK_GLA, DV_GLA), jnp.float32),
        lambda e: None)
    y_s, k_s, v_s, lf_s, conv_s, gla_s = run_group(
        x_sample, c_sample,
        lambda e: state_conv[:, e],
        lambda o: state_gla[:, o],
        lambda e: (gather(cache_k, e), gather(cache_v, e), gather(cache_logf, e)))
    return (y_p, y_s, k_p, v_p, lf_p, k_s, v_s, lf_s, conv_p, conv_s, gla_p, gla_s)


_drawn_inputs = setup_inputs


def setup_inputs(seed=0):
    import zlib

    import numpy as np

    out = dict(_drawn_inputs(seed))
    spreads = {}
    factors = {'cache_logf': 5.151, 'g_q': 8.0, 'b_gk': 8.0, 'g_o': 5.716}
    for name, (base, spread) in spreads.items():
        noise = np.random.default_rng([zlib.crc32(name.encode()), seed]).standard_normal(out[name].shape)
        drawn = base * np.exp(spread * noise) if base else spread * noise
        out[name] = __import__('jax').numpy.asarray(drawn.astype(out[name].dtype))
    for name, factor in factors.items():
        out[name] = (out[name] * factor).astype(out[name].dtype)
    return out
```

```python
from contextlib import ExitStack

import concourse.bass as bass
from concourse import mybir

F32 = mybir.dt.float32
F32R = mybir.dt.float32r
BF16 = mybir.dt.bfloat16
I32 = mybir.dt.int32
U32 = mybir.dt.uint32
ALU = mybir.AluOpType
ACT = mybir.ActivationFunctionType
X = mybir.AxisListType.X
ds = bass.ds

P = 128
D = 1024
KT = D // P
SEQ = 1024
NB = SEQ // P
NS = 8
T = NS + SEQ
CH = T // 3
NC = NS + 1
DEPTH = 2
NH, HD = 8, 64
PAGES, PS = 16, 128
NG, DK, DV = 4, 128, 256
CHUNK = 64
NPAIR = 4096 // 256
EPS = 1e-6
NEG = -1e30


class V:

    def __init__(self, c, g=0, L=0):
        self.c, self.g, self.L = c, g, L
        self.v = c + g * L if L else c

    def plus(self, n):
        return V(self.c + n, self.g, self.L)

    def times(self, m):
        return V(self.c * m, self.g, self.L * m)

    @property
    def half(self):
        assert self.L % 2 == 0
        return V(self.c // 2, self.g, self.L // 2)

    @property
    def par(self):
        assert self.L % 2 == 0
        return self.c % 2


class Link:

    def __init__(self, eng, sem):
        self.eng, self.sem, self.n = eng, sem, V(0)

    def __call__(self, ins):
        self.n = self.n.plus(1)
        ins.then_inc(self.sem, 1)
        self.eng.wait_ge(self.sem, self.n.v)


def loop(eng, n, per, body, link=None, links=0, peel=0):
    for j in range(peel):
        body(V(j))
    n -= peel
    inner, body = body, lambda i: inner(i.plus(peel))
    full = n // per
    start = link.n if link else None
    if full > 1:
        with eng.Fori(0, full) as g:
            if link:
                link.n = V(start.c, g, per * links)
            for j in range(per):
                body(V(j, g, per))
            if link:
                assert link.n.c == start.c + per * links, (link.n.c - start.c, per)
        if link:
            link.n = V(start.c + full * per * links)
        done = full * per
    else:
        done = 0
    for j in range(done, n):
        body(V(j))


def build(nc, x_prompt, x_sample, c_prompt, c_sample, cache_k, cache_v, cache_logf, page_table, state_conv,
          state_gla, g_mix, g_ffn, w_ada, b_ada, w_in_even, b_f, g_q, g_k, w_conv, w_out_even, w_in_odd, w_gk,
          b_gk, g_o, w_out_odd, w_ff1, w_ff2,
          y_prompt, y_sample, k_prompt, v_prompt, logf_prompt, k_sample, v_sample, logf_sample, conv_prompt,
          conv_sample, gla_prompt, gla_sample):
    with ExitStack() as ctx:
        slab_start = (nc.sbuf_base + 31) // 32 * 32

        def at(name, shape, dt, offset):
            return nc.alloc_sbuf_tensor_at(name, shape, dt, offset=offset)

        def size(shape, dt):
            n = 2 if dt == BF16 else 4
            for s in shape[1:]:
                n *= s
            return (n + 31) // 32 * 32

        TILE = T * 4
        A0 = slab_start
        B0 = A0 + KT * TILE
        C0 = B0 + KT * TILE
        F0 = C0 + KT * TILE
        W0 = F0 + KT * TILE
        top = [W0]

        def put(name, shape, dt=F32):
            o = top[0]
            top[0] += size(shape, dt)
            return at(name, shape, dt, o)

        stage = put("stage", [P, 2, D])
        whi = put("whi", [P, 4, D], F32R)
        wlo = put("wlo", [P, 4, D], F32R)
        tmp = put("tmp", [P, 2, T])
        ident = put("ident", [P, P])
        ones = put("ones", [P, P])
        pairmask = put("pairmask", [P, P])
        eye8 = put("eye8", [P, 8, 8])
        vecT = put("vecT", [P, 144])
        modT = put("modT", [P, DEPTH, 48, NC])
        gain = put("gain", [P, 2 * DEPTH, KT, NC])
        eps = put("eps", [P, 1])
        t8 = put("t8", [P, NS])
        lay = top[0]
        tri = put("tri", [P, P])
        trisuf = put("trisuf", [P, P])
        later = put("later", [P, P])
        identb = put("identb", [P, P], BF16)
        negb = put("negb", [P, P], BF16)
        headrow = put("headrow", [8, NH, HD])
        gqb = put("gqb", [P, HD])
        gkb = put("gkb", [P, HD])
        bfb = put("bfb", [P, NH])
        sF = put("sF", [P, 13, NS])
        sNat = put("sNat", [NS, 3, 512])
        lf = put("lf", [P, NB + 1, NH])
        lft = put("lft", [P, NB + 1, NH])
        fcum = put("fcum", [P, NB, NH])
        prevT = put("prevT", [P, 4, 16])
        uOut = put("uOut", [P, 4, 10])
        rsq = put("rsq", [P, 2 * NB * NH + 16])
        only8 = put("only8", [8, 8])
        snew = put("snew", [8, 8])
        nmx = put("nmx", [P, 2])
        rsum = put("rsum", [P, 2])
        rinv = put("rinv", [P, 2])
        U = at("U", [P, T + 2], F32, top[0])
        QA = put("QA", [P, NB, HD + 2])
        KA = put("KA", [P, NB, HD + 2])
        Lraw = at("Lraw", [P, PS, NH], F32, top[0])
        Lsuf = put("Lsuf", [P, NH, P])
        sc = put("sc", [P, PAGES + 1, NH])
        PBx = put("PBx", [P, PAGES + 1, NH])
        idx = put("idx", [P, 1], I32)
        pt = put("pt", [1, P], I32)
        assert top[0] <= nc.sbuf_usable_end, top[0] - nc.sbuf_usable_end
        top[0] = lay
        gob = put("gob", [P, DV])
        wgk = put("wgk", [P, NG * DK])
        bcum = put("bcum", [P, T])
        qe = put("qe", [P, T])
        ke = put("ke", [P, T])
        scanm = put("scanm", [P, SEQ])
        S = put("S", [P, DV])
        kdn = put("kdn", [P, 2, P])
        aT = put("aT", [P, P])
        wgh = put("wgh", [P, P])
        dec = put("dec", [P, 16])
        dec_s = put("dec_s", [P, NG, NS])
        qks = put("qks", [P, 8, NS])
        vs_f = put("vs_f", [P, 8, NS])
        rs_f = put("rs_f", [P, 8, NS])
        ss1 = put("ss1", [P, 2])
        ss8 = put("ss8", [NS, NG])
        assert top[0] <= nc.sbuf_usable_end, top[0] - nc.sbuf_usable_end

        xT = at("xT", [P, KT, T], F32, A0)
        hh = at("hh", [P, KT, T], F32R, B0)
        hl = at("hl", [P, KT, T], F32R, C0)
        hid = [at(n, [P, 2, 2, T], F32R, F0 + i * 4 * TILE) for i, n in enumerate(("hid_hi", "hid_lo"))]
        ada = at("ada", [P, 4, KT, 512], F32, B0)
        xin = at("xin", [P, NB, D], F32, F0)
        vec1 = at("vec1", [P, P], F32, W0)
        vec2 = at("vec2", [16, P], F32, W0 + 512)
        c9 = at("c9", [NC, D], F32, W0 + 1024)
        c9e = at("c9e", [NC, D], F32, W0 + 1024 + 4096)
        xs = at("xs", [NS, D], F32, W0 + 1024 + 8192)
        sconv = at("sconv", [16, 512], F32, W0 + 1024 + 12288)
        scT = at("scT", [P, KT, NC], F32, W0 + 1024 + 12288 + 2048)
        rstd = at("rstd", [P, T], F32, F0)
        xstore = nc.dram_tensor("xstore", (P, KT * T), F32, kind="Internal").ap()
        QK = at("QK", [P, 2, NB, NH * HD], F32, A0)
        Vn = at("Vn", [P, NB, NH * HD], F32, F0)
        ya = at("ya", [P, 4, T], F32, F0 + 16384)
        sq8 = at("sq8", [NS, 2, 512], F32, C0)
        crow = at("crow", [10, 512], F32, C0 + 8192)
        sqs = at("sqs", [P, 2, NB, NH * HD], F32, B0)
        qT = at("qT", [HD + 2, SEQ], F32, B0)
        kT = at("kT", [HD + 2, SEQ], F32, B0 + 4096)
        Pm = at("Pm", [P, SEQ], F32, B0 + 8192)
        PT = at("PT", [P, SEQ], F32, B0 + 12288)
        onat = at("onat", [P, NB, P], F32, W0 - 0 + 8192 + 32768)
        LT = at("LT", [P, NH, P], F32, B0)
        TB = at("TB", [P, NH, P], F32, B0 + 4096)
        LN = at("LN", [8, NH, P], F32, B0 + 8192)
        ptot = at("ptot", [P, NH], F32, B0 + 12288)
        pages = at("pages", [P, 2, 4, 512], F32, C0)
        qsel = at("qsel", [8, 512], F32, B0)
        qbc = at("qbc", [P, 512], F32, B0 + 2048)
        osum = at("osum", [8, 512], F32, B0 + 4096)
        omask = at("omask", [8, 512], F32, B0 + 6144)
        mx8 = at("mx8", [P, 8], F32, B0 + 8192)
        small = at("small", [P, 64], F32, B0 + 8192 + 64)
        qk1 = at("qk1", [P, KT, T], F32, A0)
        Vo = at("Vo", [P, NB, D], F32, F0)
        sst = at("sst", [P, NS, DV], F32, B0)
        sout = at("sout", [P, NS, DV], F32, B0 + 8192)
        kmask = at("kmask", [NS, NS, P], F32, B0 + 16384)
        qmask = at("qmask", [P, NS, NS], F32, B0 + 20480)
        kvnat = at("kvnat", [NS, NG * DK + D], F32, B0 + 20736)
        osn = at("osn", [NS, D], F32, B0 + 26880)
        ynat = at("ynat", [P, NB, D], F32, F0)
        ysn = at("ysn", [NS, D], F32, B0)

        ps = ctx.enter_context(nc.psum_tensor("ps", [P, 8, 512], F32))

        def acc(par):
            return ps[:, 3 * par:3 * par + 3, 0:CH]

        def thirds(ap):
            return ap.rearrange("p (c n) -> p c n", c=3)

        def sem(name):
            return ctx.enter_context(nc.semaphore(name))

        consts_made = sem("consts_made")
        small_loaded = sem("small_loaded")
        x_loaded = sem("x_loaded")
        ada_loaded = [sem(f"ada_loaded{i}") for i in range(4)]
        w_loaded = [sem(f"w_loaded{i}") for i in range(2)]
        w_split = sem("w_split")
        acc_done = sem("acc_done")
        acc_free = [sem("acc_free0"), sem("acc_free1")]
        passed = sem("passed")
        pool_link = sem("pool_link")
        dve_link = sem("dve_link")
        act_link = sem("act_link")
        setup_pe = sem("setup_pe")
        setup_dve = sem("setup_dve")
        silu_pos = sem("silu_pos")
        ada_done = sem("ada_done")
        ada_kept = sem("ada_kept")
        xt_done = sem("xt_done")
        xt_kept = sem("xt_kept")
        sq_ready = sem("sq_ready")
        sq_summed = sem("sq_summed")
        rstd_ready = sem("rstd_ready")
        norm_scaled = sem("norm_scaled")
        norm_affine = sem("norm_affine")
        norm_hi = sem("norm_hi")
        h_ready = sem("h_ready")
        x_spilled = sem("x_spilled")
        x_back = sem("x_back")
        tmp_full = sem("tmp_full")
        nat_done = sem("nat_done")
        nat_kept = sem("nat_kept")
        relu_ready = sem("relu_ready")
        hid_squared = sem("hid_squared")
        hid_hi_ready = sem("hid_hi_ready")
        hid_ready = sem("hid_ready")
        x_done = sem("x_done")
        prep_pe = sem("prep_pe")
        prep_act = sem("prep_act")
        prep_dve = sem("prep_dve")
        kv_out = sem("kv_out")
        outs = sem("outs")
        a_built = sem("a_built")
        a_turned = sem("a_turned")
        a_q = sem("a_q")
        a_k = sem("a_k")
        a_s = sem("a_s")
        a_max = sem("a_max")
        a_p = sem("a_p")
        a_pt = sem("a_pt")
        a_ptk = sem("a_ptk")
        a_av = sem("a_av")
        a_o = sem("a_o")
        a_pair = sem("a_pair")
        a_pair_hi = sem("a_pair_hi")
        a_pair_lo = sem("a_pair_lo")
        lf_gathered = sem("lf_gathered")
        pages_in = [sem("pages_in0"), sem("pages_in1")]
        k_used = sem("k_used")
        v_used = sem("v_used")
        d_pe = sem("d_pe")
        d_act = sem("d_act")
        d_dve = sem("d_dve")
        y_hi = sem("y_hi")
        y_ready = sem("y_ready")
        g_pe = sem("g_pe")
        g_act = sem("g_act")
        g_dve = sem("g_dve")
        gb_a = sem("gb_a")
        gb_scores = sem("gb_scores")
        gb_kd = sem("gb_kd")
        gb_state = sem("gb_state")
        gb_inter = sem("gb_inter")
        gb_kv = sem("gb_kv")
        gb_rs = sem("gb_rs")
        gb_out = sem("gb_out")
        g_stored = sem("g_stored")
        gate_cleared = sem("gate_cleared")
        gate_loaded = sem("gate_loaded")
        r_exp = sem("r_exp")
        r_done = sem("r_done")
        s_act = sem("s_act")
        s_ss = sem("s_ss")
        s_out = sem("s_out")
        gla_stored = sem("gla_stored")
        y_s = sem("y_s")
        g_tr = sem("g_tr")
        g_trk = sem("g_trk")
        s_in = sem("s_in")
        s_pe = sem("s_pe")
        s_dve = sem("s_dve")
        y_turned = sem("y_turned")
        y_kept = sem("y_kept")

        block = ctx.enter_context(nc.Block())

        wie = w_in_even[0].rearrange("(k p) n -> p k n", p=P)
        woe = w_out_even[0].rearrange("(k p) n -> p k n", p=P)
        wio = w_in_odd[0].rearrange("(k p) n -> p k n", p=P)
        woo = w_out_odd[0].rearrange("(k p) n -> p k n", p=P)
        E_IN, O_IN = w_in_even.shape[2], w_in_odd.shape[2]

        U_IN, U_OUT, U_MLP = [0, 97], [25, 122], [33, 130]
        T_NORM, T_IN, T_OUT, T_MLP = [0, 34, 195, 229], [1, 196], [26, 221], [35, 230]
        N_UNITS = 194
        SMALL = 14

        def all_read(eng, t):
            eng.wait_ge(acc_free[0], (t + 1) // 2)
            eng.wait_ge(acc_free[1], t // 2)

        def done(t, nn):
            return t.plus(1 - nn).v

        @block.sync
        def _(sp):
            def small_load(dst, src):
                sp.dma_start(dst, src).then_inc(small_loaded, 16)

            small_load(vec1[0:96, :], b_ada.rearrange("l (n p) -> (l n) p", p=P))
            small_load(vec1[96:112, :], g_mix.rearrange("l (n p) -> (l n) p", p=P))
            small_load(vec1[112:128, :], g_ffn.rearrange("l (n p) -> (l n) p", p=P))
            small_load(vec2[0:12, :], w_conv[0].rearrange("j (c p) -> (j c) p", p=P))
            small_load(vec2[12:16, :], b_gk.rearrange("o (c p) -> (o c) p", p=P))
            small_load(c9[0:NS, :], c_sample)
            small_load(c9[NS:NC, :], c_prompt)
            small_load(xs[:, :], x_sample.rearrange("b s d -> (b s) d"))
            small_load(sconv[:, :], state_conv.rearrange("b e j c -> (b e j) c"))
            small_load(gqb[:, :], g_q.to_broadcast([P, HD]))
            small_load(gkb[:, :], g_k.to_broadcast([P, HD]))
            small_load(bfb[:, :], b_f.to_broadcast([P, NH]))
            small_load(idx[:, :], page_table.rearrange("b (p o) -> (b p) o", o=1))
            small_load(pt[:, :], page_table.rearrange("(o b) p -> o (b p)", o=1))
            for b in range(NB):
                sp.dma_start(xin[:, b, :], x_prompt[0, b * P:(b + 1) * P, :]).then_inc(x_loaded, 16)

            def load_ada(i, l):
                if l or i.c >= 4 or i.L:
                    sp.wait_ge(ada_done, i.plus(12 * l - 3).v)
                sp.dma_start(ada[:, i.c % 4, :, :],
                             w_ada[l].rearrange("(k p) n -> p k n", p=P)[:, :, ds(i.times(512).v, 512)]
                             ).then_inc(ada_loaded[i.c % 4], 16)

            for l in range(DEPTH):
                loop(sp, 12, 4, lambda i: load_ada(i, l), peel=4)

            def load_unit(u, src):
                if u.c >= 2 or u.L:
                    sp.wait_ge(w_split, u.plus(-1).v)
                sp.sem_inc(passed, 1)
                dst = stage[:, u.c % 2, :]
                if len(src.shape) == 3:
                    dst = dst.rearrange("p (k n) -> p k n", n=P)
                sp.dma_start(dst, src).then_inc(w_loaded[u.par], 16)

            def in_units(base, w, col, n, per=4):
                loop(sp, n, per, lambda i: load_unit(i.plus(base), w[:, :, ds(i.times(P).plus(col).v, P)]), peel=2)

            def mlp_units(l):
                base = U_MLP[l]
                w1 = w_ff1[l].rearrange("(k p) n -> p k n", p=P)
                w2 = w_ff2[l].rearrange("(r p) n -> p r n", p=P)

                def up(i, u):
                    for j in range(2):
                        load_unit(u.plus(j), w1[:, :, ds(i.times(256).plus(128 * j).v, P)])

                def down(i, u):
                    for j in range(2):
                        load_unit(u.plus(j), w2[:, ds(i.times(2).plus(j).v, 1), :].rearrange("p r n -> p (r n)"))

                def step(i):
                    up(i.plus(1), i.times(4).plus(base + 2))
                    down(i, i.times(4).plus(base + 4))

                up(V(0), V(base))
                loop(sp, NPAIR - 1, 1, step)
                down(V(NPAIR - 1), V(base + 62))

            sp.wait_ge(ada_done, 24)
            sp.wait_ge(setup_dve, 4)
            in_units(U_IN[0], wie, 1536, 12)

            def conv_units(c):
                for j, col in enumerate((512, 1024, 0)):
                    load_unit(c.times(3).plus(U_IN[0] + 12 + j), wie[:, :, ds(c.times(P).plus(col).v, P)])
            loop(sp, 4, 2, conv_units)
            load_unit(V(U_IN[0] + 24), wie[:, :, E_IN - P:E_IN])
            load_unit(V(U_OUT[0]), woe[:, :, 0:P])
            load_unit(V(U_OUT[0] + 1), woe[:, :, P:2 * P])
            sp.wait_ge(prep_dve, 6)
            tok = "(b p) h d -> p b (h d)"
            for dst, src in ((k_prompt[0, 0].rearrange(tok, p=P), QK[:, 1]), (v_prompt[0, 0].rearrange(tok, p=P), Vn[:, :, :]),
                             (logf_prompt[0, 0].rearrange("(b p) h -> p b h", p=P), lf[:, 0:NB, :]),
                             (k_sample.rearrange("b e s h d -> (b e s) (h d)"), sNat[:, 1, :]),
                             (v_sample.rearrange("b e s h d -> (b e s) (h d)"), sNat[:, 2, :]),
                             (logf_sample.rearrange("b e s h -> (b e s) h"), lf[0:NS, NB, :])):
                sp.dma_start(dst, src).then_inc(kv_out, 16)
            cs = conv_sample.rearrange("b e j c -> (b e) j c")
            sp.dma_start(cs[:, 0, :], state_conv.rearrange("b e j c -> (b e) j c")[:, 1, :]).then_inc(kv_out, 16)
            sp.dma_start(cs[:, 1, :], crow[0:NS, :]).then_inc(kv_out, 16)
            sp.dma_start(conv_prompt[0, 0], crow[NS:10, :]).then_inc(kv_out, 16)

            def load_pages(b):
                for j in range(8):
                    cache = cache_k if j < 4 else cache_v
                    m = j % 2
                    if j < 2:
                        if b.c == 0 and not b.L:
                            sp.wait_ge(a_pair_lo, NH // 2)
                        else:
                            sp.wait_ge(v_used, b.times(4).plus(j - 1).v)
                    elif j < 6:
                        sp.wait_ge(k_used, b.times(4).plus(j - 1).v)
                    else:
                        sp.wait_ge(v_used, b.times(4).plus(j - 5).v)
                    sp.sem_inc(passed, 1)
                    for q in range(4):
                        page = sp.value_load(pt[0:1, ds(b.times(PAGES).plus(4 * (j % 4) + q).v, 1)],
                                             min_val=0, max_val=cache_k.shape[0] - 1)
                        sp.dma_start(pages[:, m, q, :], cache[ds(page, 1), 0].rearrange("a p h d -> (a p) (h d)")
                                     ).then_inc(pages_in[m], 16)
            load_pages(V(0))
            loop(sp, NS - 1, 1, lambda b: load_pages(b.plus(1)))

            sp.wait_ge(x_spilled, 16)
            sp.wait_ge(kv_out, 16 * 9)
            sp.wait_ge(a_built, NH)
            sp.dma_start(xT[:, :, :], xstore.rearrange("p (k n) -> p k n", k=KT)).then_inc(x_back, 16)
            in_units(U_OUT[0] + 2, woe, 256, 6)
            mlp_units(0)

            sp.wait_ge(gate_cleared, 1)
            sp.dma_start(gob[:, :], g_o.to_broadcast([P, DV])).then_inc(gate_loaded, 16)
            sp.dma_start(wgk[P - 16:P, :], w_gk[0]).then_inc(gate_loaded, 16)
            in_units(U_IN[1], wio, 0, 16)
            load_unit(V(U_IN[1] + 16), wio[:, :, O_IN - P:O_IN])
            in_units(U_IN[1] + 17, wio, 2048, 8)
            sp.wait_ge(x_spilled, 32)
            for h in range(NG):
                if h:
                    sp.wait_ge(s_dve, 10 * h)
                else:
                    all_read(sp, T_IN[1] + 25)
                sp.dma_start(sst[:, :, :], state_gla[:, 0, h].rearrange("b k v -> k b v")).then_inc(s_in, 16)
                sp.wait_ge(s_dve, 10 * h + 10)
                sp.dma_start(gla_sample[:, 0, h].rearrange("b k v -> k b v"), sout[:, :, :]).then_inc(gla_stored, 16)
            load_unit(V(U_OUT[1]), woo[:, :, 0:P])
            load_unit(V(U_OUT[1] + 1), woo[:, :, P:2 * P])
            sp.wait_ge(y_ready, 2 * KT)
            sp.dma_start(xT[:, :, :], xstore.rearrange("p (k n) -> p k n", k=KT)).then_inc(x_back, 16)
            in_units(U_OUT[1] + 2, woo, 256, 6)
            mlp_units(1)
            for b in range(NB):
                sp.wait_ge(y_kept, b + 1)
                sp.dma_start(y_prompt[0, b * P:(b + 1) * P, :], ynat[:, b, :]).then_inc(outs, 16)
            sp.wait_ge(y_kept, NB + 1)
            sp.dma_start(y_sample.rearrange("b s d -> (b s) d"), ysn[:, :]).then_inc(outs, 16)
            sp.wait_ge(outs, 16 * (NB + 1))
            sp.wait_ge(gla_stored, 16 * NG)

        used_at = {}
        for l in range(DEPTH):
            nn = 2 * l + 1
            for i in range(25):
                used_at[U_IN[l] + i] = T_IN[l] - nn + i + 1
            for i in range(8):
                used_at[U_OUT[l] + i] = T_OUT[l] - nn + i + 1
            nn += 1
            for j in range(2):
                used_at[U_MLP[l] + j] = T_MLP[l] - nn + j + 1
            for i in range(NPAIR):
                if i < NPAIR - 1:
                    for j in range(2):
                        used_at[U_MLP[l] + 2 + 4 * i + j] = T_MLP[l] - nn + 10 * i + 2 + j + 1
                last = i < NPAIR - 1
                for j in range(2):
                    used_at[U_MLP[l] + (4 if last else 2) + 4 * i + j] = T_MLP[l] - nn + 10 * i + (12 if last else 10)

        @block.gpsimd
        def _(pool):
            link = Link(pool, pool_link)

            def select(t, cmp, fill, base, pattern, mult):
                link(pool.affine_select(out=t, in_=t, compare_op=cmp, fill=fill, base=base, pattern=pattern,
                                        channel_multiplier=mult))

            for t, v in ((ident, 0.0), (ones, 1.0), (tri, 1.0), (trisuf, 1.0), (later, 1.0), (pairmask, 1.0),
                         (eye8, 0.0), (headrow, 0.0), (only8, 0.0), (identb, 0.0), (negb, 0.0), (eps, EPS)):
                link(pool.memset(t[tuple(slice(None) for _ in t.shape)], v))
            select(ident[:, :], ALU.not_equal, 1.0, 0, [[-1, P]], 1)
            select(identb[:, :], ALU.not_equal, 1.0, 0, [[-1, P]], 1)
            select(tri[:, :], ALU.is_ge, 0.0, 0, [[1, P]], -1)
            select(trisuf[:, :], ALU.is_ge, 0.0, -1, [[-1, P]], 1)
            select(later[:, :], ALU.is_ge, 0.0, -1, [[-1, P]], 1)
            select(later[:, :].rearrange("p (b g) -> p b g", g=PAGES), ALU.is_ge, 0.0, PAGES - 1,
                   [[PAGES, NS], [0, PAGES]], -1)
            select(pairmask[:, :], ALU.is_ge, 0.0, 0, [[1, P]], -1)
            select(pairmask[:, :].rearrange("p (c r) -> p c r", r=CHUNK), ALU.is_ge, 0.0, 0,
                   [[-CHUNK, 2], [0, CHUNK]], 1)
            select(eye8[:, :, :], ALU.not_equal, 1.0, 0, [[1, 8], [-1, 8]], 0)
            select(headrow[:, :, :], ALU.not_equal, 1.0, 0, [[-1, NH], [0, HD]], 1)
            select(only8[:, :], ALU.is_equal, NEG, 0, [[-1, 8]], 1)
            pool.affine_select(out=negb[:, :], in_=negb[:, :], compare_op=ALU.is_ge, fill=NEG, base=0,
                               pattern=[[-1, P]], channel_multiplier=1).then_inc(consts_made, 1)
            pool.wait_ge(small_loaded, 16 * SMALL)
            pool.indirect_dma_start(Lraw[:, :, :].rearrange("p s h -> p (s h)"), None,
                                    cache_logf.rearrange("a e s h -> (a e) (s h)"),
                                    bass.IndirectOffsetOnAxis(ap=idx[:, 0:1].bitcast(U32), axis=0)
                                    ).then_inc(lf_gathered, 16)

            def split(u, used=None):
                if used is None and u.c >= 4:
                    used = V(used_at[u.c - 4])
                if used is not None:
                    pool.wait_ge(acc_done, used.v)
                pool.wait_ge(w_loaded[u.par], u.half.times(16).plus(16).v)
                pool.sem_inc(passed, 1)
                link(pool.tensor_copy(whi[:, u.c % 4, :], stage[:, u.c % 2, :]))
                pool.tensor_tensor(wlo[:, u.c % 4, :], stage[:, u.c % 2, :], whi[:, u.c % 4, :].bitcast(F32),
                                   ALU.subtract).then_inc(w_split, 1)

            def in_split(base, first, n):
                loop(pool, n, 4, lambda i: split(i.plus(base + first), i.plus(used_at[base + first - 4])
                                                 if first >= 4 else None), link, 1)

            for l in range(DEPTH):
                for i in range(4):
                    split(V(U_IN[l] + i))
                in_split(U_IN[l], 4, 20)
                split(V(U_IN[l] + 24))
                for i in range(8):
                    split(V(U_OUT[l] + i))
                for i in range(6):
                    split(V(U_MLP[l] + i))
                base, done = U_MLP[l], T_MLP[l] - 2 * l - 2

                def step(i):
                    for j in range(2):
                        split(i.times(4).plus(base + 2 + j), i.times(10).plus(done - 8 + j + 1))
                    for j in range(2):
                        split(i.times(4).plus(base + 4 + j), i.times(10).plus(done + 2))
                loop(pool, NPAIR - 2, 1, lambda i: step(i.plus(1)), link, 4)
                for j in range(2):
                    split(V(U_MLP[l] + 62 + j))

        @block.tensor
        def _(pe):
            def turn(out, in_):
                k = in_.shape[0]
                return pe.transpose(out, in_, ident[0:k, 0:k])

            def acc_wait(t):
                if t.c >= 2 or t.L:
                    pe.wait_ge(acc_free[t.par], t.half.v)

            def product(t, parts):
                acc_wait(t)
                n = len(parts)
                for k, (wh, wl, xh, xl) in enumerate(parts):
                    for q, (w, x) in enumerate(((wh, xh), (wh, xl), (wl, xh))):
                        for c in range(3):
                            last = pe.matmul(ps[:, 3 * t.par + c, 0:CH], w, x[:, c * CH:(c + 1) * CH],
                                             start=(k == 0 and q == 0), stop=(k == n - 1 and q == 2))
                last.then_inc(acc_done, 1)

            def gemm(u, t):
                pe.wait_ge(w_split, u.plus(1).v)
                s = u.c % 4
                product(t, [(whi[:, s, k * P:(k + 1) * P], wlo[:, s, k * P:(k + 1) * P], hh[:, k, :], hl[:, k, :])
                            for k in range(KT)])

            def norm(n):
                t = V(T_NORM[n])
                acc_wait(t)
                for k in range(KT):
                    pe.wait_ge(sq_ready, KT * n + k + 1)
                    for c in range(3):
                        last = pe.matmul(ps[:, 3 * t.par + c, 0:CH], ones[:, :], tmp[:, k % 2, c * CH:(c + 1) * CH],
                                         start=(k == 0), stop=(k == KT - 1))
                    last.then_inc(sq_summed, 1)

            def to_tokens(i):
                pe.wait_ge(tmp_full, i.plus(1).v)
                if i.c or i.L:
                    pe.wait_ge(nat_kept, i.v)
                for b in range(NB):
                    last = turn(ps[:, 6 + b // 4, (b % 4) * P:(b % 4 + 1) * P],
                                tmp[:, i.c % 2, NS + b * P:NS + (b + 1) * P])
                last.then_inc(nat_done, 1)

            def mlp(l):
                u0, t0 = U_MLP[l], T_MLP[l]

                def up(i, u, t):
                    for j in range(2):
                        gemm(u.plus(j), t.plus(j))

                def down(i, u, t):
                    pe.wait_ge(w_split, u.plus(2).v)
                    pe.wait_ge(hid_ready, i.times(2).plus(2 * NPAIR * l + 2).v)
                    for f in range(KT):
                        product(t.plus(f), [(whi[:, (u.c + j) % 4, f * P:(f + 1) * P],
                                             wlo[:, (u.c + j) % 4, f * P:(f + 1) * P],
                                             hid[0][:, i.c % 2, j, :], hid[1][:, i.c % 2, j, :]) for j in range(2)])

                def step(i):
                    up(i.plus(1), i.times(4).plus(u0 + 2), i.times(10).plus(t0 + 2))
                    down(i, i.times(4).plus(u0 + 4), i.times(10).plus(t0 + 4))
                up(V(0), V(u0), V(t0))
                loop(pe, NPAIR - 1, 2, step, peel=1)
                down(V(NPAIR - 1), V(u0 + 62), V(t0 + 152))

            def out_proj(l):
                pe.wait_ge(y_ready, KT * (l + 1))
                loop(pe, KT, 4, lambda i: gemm(i.plus(U_OUT[l]), i.plus(T_OUT[l])))

            pe.wait_ge(consts_made, 1)
            pe.wait_ge(small_loaded, 16 * SMALL)
            turn(ps[:, 0, 0:P], vec1[:, :])
            turn(ps[:, 0, P:P + 16], vec2[:, :])
            for c in range(4):
                turn(ps[:, 0, 256 + 16 * c:272 + 16 * c], sconv[:, c * P:(c + 1) * P])
            for k in range(KT):
                last = turn(ps[:, 1, NS * k:NS * k + NS], xs[:, k * P:(k + 1) * P])
            last.then_inc(setup_pe, 1)
            pe.wait_ge(setup_dve, 2)
            for k in range(KT):
                last = turn(ps[:, 1, P + NC * k:P + NC * (k + 1)], c9[:, k * P:(k + 1) * P])
            last.then_inc(setup_pe, 1)
            pe.wait_ge(x_loaded, 16 * NB)
            for k in range(KT):
                if k >= 2:
                    pe.wait_ge(xt_kept, k - 1)
                for b in range(NB):
                    last = turn(ps[:, 2 + 2 * (k % 2) + b // 4, (b % 4) * P:(b % 4 + 1) * P],
                                xin[:, b, k * P:(k + 1) * P])
                last.then_inc(xt_done, 1)
            pe.wait_ge(setup_dve, 3)

            def modulation(i):
                pe.wait_ge(ada_loaded[i.c % 4], V(i.c // 4, i.g, i.L // 4).times(16).plus(16).v)
                if i.c >= 2 or i.L:
                    pe.wait_ge(ada_kept, i.plus(-1).v)
                for f in range(4):
                    for k in range(KT):
                        last = pe.matmul(ps[:, 6 + i.c % 2, NC * f:NC * (f + 1)], ada[:, i.c % 4, k, f * P:(f + 1) * P],
                                         scT[:, k, :], start=(k == 0), stop=(k == KT - 1))
                last.then_inc(ada_done, 1)
            loop(pe, 24, 4, modulation, peel=4)

            norm(0)
            pe.wait_ge(h_ready, KT)
            gemm(V(U_IN[0]), V(T_IN[0]))

            def natural(i):
                gemm(i.plus(U_IN[0] + 1), i.plus(T_IN[0] + 1))
                to_tokens(i)
            loop(pe, 11, 4, natural, peel=3)
            gemm(V(U_IN[0] + 12), V(T_IN[0] + 12))
            to_tokens(V(11))
            loop(pe, 12, 4, lambda i: gemm(i.plus(U_IN[0] + 13), i.plus(T_IN[0] + 13)))
            to_tokens(V(12))
            all_read(pe, T_IN[0] + 25)
            for i in range(12):
                turn(ps[0:NS, i // 4, (i % 4) * P:(i % 4 + 1) * P], sF[:, i, :])
            turn(ps[0:NS, 3, 0:P], sF[:, 12, :])
            for c in range(4):
                last = turn(ps[0:10, 4, c * P:(c + 1) * P], uOut[:, c, :])
            last.then_inc(prep_pe, 1)
            pe.wait_ge(prep_dve, 5)
            for b in range(NB):
                for j in range(b):
                    pe.matmul(ps[:, 5, NH * b:NH * (b + 1)], ones[:, :], lf[:, j, :], start=(j == 0), stop=False)
                last = pe.matmul(ps[:, 5, NH * b:NH * (b + 1)], tri[:, :], lf[:, b, :], start=(b == 0), stop=True)
            last.then_inc(prep_pe, 1)

            def head(h, odd):
                n = h.times(NB)
                pe.wait_ge(a_built, h.plus(1).v)
                if h.c or h.L:
                    pe.wait_ge(a_ptk, n.v)
                    pe.wait_ge(a_o, n.v)
                    pe.wait_ge(a_p, n.v)
                if not odd and (h.c or h.L):
                    pe.wait_ge(a_pair_lo, V(h.c // 2, h.g, h.L // 2).v)
                for b in range(NB):
                    last = turn(ps[0:HD + 2, b // 4, (b % 4) * P:(b % 4 + 1) * P], QA[:, b, :])
                last.then_inc(a_turned, 1)
                for b in range(NB):
                    last = turn(ps[0:HD + 2, 2 + b // 4, (b % 4) * P:(b % 4 + 1) * P], KA[:, b, :])
                last.then_inc(a_turned, 1)
                pe.wait_ge(a_q, h.plus(1).v)
                pe.wait_ge(a_k, h.plus(1).v)

                def scores(i):
                    if i > 1:
                        pe.wait_ge(a_p, n.plus(i - 1).v)
                    bank = 4 + 2 * (i % 2)
                    q = qT[:, i * P:(i + 1) * P]
                    if i >= 4:
                        pe.matmul(ps[:, bank, :], q, kT[:, 0:512], start=True, stop=True)
                    lo = 4 * (i // 4)
                    w = (i - lo + 1) * P
                    pe.matmul(ps[:, bank + i // 4, 0:w], q, kT[:, lo * P:lo * P + w], start=True, stop=False)
                    pe.matmul(ps[:, bank + i // 4, w - P:w], identb[:, :], negb[:, :], start=False, stop=True
                              ).then_inc(a_s, 1)

                scores(0)
                for i in range(NB):
                    if i + 1 < NB:
                        scores(i + 1)
                    pe.wait_ge(a_p, n.plus(i + 1).v)
                    if i:
                        pe.wait_ge(a_ptk, n.plus(i).v)
                    for j in range(i + 1):
                        last = turn(ps[:, j // 4, (j % 4) * P:(j % 4 + 1) * P], Pm[:, j * P:(j + 1) * P])
                    last.then_inc(a_pt, 1)
                    pe.wait_ge(a_ptk, n.plus(i + 1).v)
                    if i >= 2:
                        pe.wait_ge(a_o, n.plus(i - 1).v)
                    for j in range(i + 1):
                        last = pe.matmul(ps[:, 2 + i % 2, 0:HD], PT[:, j * P:(j + 1) * P],
                                         Vn[:, j, ds(h.times(HD).v, HD)], start=(j == 0), stop=(j == i))
                    last.then_inc(a_av, 1)

            def pair(p):
                for e in range(2):
                    head(p.times(2).plus(e), e)
                pe.wait_ge(a_o, p.times(2 * NB).plus(2 * NB).v)
                for b in range(NB):
                    last = turn(ps[:, b // 4, (b % 4) * P:(b % 4 + 1) * P], onat[:, b, :])
                last.then_inc(a_pair, 1)
            pe.wait_ge(prep_dve, 6)
            loop(pe, NH // 2, 1, pair, peel=1)

            pe.wait_ge(lf_gathered, 16)
            pe.wait_ge(a_pair_lo, NH // 2)
            for h in range(NH):
                last = turn(ps[:, 2 + h // 4, (h % 4) * P:(h % 4 + 1) * P], Lraw[:, :, h])
            last.then_inc(d_pe, 1)
            pe.wait_ge(d_dve, 1)
            for h in range(NH):
                o = ps[:, 4 + h // 4, (h % 4) * P:(h % 4 + 1) * P]
                pe.matmul(o, trisuf[:, :], LT[:, h, :], start=True, stop=False)
                pe.matmul(o, TB[:, h, :], later[:, :], start=False, stop=False)
                last = pe.matmul(o.rearrange("p (b g) -> p b g", g=PAGES), LN[:, h, :],
                                 ident[0:NS, 0:NS].unsqueeze(2).to_broadcast([NS, NS, PAGES]), start=False, stop=True)
            last.then_inc(d_pe, 1)

            def sequence(b):
                g = b.times(7).plus(2)
                pe.wait_ge(d_dve, g.plus(1).v)
                pe.matmul(ps[:, 0, :], ones[0:NS, :], qsel[:, :], start=True, stop=True).then_inc(d_pe, 1)
                pe.wait_ge(d_dve, g.plus(2).v)
                turn(ps[0:8, 1, 0:P], mx8[:, :]).then_inc(d_pe, 1)
                pe.wait_ge(d_dve, g.plus(3).v)
                pe.matmul(ps[:, 2, 0:8], ones[0:8, :], small[0:8, 8:16], start=True, stop=True).then_inc(d_pe, 1)
                pe.wait_ge(d_dve, g.plus(5).v)
                pe.wait_ge(d_act, b.times(2).plus(2).v)
                for j in range(4):
                    pe.wait_ge(pages_in[j % 2], b.times(256).plus(64 * (3 + j // 2)).v)
                    for q in range(4):
                        last = pe.matmul(ps[0:8, 3, :], PBx[:, 4 * j + q, :], pages[:, j % 2, q, :],
                                         start=(j == 0 and q == 0), stop=False)
                    last.then_inc(v_used, 1)
                pe.matmul(ps[0:8, 3, :], PBx[0:NS, PAGES, :], sNat[:, 2, :], start=False, stop=True)
                pe.matmul(ps[0:8, 2, 128:129], small[:, 16:24], ones[:, 0:1], start=True, stop=True).then_inc(d_pe, 1)
                pe.wait_ge(d_dve, g.plus(6).v)
                pe.sem_inc(passed, 1)
                pe.matmul(ps[0:8, 4, :], small[0:8, 24:32], omask[:, :], start=True, stop=True).then_inc(d_pe, 1)
            pe.wait_ge(d_dve, 2)
            loop(pe, NS, 1, sequence)
            pe.wait_ge(d_dve, 2 + 7 * NS)
            for c in range(4):
                last = turn(ps[:, 5, NS * c:NS * (c + 1)], osum[:, c * P:(c + 1) * P])
            last.then_inc(d_pe, 1)
            out_proj(0)
            norm(1)
            pe.wait_ge(h_ready, 2 * KT)
            mlp(0)

            norm(2)
            pe.wait_ge(h_ready, 3 * KT)
            loop(pe, 8, 4, lambda i: gemm(i.plus(U_IN[1]), i.plus(T_IN[1])))
            gemm(V(U_IN[1] + 8), V(T_IN[1] + 8))

            def values(i):
                gemm(i.plus(U_IN[1] + 9), i.plus(T_IN[1] + 9))
                to_tokens(i.plus(13))
            loop(pe, 8, 4, values)

            def gla_head(h):
                pe.wait_ge(g_dve, h.times(6).plus(1).v)
                for c in range(3):
                    last = pe.matmul(ps[:, c, 0:CH], wgh[:, :], tmp[:, 1, c * CH:(c + 1) * CH], start=True, stop=True)
                last.then_inc(g_pe, 1)
                pe.wait_ge(g_dve, h.times(6).plus(6).v)
                n = h.times(NB)
                for b in range(NB):
                    m = n.plus(b)
                    cols = slice(NS + b * P, NS + (b + 1) * P)
                    if b or h.c or h.L:
                        pe.wait_ge(gb_scores, m.v)
                        pe.wait_ge(gb_kd, m.v)
                    pe.matmul(ps[:, 0, 0:P], ke[:, cols], qe[:, cols], start=True, stop=True).then_inc(gb_a, 1)
                    turn(ps[:, 1, 0:P], bcum[:, cols]).then_inc(gb_a, 1)
                    pe.wait_ge(gb_scores, m.plus(1).v)
                    pe.wait_ge(gb_kd, m.plus(1).v)
                    v = Vo[:, b, ds(h.times(DV).v, DV)]
                    if b >= 2 or h.c or h.L:
                        pe.wait_ge(gb_out, m.plus(-1).v)
                    O = ps[:, 2 + b % 2, 0:DV]
                    pe.matmul(O, aT[:, :], v, start=True, stop=False, skip_group_check=True)
                    for c in range(2):
                        half = slice(CHUNK * c, CHUNK * (c + 1))
                        pe.wait_ge(gb_state, h.times(2 * NB + 1).plus(2 * b + c + 1).v)
                        pe.matmul(O[half, :], qe[:, NS + b * P + CHUNK * c:NS + b * P + CHUNK * (c + 1)], S[:, :],
                                  start=False, stop=(c == 1), skip_group_check=True).then_inc(gb_inter, 1)
                        pe.matmul(ps[:, 4 + c, 0:DV], kdn[:, c, :], v, start=True, stop=True
                                  ).then_inc(gb_kv, 1)
                    pe.wait_ge(gb_out, m.plus(1).v)
                    if b or h.c or h.L:
                        pe.wait_ge(g_trk, m.v)
                    for e in range(2):
                        last = turn(ps[:, 6, e * P:(e + 1) * P], tmp[:, 0, e * P:(e + 1) * P])
                    last.then_inc(g_tr, 1)
            all_read(pe, T_IN[1] + 17)
            loop(pe, NG, 1, gla_head, peel=1)
            loop(pe, 8, 4, lambda i: gemm(i.plus(U_IN[1] + 17), i.plus(T_IN[1] + 17)))

            all_read(pe, T_IN[1] + 25)
            for i in range(12):
                last = turn(ps[0:NS, i // 4, (i % 4) * P:(i % 4 + 1) * P], qks[:, 4 + i, :] if i < 4 else vs_f[:, i - 4, :])
            last.then_inc(s_pe, 1)
            for h in range(NG):
                pe.wait_ge(s_dve, 1 + 10 * h + 1)
                for b in range(NS):
                    def outer(b):
                        pe.matmul(ps[:, 3 + b % 2, 0:DV], kmask[:, b, :], kvnat[:, 512 + h * DV:512 + (h + 1) * DV],
                                  start=True, stop=True).then_inc(s_pe, 1)
                    if b == 0:
                        outer(0)
                        outer(1)
                    pe.wait_ge(s_dve, 1 + 10 * h + 1 + b + 1)
                    pe.matmul(ps[0:NS, 5, 0:DV], qmask[:, b, :], sout[:, b, :], start=(b == 0), stop=(b == NS - 1)
                              ).then_inc(s_out, 1)
                    if b + 2 < NS:
                        outer(b + 2)
            pe.wait_ge(s_dve, 42)
            for k in range(KT):
                last = turn(ps[:, 6, NS * k:NS * (k + 1)], osn[:, k * P:(k + 1) * P])
            last.then_inc(s_pe, 1)
            out_proj(1)
            norm(3)
            pe.wait_ge(h_ready, 4 * KT)
            mlp(1)
            all_read(pe, T_MLP[1] + 160)
            for b in range(NB + 1):
                if b >= 2:
                    pe.wait_ge(y_kept, b - 1)
                for k in range(KT):
                    if b < NB:
                        last = turn(ps[:, 2 * (b % 2) + k // 4, (k % 4) * P:(k % 4 + 1) * P],
                                    xT[:, k, NS + b * P:NS + (b + 1) * P])
                    else:
                        last = turn(ps[0:NS, 2 * (b % 2) + k // 4, (k % 4) * P:(k % 4 + 1) * P], xT[:, k, 0:NS])
                last.then_inc(y_turned, 1)

        @block.scalar
        def _(act):
            link = Link(act, act_link)

            def rsqrt(out, in_, n, sem, read=None, read_count=None):
                if read is None:
                    link(act.activation(out, in_, ACT.Ln, bias=eps[0:out.shape[0], 0:1], scale=1.0 / n))
                else:
                    act.activation(out, in_, ACT.Ln, bias=eps[0:out.shape[0], 0:1], scale=1.0 / n).then_inc(read, 1)
                    act.wait_ge(read, read_count)
                act.activation(out, out, ACT.Exp, scale=-0.5).then_inc(sem, 1)

            def norm(n, last_tiles=None):
                l, w = n // 2, n % 2
                for k in range(KT):
                    if last_tiles is not None:
                        t = V(last_tiles + k)
                        act.wait_ge(acc_free[t.par], t.half.plus(1).v)
                    if k >= 2:
                        act.wait_ge(sq_summed, KT * n + k - 1)
                    act.activation(tmp[:, k % 2, :], xT[:, k, :], ACT.Square).then_inc(sq_ready, 1)
                t = V(T_NORM[n])
                act.wait_ge(sq_summed, KT * (n + 1))
                rsqrt(thirds(rstd[:, :]), acc(t.par), D, rstd_ready, acc_free[t.par], t.half.plus(1).v)
                for k in range(KT):
                    act.wait_ge(norm_scaled, KT * n + k + 1)
                    link(act.activation(tmp[:, k % 2, NS:T], tmp[:, k % 2, NS:T], ACT.Identity,
                                        bias=modT[:, l, 24 * w + k, NS:NC], scale=gain[:, n, k, NS:NC]))
                    act.wait_ge(norm_affine, KT * n + k + 1)
                    act.activation(hh[:, k, :], tmp[:, k % 2, :], ACT.Copy).then_inc(norm_hi, 1)

            def token_tile(i, t, nn, keep):
                act.wait_ge(acc_done, done(t, nn))
                if i.c >= 2 or i.L:
                    act.wait_ge(nat_done, i.plus(-1).v)
                act.activation(thirds(tmp[:, i.c % 2, :]), acc(t.par), ACT.Copy).then_inc(tmp_full, 1)
                act.activation(keep, ps[:, 3 * t.par, 0:NS], ACT.Copy).then_inc(acc_free[t.par], 1)

            def mlp(l):
                t0, nn = T_MLP[l], 2 * l + 2

                def up(i, t):
                    for j in range(2):
                        q = i.times(2).plus(2 * NPAIR * l + j)
                        act.wait_ge(acc_done, done(t.plus(j), nn))
                        if q.c >= 2 or q.L:
                            act.wait_ge(hid_ready, q.plus(-1).v)
                        tt = t.plus(j)
                        act.activation(thirds(tmp[:, j, :]), acc(tt.par), ACT.Relu).then_inc(acc_free[tt.par], 1)
                        act.wait_ge(hid_squared, q.plus(1).v)
                        act.activation(hid[0][:, i.c % 2, j, :], tmp[:, j, :], ACT.Copy).then_inc(hid_hi_ready, 1)
                up(V(0), V(t0))
                loop(act, NPAIR - 1, 2, lambda i: up(i.plus(1), i.times(10).plus(t0 + 2)), peel=1)

            act.wait_ge(small_loaded, 16 * SMALL)
            act.activation(c9e[:, :], c9[:, :], ACT.Exp, scale=-1.0).then_inc(silu_pos, 1)
            for k in range(KT):
                act.wait_ge(xt_done, k + 1)
                act.activation(xT[:, k, NS:T].rearrange("p (a n) -> p a n", a=2),
                               ps[:, 2 + 2 * (k % 2):4 + 2 * (k % 2), :], ACT.Copy).then_inc(xt_kept, 1)
            act.wait_ge(xt_kept, KT)
            act.wait_ge(setup_dve, 4)
            norm(0)

            def residual_out(l):
                act.wait_ge(h_ready, KT * (2 * l + 1))
                act.dma_start(xstore.rearrange("p (k n) -> p k n", k=KT), xT[:, :, :]).then_inc(x_spilled, 16)
            residual_out(0)
            loop(act, 12, 2, lambda i: token_tile(i, i.plus(T_IN[0]), 1, sF[:, ds(i.v, 1), :].rearrange("p a n -> p (a n)")), peel=2)

            def conv(c):
                t = c.times(3).plus(T_IN[0] + 12)
                act.wait_ge(acc_done, done(t, 1))
                if c.c < 2 and not c.L:
                    act.wait_ge(nat_done, 12)
                else:
                    u = c.times(3).plus(T_IN[0] + 12 - 6 + 1)
                    act.wait_ge(acc_free[u.par], u.half.plus(1).v)
                act.activation(thirds(tmp[:, c.c % 2, :]), acc(t.par), ACT.Copy).then_inc(acc_free[t.par], 1)
            loop(act, 4, 2, conv, peel=2)
            all_read(act, T_IN[0] + 12 + 3 * 3 + 2)
            token_tile(V(12), V(T_IN[0] + 24), 1, sF[:, 12, :])
            act.wait_ge(nat_kept, 13)
            for j in range(2):
                last = act.activation(sqs[:, j], QK[:, j], ACT.Square)
            last.then_inc(prep_act, 1)
            act.wait_ge(prep_dve, 1)
            act.activation(sq8[:, :, :], sNat[:, 0:2, :], ACT.Square).then_inc(prep_act, 1)
            act.wait_ge(prep_dve, 3)
            link(act.activation(lft[:, :, :], lft[:, :, :], ACT.Exp))
            act.activation(lft[:, :, :], lft[:, :, :], ACT.Ln, bias=1.0).then_inc(prep_act, 1)
            act.wait_ge(prep_dve, 4)
            rsqrt(rsq[:, :], rsq[:, :], HD, prep_act)

            def head(h):
                n = h.times(NB)
                act.wait_ge(a_turned, h.times(2).plus(1).v)
                act.activation(qT[:, :].rearrange("p (a n) -> p a n", a=2), ps[0:HD + 2, 0:2, :], ACT.Copy).then_inc(a_q, 1)
                for i in range(NB):
                    act.wait_ge(a_max, n.plus(i + 1).v)
                    if i or h.c or h.L:
                        act.wait_ge(a_pt, n.plus(i).v)
                        act.wait_ge(a_o, n.plus(i - 1).v) if (i > 1 or h.c or h.L) else None
                    w = (i + 1) * P
                    bank = 4 + 2 * (i % 2)
                    src = ps[:, bank:bank + 2, :].rearrange("p a n -> p (a n)")[:, 0:w]
                    act.activation(Pm[:, 0:w], src, ACT.Exp, bias=nmx[:, i % 2:i % 2 + 1],
                                   accum_out=rsum[:, i % 2:i % 2 + 1]).then_inc(a_p, 1)

            def pair(p):
                for e in range(2):
                    head(p.times(2).plus(e))
                act.wait_ge(a_pair, p.plus(1).v)
                act.activation(hh[:, ds(p.plus(4).v, 1), NS:T].rearrange("p o (a n) -> p (o a) n", a=2), ps[:, 0:2, :],
                               ACT.Copy).then_inc(a_pair_hi, 1)
            loop(act, NH // 2, 1, pair, peel=1)

            def sequence(b):
                act.wait_ge(d_pe, b.times(5).plus(3).v)
                act.activation(qbc[:, :], ps[:, 0, :], ACT.Copy).then_inc(d_act, 1)
                act.wait_ge(d_dve, b.times(7).plus(2 + 4).v)
                act.activation(PBx[:, :, :], PBx[:, :, :], ACT.Exp).then_inc(d_act, 1)
            loop(act, NS, 1, sequence)
            act.wait_ge(d_pe, 3 + 5 * NS)
            act.wait_ge(d_dve, 2 + 7 * NS)
            for k in range(4):
                act.activation(hh[:, k, :], ya[:, k, :], ACT.Copy).then_inc(y_hi, 1)
            for c in range(4):
                act.activation(hh[:, 4 + c, 0:NS], ps[:, 5, NS * c:NS * (c + 1)], ACT.Copy).then_inc(y_hi, 1)
            norm(1, T_OUT[0])
            mlp(0)

            norm(2, T_MLP[0] + 152)
            residual_out(1)

            def query_or_key(i, k):
                t = i.plus(T_IN[1] + 4 * k)
                act.wait_ge(acc_done, done(t, 3))
                if not k and not i.c and not i.L:
                    act.wait_ge(x_spilled, 32)
                act.activation(qk1[:, ds(i.times(2).plus(k).v, 1), :].rearrange("p o (c n) -> p (o c) n", c=3),
                               acc(t.par), ACT.Copy).then_inc(acc_free[t.par], 1)
            for k in range(2):
                loop(act, 4, 2, lambda i: query_or_key(i, k), peel=2 if k == 0 else 0)
            loop(act, 8, 2, lambda i: token_tile(i.plus(13), i.plus(T_IN[1] + 8), 3,
                                                 vs_f[:, ds(i.v, 1), :].rearrange("p a n -> p (a n)")))
            t = V(T_IN[1] + 16)
            act.wait_ge(acc_done, done(t, 3))
            act.wait_ge(nat_done, 21)
            act.activation(thirds(tmp[:, 1, :]), acc(t.par), ACT.Copy).then_inc(acc_free[t.par], 1)

            def gla_head(h):
                g = h.times(6)
                act.wait_ge(g_dve, g.plus(2).v)
                link(act.activation(tmp[:, 0, :], tmp[:, 0, :], ACT.Exp))
                act.activation(tmp[:, 0, :], tmp[:, 0, :], ACT.Ln, bias=1.0).then_inc(g_act, 1)
                act.wait_ge(g_dve, g.plus(3).v)
                act.activation(dec[:, :], bcum[:, NS:T].rearrange("p (c r) -> p c r", r=CHUNK)[:, :, CHUNK - 1], ACT.Exp)
                act.activation(tmp[:, 0, NS:T], bcum[:, NS:T], ACT.Exp).then_inc(g_act, 1)
                act.wait_ge(g_dve, g.plus(4).v)
                act.activation(tmp[:, 0, NS:T], bcum[:, NS:T], ACT.Exp, scale=-1.0).then_inc(g_act, 1)
                act.wait_ge(g_dve, g.plus(5).v)
                act.activation(tmp[:, 0, NS:T], tmp[:, 0, NS:T], ACT.Exp).then_inc(g_act, 1)
                for b in range(NB):
                    m = h.times(NB).plus(b)
                    act.wait_ge(gb_a, m.times(2).plus(2).v)
                    if b or h.c or h.L:
                        act.wait_ge(gb_kv, m.times(2).v)
                    act.activation(kdn[0:CHUNK, 0, :], ps[0:CHUNK, 1, 0:P], ACT.Copy)
                    act.activation(kdn[CHUNK:P, 1, :], ps[CHUNK:P, 1, 0:P], ACT.Copy).then_inc(gb_kd, 1)
                    act.wait_ge(gb_inter, m.times(2).plus(2).v)
                    if b or h.c or h.L:
                        act.wait_ge(g_tr, m.v)
                    link(act.activation(tmp[:, 0, DV:2 * DV], ps[:, 2 + b % 2, 0:DV], ACT.Square, accum_out=ss1[:, 0:1]))
                    rsqrt(ss1[:, 1:2], ss1[:, 0:1], DV, gb_rs)
                    act.wait_ge(g_tr, m.plus(1).v)
                    act.activation(qk1[:, ds(h.times(2).v, 2), NS + b * P:NS + (b + 1) * P],
                                   ps[:, 6, 0:2 * P].rearrange("p (e n) -> p e n", e=2), ACT.Copy).then_inc(g_trk, 1)
                act.wait_ge(gb_state, h.times(2 * NB + 1).plus(2 * NB + 1).v)
                act.dma_start(gla_prompt[0, 0, ds(h.v, 1)].rearrange("o k v -> (o k) v"), S[:, :]).then_inc(g_stored, 16)
            loop(act, NG, 1, gla_head, link, 1 + 2 * NB, peel=1)

            def gate(f):
                t = f.plus(T_IN[1] + 17)
                act.wait_ge(acc_done, done(t, 3))
                if f.c >= 2 or f.L:
                    act.wait_ge(r_done, f.plus(-1).v)
                act.activation(thirds(tmp[:, f.c % 2, :]), acc(t.par), ACT.Exp, scale=-1.0).then_inc(r_exp, 1)
            loop(act, KT, 2, gate, peel=2)
            act.activation(dec_s[:, :, :], dec_s[:, :, :], ACT.Exp).then_inc(s_act, 1)
            act.wait_ge(s_ss, 1)
            rsqrt(ss8[:, :], ss8[:, :], DV, s_act)
            act.wait_ge(y_s, 1)
            act.wait_ge(r_done, KT)
            act.wait_ge(gla_stored, 16 * NG)
            for k in range(KT):
                act.activation(hh[:, k, :], qk1[:, k, :], ACT.Copy).then_inc(y_hi, 1)
            norm(3, T_OUT[1])
            mlp(1)
            act.wait_ge(g_stored, 16 * NG)

        @block.vector
        def _(dve):
            link = Link(dve, dve_link)
            tt, stt = dve.tensor_tensor, dve.scalar_tensor_tensor

            def norm(n):
                l, w = n // 2, n % 2
                dve.wait_ge(rstd_ready, n + 1)

                def low(k):
                    dve.wait_ge(norm_hi, KT * n + k + 1)
                    tt(hl[:, k, :], tmp[:, k % 2, :], hh[:, k, :].bitcast(F32), ALU.subtract).then_inc(h_ready, 1)
                for k in range(KT):
                    if k >= 2:
                        dve.wait_ge(h_ready, KT * n + k - 1)
                    tt(tmp[:, k % 2, :], xT[:, k, :], rstd[:, :], ALU.mult).then_inc(norm_scaled, 1)
                    dve.wait_ge(norm_scaled, KT * n + k + 1)
                    link(tt(tmp[:, k % 2, 0:NS], tmp[:, k % 2, 0:NS], gain[:, n, k, 0:NS], ALU.mult))
                    tt(tmp[:, k % 2, 0:NS], tmp[:, k % 2, 0:NS], modT[:, l, 24 * w + k, 0:NS], ALU.add
                       ).then_inc(norm_affine, 1)
                    if k:
                        low(k - 1)
                low(KT - 1)

            def token_tile(i, dst):
                dve.wait_ge(nat_done, i.plus(1).v)
                dve.tensor_copy(dst, ps[:, 6:8, :].rearrange("p a (b n) -> p (a b) n", n=P)).then_inc(nat_kept, 1)

            def residual(t, nn, f, l, comp):
                dve.wait_ge(acc_done, done(t, nn))
                m = KT * comp + f
                s = 3 * t.par
                link(tt(t8[:, :], ps[:, s, 0:NS], modT[:, l, m, 0:NS], ALU.mult))
                tt(xT[:, f, 0:NS], xT[:, f, 0:NS], t8[:, :], ALU.add)
                stt(out=xT[:, f, NS:CH], in0=ps[:, s, NS:CH], scalar=modT[:, l, m, NS:NC], in1=xT[:, f, NS:CH],
                    op0=ALU.mult, op1=ALU.add)
                x2 = xT[:, f, CH:T].rearrange("p (c n) -> p c n", c=2)
                stt(out=x2, in0=ps[:, s + 1:s + 3, 0:CH], scalar=modT[:, l, m, NS:NC], in1=x2,
                    op0=ALU.mult, op1=ALU.add).then_inc(acc_free[t.par], 1)
                dve.wait_ge(acc_free[t.par], t.half.plus(1).v)

            def out_proj(l):
                dve.wait_ge(x_back, 16 * (l + 1))
                for f in range(KT):
                    residual(V(T_OUT[l] + f), 2 * l + 1, f, l, 2)

            def mlp(l):
                t0, nn = T_MLP[l], 2 * l + 2

                def up(i, t):
                    for j in range(2):
                        q = i.times(2).plus(2 * NPAIR * l + j)
                        tj = t.plus(j)
                        dve.wait_ge(acc_free[tj.par], tj.half.plus(1).v)
                        tt(tmp[:, j, :], tmp[:, j, :], tmp[:, j, :], ALU.mult).then_inc(hid_squared, 1)
                        dve.wait_ge(hid_hi_ready, q.plus(1).v)
                        tt(hid[1][:, i.c % 2, j, :], tmp[:, j, :], hid[0][:, i.c % 2, j, :].bitcast(F32), ALU.subtract
                           ).then_inc(hid_ready, 1)

                def down(i, t):
                    for f in range(KT):
                        residual(t.plus(f), nn, f, l, 5)

                def step(i):
                    up(i.plus(1), i.times(10).plus(t0 + 2))
                    down(i, i.times(10).plus(t0 + 4))
                up(V(0), V(t0))
                loop(dve, NPAIR - 1, 2, step, link, KT, peel=1)
                down(V(NPAIR - 1), V(t0 + 152))

            dve.wait_ge(consts_made, 1)
            dve.wait_ge(setup_pe, 1)
            dve.tensor_copy(vecT[:, :], ps[:, 0, 0:144])
            dve.tensor_copy(prevT[:, :, :], ps[:, 0, 256:320].rearrange("p (c n) -> p c n", c=4))
            dve.tensor_copy(xT[:, :, 0:NS], ps[:, 1, 0:NS * KT].rearrange("p (k n) -> p k n", k=KT)).then_inc(setup_dve, 1)
            link(dve.tensor_scalar(gqb[:, :], gqb[:, :], HD ** -0.5, None, ALU.mult))
            dve.wait_ge(silu_pos, 1)
            link(dve.tensor_scalar(c9e[:, :], c9e[:, :], 1.0, None, ALU.add))
            link(dve.reciprocal(c9e[:, :], c9e[:, :]))
            tt(c9[:, :], c9[:, :], c9e[:, :], ALU.mult).then_inc(setup_dve, 1)
            dve.wait_ge(setup_pe, 2)
            dve.tensor_copy(scT[:, :, :], ps[:, 1, P:P + NC * KT].rearrange("p (k n) -> p k n", k=KT)).then_inc(setup_dve, 1)
            modA = modT[:, :, :, :].rearrange("p l n c -> p (l n) c")

            def modulation(i):
                dve.wait_ge(ada_done, i.plus(1).v)
                n = i.times(4).v
                tt(modA[:, ds(n, 4), :], ps[:, 6 + i.c % 2, 0:4 * NC].rearrange("p (f c) -> p f c", f=4),
                   vecT[:, ds(n, 4)].unsqueeze(2).to_broadcast([P, 4, NC]), ALU.add).then_inc(ada_kept, 1)
            loop(dve, 24, 2, modulation)
            dve.wait_ge(ada_kept, 24)
            for n in range(4):
                l, w = n // 2, n % 2
                last = stt(out=gain[:, n, :, :], in0=modT[:, l, 24 * w + 8:24 * w + 16, :], scalar=1.0,
                           in1=vecT[:, 96 + 16 * w + 8 * l:104 + 16 * w + 8 * l].unsqueeze(2).to_broadcast([P, KT, NC]),
                           op0=ALU.add, op1=ALU.mult)
            last.then_inc(setup_dve, 1)
            dve.wait_ge(setup_dve, 4)
            norm(0)

            dve.wait_ge(x_spilled, 16)
            for j in range(2):
                loop(dve, 4, 2, lambda i: token_tile(i.plus(4 * j), QK[:, j, :, ds(i.times(P).v, P)]))
            loop(dve, 4, 2, lambda i: token_tile(i.plus(8), Vn[:, :, ds(i.times(P).v, P)]))

            def conv(c):
                t = c.times(3).plus(T_IN[0] + 12)
                m = c.c % 2
                dve.wait_ge(acc_free[t.par], t.half.plus(1).v)
                t = t.plus(1)
                dve.wait_ge(acc_done, done(t, 1))
                s = 3 * t.par
                tt(U[:, 0:NS], ps[:, s, 0:NS], tmp[:, m, 0:NS], ALU.mult)
                tt(U[:, NS + 2:CH + 2], ps[:, s, NS:CH], tmp[:, m, NS:CH], ALU.mult)
                tt(U[:, CH + 2:T + 2].rearrange("p (c n) -> p c n", c=2), ps[:, s + 1:s + 3, 0:CH],
                   tmp[:, m, CH:T].rearrange("p (c n) -> p c n", c=2), ALU.mult).then_inc(acc_free[t.par], 1)
                dve.wait_ge(acc_free[t.par], t.half.plus(1).v)
                w = [vecT[:, ds(c.plus(P + 4 * j).v, 1)] for j in range(3)]
                y = ya[:, ds(c.v, 1), :].rearrange("p o n -> p (o n)")
                link(dve.tensor_scalar(y[:, NS:T], U[:, NS + 2:T + 2], w[2], None, ALU.mult))
                link(stt(out=y[:, NS:T], in0=U[:, NS + 1:T + 1], scalar=w[1], in1=y[:, NS:T], op0=ALU.mult, op1=ALU.add))
                link(stt(out=y[:, NS:T], in0=U[:, NS:T], scalar=w[0], in1=y[:, NS:T], op0=ALU.mult, op1=ALU.add))
                prev = prevT[:, ds(c.v, 1), :].rearrange("p o (b j) -> p (o b) j", j=2)
                link(dve.tensor_scalar(y[:, 0:NS], U[:, 0:NS], w[2], None, ALU.mult))
                for j in (1, 0):
                    link(stt(out=y[:, 0:NS], in0=prev[:, :, j], scalar=w[j], in1=y[:, 0:NS], op0=ALU.mult, op1=ALU.add))
                dve.tensor_copy(uOut[:, ds(c.v, 1), 0:NS].rearrange("p o n -> p (o n)"), U[:, 0:NS])
                dve.tensor_copy(uOut[:, ds(c.v, 1), NS:10].rearrange("p o n -> p (o n)"), U[:, T:T + 2])
                t = t.plus(1)
                dve.wait_ge(acc_done, done(t, 1))
                tt(thirds(y), thirds(y), acc(t.par), ALU.mult).then_inc(acc_free[t.par], 1)
                dve.wait_ge(acc_free[t.par], t.half.plus(1).v)
            dve.wait_ge(setup_pe, 2)
            link(dve.memset(U[:, NS:NS + 2], 0.0))
            loop(dve, 4, 2, conv, link, 6)

            link(dve.memset(lf[:, :, :], 0.0))
            link(dve.memset(rsq[:, :], 1.0))
            dve.wait_ge(nat_done, 13)
            tt(lf[:, 0:NB, :], ps[:, 6:8, :].rearrange("p a (b n) -> p (a b) n", n=P)[:, :, P - NH:P],
               bfb[:, :].unsqueeze(1).to_broadcast([P, NB, NH]), ALU.add).then_inc(nat_kept, 1)
            dve.wait_ge(prep_pe, 1)
            dve.tensor_copy(sNat[:, :, :], ps[0:NS, 0:3, :]).then_inc(prep_dve, 1)
            tt(lf[0:NS, NB, :], ps[0:NS, 3, P - NH:P], bfb[0:NS, :], ALU.add)
            dve.tensor_copy(crow[:, :], ps[0:10, 4, :]).then_inc(prep_dve, 1)
            dve.wait_ge(prep_dve, 2)
            stt(out=lft[:, :, :], in0=lf[:, :, :], scalar=-1.0, in1=lf[:, :, :], op0=ALU.mult, op1=ALU.min
                ).then_inc(prep_dve, 1)
            dve.wait_ge(prep_act, 1)
            groups = "p j b (h d) -> p (j b h) d"
            dve.tensor_reduce(rsq[:, 0:2 * NB * NH], sqs[:, :, :, :].rearrange(groups, d=HD), X, ALU.add)
            dve.wait_ge(prep_act, 2)
            dve.tensor_reduce(rsq[0:NS, 2 * NB * NH:], sq8[:, :, :].rearrange("p j (h d) -> p (j h) d", d=HD), X, ALU.add
                              ).then_inc(prep_dve, 1)
            dve.wait_ge(prep_act, 3)
            stt(out=lf[:, :, :], in0=lf[:, :, :], scalar=0.0, in1=lft[:, :, :], op0=ALU.min, op1=ALU.subtract
                ).then_inc(prep_dve, 1)
            dve.wait_ge(prep_act, 4)
            rs = rsq[:, 0:2 * NB * NH].rearrange("p (j g) -> p j g", j=2)
            rs8 = rsq[0:NS, 2 * NB * NH:].rearrange("p (j g) -> p j g", j=2)
            for j, g in ((0, gqb), (1, gkb)):
                q = QK[:, j].rearrange("p b (h d) -> p (b h) d", d=HD)
                s = sNat[:, j, :].rearrange("p (h d) -> p h d", d=HD)
                link(tt(q, q, rs[:, j, :].unsqueeze(2).to_broadcast([P, NB * NH, HD]), ALU.mult))
                link(tt(q, q, g[:, :].unsqueeze(1).to_broadcast([P, NB * NH, HD]), ALU.mult))
                link(tt(s, s, rs8[:, j, :].unsqueeze(2).to_broadcast([NS, NH, HD]), ALU.mult))
                link(tt(s, s, g[0:NS, :].unsqueeze(1).to_broadcast([NS, NH, HD]), ALU.mult))
            tt(sq8[:, 0, :], sNat[:, 0, :], sNat[:, 1, :], ALU.mult).then_inc(prep_dve, 1)
            dve.wait_ge(prep_dve, 6)
            dve.tensor_reduce(snew[:, :], sq8[:, 0, :].rearrange("p (h d) -> p h d", d=HD), X, ALU.add)
            dve.wait_ge(prep_pe, 2)
            link(dve.tensor_copy(fcum[:, :, :], ps[:, 5, 0:NB * NH].rearrange("p (b h) -> p b h", h=NH)))
            dve.memset(QA[:, :, HD + 1:HD + 2], 1.0)
            dve.memset(KA[:, :, HD:HD + 1], 1.0)

            def head(h, odd):
                n = h.times(NB)
                if h.c or h.L:
                    dve.wait_ge(a_turned, h.times(2).v)
                dve.tensor_copy(QA[:, :, 0:HD], QK[:, 0, :, ds(h.times(HD).v, HD)])
                dve.tensor_copy(QA[:, :, HD:HD + 1], fcum[:, :, ds(h.v, 1)])
                dve.tensor_copy(KA[:, :, 0:HD], QK[:, 1, :, ds(h.times(HD).v, HD)])
                dve.tensor_scalar(KA[:, :, HD + 1:HD + 2], fcum[:, :, ds(h.v, 1)], -1.0, None, ALU.mult
                                  ).then_inc(a_built, 1)
                dve.wait_ge(a_turned, h.times(2).plus(2).v)
                dve.tensor_copy(kT[:, :].rearrange("p (a n) -> p a n", a=2), ps[0:HD + 2, 2:4, :]).then_inc(a_k, 1)

                def peak(i):
                    dve.wait_ge(a_s, n.plus(i + 1).v)
                    bank = 4 + 2 * (i % 2)
                    src = ps[:, bank:bank + 2, :].rearrange("p a n -> p (a n)")[:, 0:(i + 1) * P]
                    dve.tensor_reduce(nmx[:, i % 2:i % 2 + 1], src, X, ALU.max, negate=True).then_inc(a_max, 1)
                peak(0)
                for i in range(NB):
                    if i + 1 < NB:
                        peak(i + 1)
                    dve.wait_ge(a_pt, n.plus(i + 1).v)
                    w = (i + 1) * P
                    dve.tensor_copy(PT[:, 0:w], ps[:, 0:2, :].rearrange("p a n -> p (a n)")[:, 0:w]).then_inc(a_ptk, 1)
                    dve.wait_ge(a_p, n.plus(i + 1).v)
                    link(dve.reciprocal(rinv[:, i % 2:i % 2 + 1], rsum[:, i % 2:i % 2 + 1]))
                    dve.wait_ge(a_av, n.plus(i + 1).v)
                    dve.tensor_scalar(onat[:, i, HD * odd:HD * (odd + 1)], ps[:, 2 + i % 2, 0:HD],
                                      rinv[:, i % 2:i % 2 + 1], None, ALU.mult).then_inc(a_o, 1)

            def pair(p):
                if p.c or p.L:
                    dve.wait_ge(a_pair, p.v)
                for e in range(2):
                    head(p.times(2).plus(e), e)
                dve.wait_ge(a_pair_hi, p.plus(1).v)
                tt(hl[:, ds(p.plus(4).v, 1), NS:T].rearrange("p o (a n) -> p (o a) n", a=2), ps[:, 0:2, :],
                   hh[:, ds(p.plus(4).v, 1), NS:T].rearrange("p o (a n) -> p (o a) n", a=2).bitcast(F32), ALU.subtract
                   ).then_inc(a_pair_lo, 1)
            dve.wait_ge(kv_out, 16 * 9)
            loop(dve, NH // 2, 1, pair, link, 2 * NB, peel=1)

            dve.wait_ge(d_pe, 1)
            dve.wait_ge(a_pair_lo, NH // 2)
            dve.tensor_copy(LT[:, :, :], ps[:, 2:4, :].rearrange("p a (h n) -> p (a h) n", n=P))
            link(dve.tensor_reduce(ptot[:, :], Lraw[:, :, :].rearrange("p s h -> p h s"), X, ALU.add))
            tt(TB[:, :, :], ptot[:, :].unsqueeze(2).to_broadcast([P, NH, P]),
               ones[:, :].unsqueeze(1).to_broadcast([P, NH, P]), ALU.mult)
            tt(LN[:, :, :], lf[0:NS, NB, :].unsqueeze(2).to_broadcast([NS, NH, P]),
               ones[0:NS, :].unsqueeze(1).to_broadcast([NS, NH, P]), ALU.mult).then_inc(d_dve, 1)
            dve.wait_ge(d_pe, 2)
            link(dve.tensor_copy(Lsuf[:, :, :], ps[:, 4:6, :].rearrange("p a (h n) -> p (a h) n", n=P)))
            link(dve.memset(sc[:, PAGES, :], NEG))
            dve.memset(osum[:, :], 0.0).then_inc(d_dve, 1)

            def sequence(b):
                g = b.times(7).plus(2)
                if b.c or b.L:
                    dve.wait_ge(d_pe, b.times(5).plus(2).v)
                dve.tensor_scalar(qsel[:, :], sNat[:, 0, :], ident[0:NS, ds(b.v, 1)], None, ALU.mult).then_inc(d_dve, 1)
                dve.tensor_copy(small[0:8, 24:32], eye8[0:8, ds(b.v, 1), :].rearrange("p o n -> p (o n)"))
                dve.wait_ge(d_act, b.times(2).plus(1).v)
                for j in range(4):
                    dve.wait_ge(pages_in[j % 2], b.times(256).plus(64 * (1 + j // 2)).v)
                    kk = pages[:, j % 2, :, :]
                    link(tt(kk, kk, qbc[:, :].unsqueeze(1).to_broadcast([P, 4, 512]), ALU.mult))
                    dve.tensor_reduce(sc[:, 4 * j:4 * j + 4, :], kk.rearrange("p g (h d) -> p g h d", d=HD), X, ALU.add
                                      ).then_inc(k_used, 1)
                dve.wait_ge(k_used, b.times(4).plus(4).v)
                s16 = sc[:, 0:PAGES, :]
                tt(s16, s16, Lsuf[:, :, ds(b.times(PAGES).v, PAGES)].rearrange("p h g -> p g h"), ALU.add)
                link(dve.tensor_scalar(sc[0:NS, PAGES, :], snew[:, :], only8[:, ds(b.v, 1)], None, ALU.add))
                dve.tensor_reduce(mx8[:, :], sc[:, :, :].rearrange("p g h -> p h g"), X, ALU.max).then_inc(d_dve, 1)
                dve.wait_ge(d_pe, b.times(5).plus(2 + 2).v)
                link(dve.tensor_reduce(small[0:8, 0:1], ps[0:8, 1, 0:P], X, ALU.max))
                dve.tensor_scalar(small[0:8, 8:16], ident[0:8, 0:8], small[0:8, 0:1], None, ALU.mult).then_inc(d_dve, 1)
                dve.wait_ge(d_pe, b.times(5).plus(2 + 3).v)
                tt(PBx[:, :, :], sc[:, :, :], ps[:, 2, 0:8].unsqueeze(1).to_broadcast([P, PAGES + 1, NH]), ALU.subtract
                   ).then_inc(d_dve, 1)
                dve.wait_ge(d_act, b.times(2).plus(2).v)
                dve.tensor_reduce(small[:, 16:24], PBx[:, :, :].rearrange("p g h -> p h g"), X, ALU.add).then_inc(d_dve, 1)
                dve.wait_ge(d_pe, b.times(5).plus(2 + 4).v)
                link(dve.reciprocal(small[0:8, 1:2], ps[0:8, 2, 128:129]))
                stt(out=omask[:, :], in0=ps[0:8, 3, :], scalar=small[0:8, 1:2],
                    in1=headrow[:, :, :].rearrange("p h d -> p (h d)"), op0=ALU.mult, op1=ALU.mult).then_inc(d_dve, 1)
                dve.wait_ge(d_pe, b.times(5).plus(2 + 5).v)
                tt(osum[:, :], osum[:, :], ps[0:8, 4, :], ALU.add).then_inc(d_dve, 1)
            loop(dve, NS, 1, sequence, link, 7)
            for k in range(4):
                dve.wait_ge(y_hi, k + 1)
                tt(hl[:, k, :], ya[:, k, :], hh[:, k, :].bitcast(F32), ALU.subtract).then_inc(y_ready, 1)
            for c in range(4):
                dve.wait_ge(y_hi, 8)
                tt(hl[:, 4 + c, 0:NS], ps[:, 5, NS * c:NS * (c + 1)], hh[:, 4 + c, 0:NS].bitcast(F32), ALU.subtract
                   ).then_inc(y_ready, 1)
            out_proj(0)
            norm(1)
            mlp(0)

            dve.memset(kdn[:, :, :], 0.0)
            dve.memset(wgk[:, :], 0.0).then_inc(gate_cleared, 1)
            link(dve.memset(scanm[:, :], 1.0))
            link(dve.memset(scanm[:, :].rearrange("p (c r) -> p c r", r=CHUNK)[:, :, 0:1], 0.0))
            norm(2)
            loop(dve, 8, 2, lambda i: token_tile(i.plus(13), Vo[:, :, ds(i.times(P).v, P)]))

            def gla_head(h):
                g = h.times(6)
                hc = h.v
                z = ke
                if h.c or h.L:
                    dve.wait_ge(g_stored, h.times(16).v)
                    dve.wait_ge(g_tr, h.times(NB).v)
                dve.tensor_copy(wgh[:, :], wgk[:, ds(h.times(DK).v, DK)]).then_inc(g_dve, 1)
                dve.wait_ge(g_pe, h.plus(1).v)
                link(dve.tensor_scalar(thirds(z[:, :]), ps[:, 0:3, 0:CH], vecT[:, ds(h.plus(140).v, 1)], None, ALU.add))
                stt(out=tmp[:, 0, :], in0=z[:, :], scalar=-1.0, in1=z[:, :], op0=ALU.mult, op1=ALU.min).then_inc(g_dve, 1)
                dve.wait_ge(g_act, h.times(4).plus(1).v)
                link(stt(out=z[:, :], in0=z[:, :], scalar=0.0, in1=tmp[:, 0, :], op0=ALU.min, op1=ALU.subtract))
                link(dve.tensor_scalar(z[:, :], z[:, :], 1.0 / 16.0, None, ALU.mult))
                dve.tensor_copy(dec_s[:, ds(hc, 1), :].rearrange("p o n -> p (o n)"), z[:, 0:NS])
                dve.tensor_tensor_scan(bcum[:, NS:T], scanm[:, :], z[:, NS:T], 0.0, ALU.mult, ALU.add).then_inc(g_dve, 1)
                qh = qk1[:, ds(h.times(2).v, 1), :].rearrange("p o n -> p (o n)")
                kh = qk1[:, ds(h.times(2).plus(1).v, 1), :].rearrange("p o n -> p (o n)")
                dve.wait_ge(g_act, h.times(4).plus(2).v)
                stt(out=qe[:, NS:T], in0=qh[:, NS:T], scalar=DK ** -0.5, in1=tmp[:, 0, NS:T], op0=ALU.mult, op1=ALU.mult
                    ).then_inc(g_dve, 1)
                dve.wait_ge(g_act, h.times(4).plus(3).v)
                link(tt(ke[:, NS:T], kh[:, NS:T], tmp[:, 0, NS:T], ALU.mult))
                bc = bcum[:, NS:T].rearrange("p (c r) -> p c r", r=CHUNK)
                tt(tmp[:, 0, NS:T].rearrange("p (c r) -> p c r", r=CHUNK),
                   bc[:, :, CHUNK - 1:CHUNK].to_broadcast([P, SEQ // CHUNK, CHUNK]), bc, ALU.subtract).then_inc(g_dve, 1)
                dve.memset(S[:, :], 0.0).then_inc(gb_state, 1)
                dve.tensor_copy(qks[:, ds(hc, 1), :].rearrange("p o n -> p (o n)"), qh[:, 0:NS])
                dve.tensor_copy(qks[:, ds(h.plus(4).v, 1), :].rearrange("p o n -> p (o n)"), kh[:, 0:NS])
                dve.wait_ge(g_act, h.times(4).plus(4).v)
                tt(bcum[:, NS:T], kh[:, NS:T], tmp[:, 0, NS:T], ALU.mult).then_inc(g_dve, 1)
                for b in range(NB):
                    m = h.times(NB).plus(b)
                    dve.wait_ge(gb_a, m.times(2).plus(1).v)
                    tt(aT[:, :], ps[:, 0, 0:P], pairmask[:, :], ALU.mult).then_inc(gb_scores, 1)
                    for c in range(2):
                        dve.wait_ge(gb_kv, m.times(2).plus(c + 1).v)
                        stt(out=S[:, :], in0=S[:, :], scalar=dec[:, 2 * b + c:2 * b + c + 1], in1=ps[:, 4 + c, 0:DV],
                            op0=ALU.mult, op1=ALU.add).then_inc(gb_state, 1)
                    dve.wait_ge(gb_rs, m.plus(1).v)
                    link(dve.tensor_scalar(tmp[:, 0, 0:DV], ps[:, 2 + b % 2, 0:DV], ss1[:, 1:2], None, ALU.mult))
                    tt(tmp[:, 0, 0:DV], tmp[:, 0, 0:DV], gob[:, :], ALU.mult).then_inc(gb_out, 1)
            dve.wait_ge(gate_loaded, 32)
            loop(dve, NG, 1, gla_head, link, 4 + NB, peel=1)

            def gate(f):
                t = f.plus(T_IN[1] + 17)
                r = tmp[:, f.c % 2, :]
                dve.wait_ge(r_exp, f.plus(1).v)
                link(dve.tensor_scalar(r, r, 1.0, None, ALU.add))
                link(dve.reciprocal(r, r))
                tt(thirds(r), thirds(r), acc(t.par), ALU.mult).then_inc(acc_free[t.par], 1)
                dve.wait_ge(acc_free[t.par], t.half.plus(1).v)
                dve.tensor_copy(rs_f[:, ds(f.v, 1), :].rearrange("p o n -> p (o n)"), r[:, 0:NS])
                o = qk1[:, ds(f.v, 1), NS:T].rearrange("p o n -> p (o n)")
                tt(o, o, r[:, NS:T], ALU.mult).then_inc(r_done, 1)
            dve.wait_ge(g_trk, NG * NB)
            loop(dve, KT, 2, gate, link, 2)

            dve.wait_ge(s_pe, 1)
            dve.tensor_copy(kvnat[:, :], ps[0:NS, 0:3, :].rearrange("p a n -> p (a n)")).then_inc(s_dve, 1)
            dve.wait_ge(s_dve, 1)
            dve.wait_ge(s_act, 1)
            for h in range(NG):
                base = 1 + 10 * h
                tt(kmask[:, :, :], kvnat[:, h * DK:(h + 1) * DK].unsqueeze(1).to_broadcast([NS, NS, DK]),
                   ident[0:NS, 0:NS].unsqueeze(2).to_broadcast([NS, NS, DK]), ALU.mult)
                stt(out=qmask[:, :, :], in0=qks[:, h, :].unsqueeze(1).to_broadcast([P, NS, NS]), scalar=DK ** -0.5,
                    in1=eye8[:, :, :], op0=ALU.mult, op1=ALU.mult).then_inc(s_dve, 1)
                dve.wait_ge(s_in, 16 * (h + 1))
                if h:
                    dve.wait_ge(gla_stored, 16 * h)
                for b in range(NS):
                    dve.wait_ge(s_pe, 1 + 8 * h + b + 1)
                    stt(out=sout[:, b, :], in0=sst[:, b, :], scalar=dec_s[:, h, b:b + 1], in1=ps[:, 3 + b % 2, 0:DV],
                        op0=ALU.mult, op1=ALU.add).then_inc(s_dve, 1)
                dve.wait_ge(s_out, 8 * (h + 1))
                dve.tensor_copy(osn[:, h * DV:(h + 1) * DV], ps[0:NS, 5, 0:DV]).then_inc(s_dve, 1)
            dve.wait_ge(s_dve, 41)
            sq = kmask[:, :, :].rearrange("p a n -> p (a n)")
            link(tt(sq, osn[:, :], osn[:, :], ALU.mult))
            dve.tensor_reduce(ss8[:, :], sq.rearrange("p (h v) -> p h v", v=DV), X, ALU.add).then_inc(s_ss, 1)
            dve.wait_ge(s_act, 2)
            o3 = osn[:, :].rearrange("p (h v) -> p h v", v=DV)
            link(tt(o3, o3, ss8[:, :].unsqueeze(2).to_broadcast([NS, NG, DV]), ALU.mult))
            tt(o3, o3, gob[0:NS, :].unsqueeze(1).to_broadcast([NS, NG, DV]), ALU.mult).then_inc(s_dve, 1)
            dve.wait_ge(s_pe, 34)
            tt(qk1[:, :, 0:NS], ps[:, 6, 0:NS * KT].rearrange("p (k n) -> p k n", k=KT), rs_f[:, :, :], ALU.mult
               ).then_inc(y_s, 1)
            for k in range(KT):
                dve.wait_ge(y_hi, KT + k + 1)
                tt(hl[:, k, :], qk1[:, k, :], hh[:, k, :].bitcast(F32), ALU.subtract).then_inc(y_ready, 1)
            out_proj(1)
            norm(3)
            mlp(1)
            for b in range(NB + 1):
                dve.wait_ge(y_turned, b + 1)
                n = P if b < NB else NS
                dst = ynat[:, b, :] if b < NB else ysn[:, :]
                dve.tensor_copy(dst.rearrange("p (a n) -> p a n", a=2), ps[0:n, 2 * (b % 2):2 * (b % 2) + 2, :]
                                ).then_inc(y_kept, 1)


_INS = ["x_prompt", "x_sample", "c_prompt", "c_sample", "cache_k", "cache_v", "cache_logf", "page_table", "state_conv",
        "state_gla", "g_mix", "g_ffn", "w_ada", "b_ada", "w_in_even", "b_f", "g_q", "g_k", "w_conv", "w_out_even",
        "w_in_odd", "w_gk", "b_gk", "g_o", "w_out_odd", "w_ff1", "w_ff2"]
_OUTS = [(1, 1024, 1024), (8, 1, 1024), (1, 1, 1024, 8, 64), (1, 1, 1024, 8, 64), (1, 1, 1024, 8),
         (8, 1, 1, 8, 64), (8, 1, 1, 8, 64), (8, 1, 1, 8), (1, 1, 2, 512), (8, 1, 2, 512),
         (1, 1, 4, 128, 256), (8, 1, 4, 128, 256)]


def kernel(**inputs):
    import numpy as _np
    import concourse.bacc as _bacc
    from concourse import mybir as _mybir
    from concourse.bass_utils import run_bass_kernel_spmd as _run

    nc = _bacc.Bacc("TRN2", target_bir_lowering=False, num_devices=1)
    arrays, args = {}, []
    for name in _INS:
        a = _np.ascontiguousarray(inputs[name])
        arrays[f"in_{name}_dram"] = a
        args.append(nc.dram_tensor(f"in_{name}_dram", a.shape, _mybir.dt.from_np(a.dtype), kind="ExternalInput").ap())
    for i, shape in enumerate(_OUTS):
        args.append(nc.dram_tensor(f"out_{i}_dram", shape, _mybir.dt.float32, kind="ExternalOutput").ap())
    build(nc, *args)
    r = _run(nc, [arrays], core_ids=[0])
    return tuple(r.results[0][f"out_{i}_dram"] for i in range(len(_OUTS)))
```

```python
from contextlib import ExitStack

import concourse.bass as bass
from concourse import mybir

F32 = mybir.dt.float32
F32R = mybir.dt.float32r
BF16 = mybir.dt.bfloat16
I32 = mybir.dt.int32
U32 = mybir.dt.uint32
ALU = mybir.AluOpType
ACT = mybir.ActivationFunctionType
X = mybir.AxisListType.X
ds = bass.ds

P = 128
D = 1024
KT = D // P
SEQ = 1024
NB = SEQ // P
NS = 8
T = NS + SEQ
CH = T // 3
NC = NS + 1
DEPTH = 2
NH, HD = 8, 64
PAGES, PS = 16, 128
NG, DK, DV = 4, 128, 256
CHUNK = 64
TAU = 16.0
NPAIR = 4096 // 256
EPS = 1e-6
NEG = -1e30


class V:

    def __init__(self, c, g=0, L=0):
        self.c, self.g, self.L = c, g, L
        self.v = c + g * L if L else c

    def plus(self, n):
        return V(self.c + n, self.g, self.L)

    def times(self, m):
        return V(self.c * m, self.g, self.L * m)

    @property
    def half(self):
        assert self.L % 2 == 0
        return V(self.c // 2, self.g, self.L // 2)

    @property
    def par(self):
        assert self.L % 2 == 0
        return self.c % 2


class Link:

    def __init__(self, eng, sem):
        self.eng, self.sem, self.n = eng, sem, V(0)

    def __call__(self, ins):
        self.n = self.n.plus(1)
        ins.then_inc(self.sem, 1)
        self.eng.wait_ge(self.sem, self.n.v)


def loop(eng, n, per, body, link=None, links=0, peel=0):
    for j in range(peel):
        body(V(j))
    n -= peel
    inner, body = body, lambda i: inner(i.plus(peel))
    full = n // per
    start = link.n if link else None
    if full > 1:
        with eng.Fori(0, full) as g:
            if link:
                link.n = V(start.c, g, per * links)
            for j in range(per):
                body(V(j, g, per))
            if link:
                assert link.n.c == start.c + per * links, (link.n.c - start.c, per)
        if link:
            link.n = V(start.c + full * per * links)
        done = full * per
    else:
        done = 0
    for j in range(done, n):
        body(V(j))


def build(nc, x_prompt, x_sample, c_prompt, c_sample, cache_k, cache_v, cache_logf, page_table, state_conv,
          state_gla, g_mix, g_ffn, w_ada, b_ada, w_in_even, b_f, g_q, g_k, w_conv, w_out_even, w_in_odd, w_gk,
          b_gk, g_o, w_out_odd, w_ff1, w_ff2,
          y_prompt, y_sample, k_prompt, v_prompt, logf_prompt, k_sample, v_sample, logf_sample, conv_prompt,
          conv_sample, gla_prompt, gla_sample):
    with ExitStack() as ctx:
        slab_start = (nc.sbuf_base + 31) // 32 * 32

        def at(name, shape, dt, offset):
            return nc.alloc_sbuf_tensor_at(name, shape, dt, offset=offset)

        def size(shape, dt):
            n = 2 if dt == BF16 else 4
            for s in shape[1:]:
                n *= s
            return (n + 31) // 32 * 32

        TILE = T * 4
        A0 = slab_start
        B0 = A0 + KT * TILE
        C0 = B0 + KT * TILE
        F0 = C0 + KT * TILE
        W0 = F0 + KT * TILE
        top = [W0]

        def put(name, shape, dt=F32):
            o = top[0]
            top[0] += size(shape, dt)
            return at(name, shape, dt, o)

        stage = put("stage", [P, 2, D])
        whi = put("whi", [P, 4, D], F32R)
        wlo = put("wlo", [P, 4, D], F32R)
        TMP0 = top[0]
        tmp = put("tmp", [P, 2, T])
        ident = put("ident", [P, P])
        ones = put("ones", [P, P])
        pairmask = put("pairmask", [P, P])
        eye8 = put("eye8", [P, 8, 8])
        vecT = put("vecT", [P, 144])
        modT = put("modT", [P, DEPTH, 48, NC])
        gain = put("gain", [P, 2 * DEPTH, KT, NC])
        eps = put("eps", [P, 1])
        t8 = put("t8", [P, NS])
        lay = top[0]
        tri = put("tri", [P, P])
        trisuf = put("trisuf", [P, P])
        later = put("later", [P, P])
        identb = put("identb", [P, P], BF16)
        negb = put("negb", [P, P], BF16)
        headrow = put("headrow", [8, NH, HD])
        gqb = put("gqb", [P, HD])
        gkb = put("gkb", [P, HD])
        bfb = put("bfb", [P, NH])
        sF = put("sF", [P, 13, NS])
        sNat = put("sNat", [NS, 3, 512])
        lf = put("lf", [P, NB + 1, NH])
        lft = put("lft", [P, NB + 1, NH])
        fcum = put("fcum", [P, NB, NH])
        prevT = put("prevT", [P, 4, 16])
        uOut = put("uOut", [P, 4, 10])
        rsq = put("rsq", [P, 2 * NB * NH + 16])
        only8 = put("only8", [8, 8])
        snew = put("snew", [8, 8])
        peaks = put("peaks", [P, NB, 2])
        peak = put("peak", [P, NB])
        ysam = put("ysam", [P, 4, NS])
        U = at("U", [P, T + 2], F32, top[0])
        QA = put("QA", [P, NB, HD + 2])
        KA = put("KA", [P, NB, HD + 2])
        Lraw = at("Lraw", [P, PS, NH], F32, top[0])
        Lsuf = put("Lsuf", [P, NH, P])
        sc = put("sc", [P, PAGES + 1, NH])
        PBx = put("PBx", [P, PAGES + 1, NH])
        idx = put("idx", [P, 1], I32)
        pt = put("pt", [1, P], I32)
        assert top[0] <= nc.sbuf_usable_end, top[0] - nc.sbuf_usable_end
        top[0] = lay
        gob = put("gob", [P, DV])
        wgk = put("wgk", [P, NG * DK])
        bcum = put("bcum", [P, T])
        qe = put("qe", [P, T])
        ke = put("ke", [P, T])
        scanm = put("scanm", [P, SEQ])
        S = tmp[:, 0, 3 * DV:4 * DV]
        kdn = put("kdn", [P, 2, 2, P])
        aT = put("aT", [P, 2, P])
        wgh = put("wgh", [P, P])
        dec = put("dec", [P, 16])
        dec_s = put("dec_s", [P, NG, NS])
        qks = put("qks", [P, 8, NS])
        vs_f = put("vs_f", [P, 8, NS])
        rs_f = put("rs_f", [P, 8, NS])
        ss1 = put("ss1", [P, 2, 2])
        ss8 = put("ss8", [NS, NG])
        assert top[0] <= nc.sbuf_usable_end, top[0] - nc.sbuf_usable_end

        xT = at("xT", [P, KT, T], F32, A0)
        hh = at("hh", [P, KT, T], F32R, B0)
        hl = at("hl", [P, KT, T], F32R, C0)
        hid = [at(n, [P, 2, 2, T], F32R, F0 + i * 4 * TILE) for i, n in enumerate(("hid_hi", "hid_lo"))]
        ada = at("ada", [P, 4, KT, 512], F32, B0)
        xin = at("xin", [P, NB, D], F32, F0)
        vec1 = at("vec1", [P, P], F32, W0)
        vec2 = at("vec2", [16, P], F32, W0 + 512)
        c9 = at("c9", [NC, D], F32, W0 + 1024)
        c9e = at("c9e", [NC, D], F32, W0 + 1024 + 4096)
        xs = at("xs", [NS, D], F32, W0 + 1024 + 8192)
        sconv = at("sconv", [16, 512], F32, W0 + 1024 + 12288)
        scT = at("scT", [P, KT, NC], F32, W0 + 1024 + 12288 + 2048)
        modrow = at("modrow", [NC, 2, 512], F32, W0 + 16384)
        rstd = at("rstd", [P, T], F32, F0)
        sqsum = at("sqsum", [P, T], F32, F0 + TILE)
        qstore = nc.dram_tensor("qstore", (NS, 512), F32, kind="Internal").ap()
        xstore = nc.dram_tensor("xstore", (P, KT * T), F32, kind="Internal").ap()
        QK = at("QK", [P, 2, NB, NH * HD], F32, A0)
        Vn = at("Vn", [P, NB, NH * HD], F32, F0)
        ya = at("ya", [P, 4, T], F32, F0 + 16384)
        sq8 = at("sq8", [NS, 2, 512], F32, C0)
        crow = at("crow", [10, 512], F32, C0 + 8192)
        sqs = at("sqs", [P, 2, NB, NH * HD], F32, B0)
        qT = at("qT", [HD + 2, SEQ], F32, B0)
        kT = at("kT", [HD + 2, SEQ], F32, B0 + 4096)
        PT = at("PT", [P, NB * (NB + 1) // 2 * P], F32, B0 + 8192)
        rden = at("rden", [P, SEQ], F32, B0 + 26624)
        qbc = at("qbc", [P, 512], F32, B0 + 30720)
        mx8 = at("mx8", [P, 8], F32, B0 + 32768)
        small = at("small", [P, 32], F32, B0 + 32768 + 32)
        Vp = at("Vp", [P, NB, P], F32, TMP0)
        Psum = at("Psum", [P, SEQ], F32, TMP0 + 4096)
        omask = sNat[:, 1, :]
        LT = at("LT", [P, NH, P], F32, B0)
        TB = at("TB", [P, NH, P], F32, B0 + 4096)
        LN = at("LN", [8, NH, P], F32, B0 + 8192)
        ptot = at("ptot", [P, NH], F32, B0 + 12288)
        pages = at("pages", [P, 8, 2, 512], F32, C0)
        qk1 = at("qk1", [P, KT, T], F32, A0)
        Vo = at("Vo", [P, NB, D], F32, F0)
        sst = at("sst", [P, NS, DV], F32, B0)
        sout = at("sout", [P, NS, DV], F32, B0 + 8192)
        kmask = at("kmask", [NS, NS, P], F32, B0 + 16384)
        qmask = at("qmask", [P, NS, NS], F32, B0 + 20480)
        kvnat = at("kvnat", [NS, NG * DK + D], F32, B0 + 20736)
        osn = at("osn", [NS, D], F32, B0 + 26880)
        ynat = at("ynat", [P, NB, D], F32, F0)
        ysn = at("ysn", [NS, D], F32, B0)

        ps = ctx.enter_context(nc.psum_tensor("ps", [P, 8, 512], F32))

        def acc(par):
            return ps[:, 3 * par:3 * par + 3, 0:CH]

        def thirds(ap):
            return ap.rearrange("p (c n) -> p c n", c=3)

        def sem(name):
            return ctx.enter_context(nc.semaphore(name))

        consts_made = sem("consts_made")
        small_loaded = sem("small_loaded")
        x_loaded = sem("x_loaded")
        ada_loaded = [sem(f"ada_loaded{i}") for i in range(4)]
        w_loaded = [sem(f"w_loaded{i}") for i in range(2)]
        w_split = sem("w_split")
        acc_done = sem("acc_done")
        acc_free = [sem("acc_free0"), sem("acc_free1")]
        passed = sem("passed")
        pool_link = sem("pool_link")
        dve_link = sem("dve_link")
        act_link = sem("act_link")
        setup_pe = sem("setup_pe")
        setup_dve = sem("setup_dve")
        silu_pos = sem("silu_pos")
        ada_done = sem("ada_done")
        mod_rows = sem("mod_rows")
        mod_turned = sem("mod_turned")
        ada_kept = sem("ada_kept")
        xt_done = sem("xt_done")
        xt_kept = sem("xt_kept")
        sq_ready = sem("sq_ready")
        sq_added = sem("sq_added")
        sq_summed = sem("sq_summed")
        rstd_ready = sem("rstd_ready")
        norm_scaled = sem("norm_scaled")
        norm_affine = sem("norm_affine")
        norm_hi = sem("norm_hi")
        h_ready = sem("h_ready")
        x_spilled = sem("x_spilled")
        x_back = sem("x_back")
        tmp_full = sem("tmp_full")
        nat_done = sem("nat_done")
        nat_kept = sem("nat_kept")
        relu_ready = sem("relu_ready")
        hid_squared = sem("hid_squared")
        hid_hi_ready = sem("hid_hi_ready")
        hid_ready = sem("hid_ready")
        x_done = sem("x_done")
        prep_pe = sem("prep_pe")
        prep_act = sem("prep_act")
        prep_dve = sem("prep_dve")
        kv_out = sem("kv_out")
        outs = sem("outs")
        a_built = sem("a_built")
        a_turned = sem("a_turned")
        a_q = sem("a_q")
        a_k = sem("a_k")
        a_s = sem("a_s")
        a_max = sem("a_max")
        a_shift = sem("a_shift")
        a_again = sem("a_again")
        a_q2 = sem("a_q2")
        a_st = sem("a_st")
        a_p = sem("a_p")
        a_av = sem("a_av")
        a_sum = sem("a_sum")
        a_den = sem("a_den")
        a_lnd = sem("a_lnd")
        a_rden = sem("a_rden")
        a_pair = sem("a_pair")
        vp_ready = sem("vp_ready")
        q_stored = sem("q_stored")
        qbc_in = sem("qbc_in")
        lf_gathered = sem("lf_gathered")
        pages_in = [sem(f"pages_in{i}") for i in range(8)]
        k_used = sem("k_used")
        v_used = sem("v_used")
        d_pe = sem("d_pe")
        d_act = sem("d_act")
        d_dve = sem("d_dve")
        y_hi = sem("y_hi")
        y_ready = sem("y_ready")
        g_pe = sem("g_pe")
        g_act = sem("g_act")
        g_dve = sem("g_dve")
        gb_a = sem("gb_a")
        gb_scores = sem("gb_scores")
        gb_kd = sem("gb_kd")
        gb_state = sem("gb_state")
        gb_inter = sem("gb_inter")
        gb_kv = sem("gb_kv")
        gb_rs = sem("gb_rs")
        gb_out = sem("gb_out")
        g_stored = sem("g_stored")
        gate_cleared = sem("gate_cleared")
        gate_loaded = sem("gate_loaded")
        r_exp = sem("r_exp")
        r_done = sem("r_done")
        s_act = sem("s_act")
        s_ss = sem("s_ss")
        s_out = sem("s_out")
        gla_stored = sem("gla_stored")
        y_s = sem("y_s")
        g_tr = sem("g_tr")
        g_trk = sem("g_trk")
        s_in = sem("s_in")
        s_pe = sem("s_pe")
        s_dve = sem("s_dve")
        y_turned = sem("y_turned")
        y_kept = sem("y_kept")

        block = ctx.enter_context(nc.Block())

        wie = w_in_even[0].rearrange("(k p) n -> p k n", p=P)
        woe = w_out_even[0].rearrange("(k p) n -> p k n", p=P)
        wio = w_in_odd[0].rearrange("(k p) n -> p k n", p=P)
        woo = w_out_odd[0].rearrange("(k p) n -> p k n", p=P)
        E_IN, O_IN = w_in_even.shape[2], w_in_odd.shape[2]

        U_IN, U_OUT, U_MLP = [0, 97], [25, 122], [33, 130]
        T_NORM, T_IN, T_OUT, T_MLP = [0, 34, 195, 229], [1, 196], [26, 221], [35, 230]
        N_UNITS = 194
        SMALL = 14

        query_pieces = [(i, c, 512 * c, min((i + 1) * P, 512 * (c + 1)) - 512 * c)
                        for i in range(NB) for c in range(2) if 512 * c < (i + 1) * P]
        key_pieces = [(j, c, max(512 * c, j * P), 512 * (c + 1) - max(512 * c, j * P))
                      for j in range(NB) for c in range(2) if 512 * (c + 1) > j * P]
        NP = len(key_pieces)
        key_at = [sum(SEQ - m * P for m in range(j)) for j in range(NB)]

        def all_read(eng, t):
            eng.wait_ge(acc_free[0], (t + 1) // 2)
            eng.wait_ge(acc_free[1], t // 2)

        def done(t, nn):
            return t.plus(1 - nn).v

        @block.sync
        def _(sp):
            def small_load(dst, src):
                sp.dma_start(dst, src).then_inc(small_loaded, 16)

            small_load(vec1[0:96, :], b_ada.rearrange("l (n p) -> (l n) p", p=P))
            small_load(vec1[96:112, :], g_mix.rearrange("l (n p) -> (l n) p", p=P))
            small_load(vec1[112:128, :], g_ffn.rearrange("l (n p) -> (l n) p", p=P))
            small_load(vec2[0:12, :], w_conv[0].rearrange("j (c p) -> (j c) p", p=P))
            small_load(vec2[12:16, :], b_gk.rearrange("o (c p) -> (o c) p", p=P))
            small_load(c9[0:NS, :], c_sample)
            small_load(c9[NS:NC, :], c_prompt)
            small_load(xs[:, :], x_sample.rearrange("b s d -> (b s) d"))
            small_load(sconv[:, :], state_conv.rearrange("b e j c -> (b e j) c"))
            small_load(gqb[:, :], g_q.to_broadcast([P, HD]))
            small_load(gkb[:, :], g_k.to_broadcast([P, HD]))
            small_load(bfb[:, :], b_f.to_broadcast([P, NH]))
            small_load(idx[:, :], page_table.rearrange("b (p o) -> (b p) o", o=1))
            small_load(pt[:, :], page_table.rearrange("(o b) p -> o (b p)", o=1))
            for b in range(NB):
                sp.dma_start(xin[:, b, :], x_prompt[0, b * P:(b + 1) * P, :]).then_inc(x_loaded, 16)

            def load_ada(i, l):
                if l or i.c >= 4 or i.L:
                    sp.wait_ge(ada_done, i.plus(12 * l - 3).v)
                sp.dma_start(ada[:, i.c % 4, :, :],
                             w_ada[l].rearrange("(k p) n -> p k n", p=P)[:, :, ds(i.times(512).v, 512)]
                             ).then_inc(ada_loaded[i.c % 4], 16)

            for l in range(DEPTH):
                loop(sp, 12, 4, lambda i: load_ada(i, l), peel=4)

            def load_unit(u, src):
                if u.c >= 2 or u.L:
                    sp.wait_ge(w_split, u.plus(-1).v)
                sp.sem_inc(passed, 1)
                dst = stage[:, u.c % 2, :]
                if len(src.shape) == 3:
                    dst = dst.rearrange("p (k n) -> p k n", n=P)
                sp.dma_start(dst, src).then_inc(w_loaded[u.par], 16)

            def in_units(base, w, col, n, per=4):
                loop(sp, n, per, lambda i: load_unit(i.plus(base), w[:, :, ds(i.times(P).plus(col).v, P)]), peel=2)

            def mlp_units(l):
                base = U_MLP[l]
                w1 = w_ff1[l].rearrange("(k p) n -> p k n", p=P)
                w2 = w_ff2[l].rearrange("(r p) n -> p r n", p=P)

                def up(i, u):
                    for j in range(2):
                        load_unit(u.plus(j), w1[:, :, ds(i.times(256).plus(128 * j).v, P)])

                def down(i, u):
                    for j in range(2):
                        load_unit(u.plus(j), w2[:, ds(i.times(2).plus(j).v, 1), :].rearrange("p r n -> p (r n)"))

                def step(i):
                    up(i.plus(1), i.times(4).plus(base + 2))
                    down(i, i.times(4).plus(base + 4))

                up(V(0), V(base))
                loop(sp, NPAIR - 1, 1, step)
                down(V(NPAIR - 1), V(base + 62))

            sp.wait_ge(ada_done, 24)
            sp.wait_ge(setup_dve, 4)
            in_units(U_IN[0], wie, 1536, 12)

            def conv_units(c):
                for j, col in enumerate((512, 1024, 0)):
                    load_unit(c.times(3).plus(U_IN[0] + 12 + j), wie[:, :, ds(c.times(P).plus(col).v, P)])
            loop(sp, 4, 2, conv_units)
            load_unit(V(U_IN[0] + 24), wie[:, :, E_IN - P:E_IN])
            for i in range(6):
                load_unit(V(U_OUT[0] + i), woe[:, :, i * P:(i + 1) * P])
            sp.wait_ge(prep_dve, 6)
            tok = "(b p) h d -> p b (h d)"
            for dst, src in ((k_prompt[0, 0].rearrange(tok, p=P), QK[:, 1]), (v_prompt[0, 0].rearrange(tok, p=P), Vn[:, :, :]),
                             (logf_prompt[0, 0].rearrange("(b p) h -> p b h", p=P), lf[:, 0:NB, :]),
                             (k_sample.rearrange("b e s h d -> (b e s) (h d)"), sNat[:, 1, :]),
                             (v_sample.rearrange("b e s h d -> (b e s) (h d)"), sNat[:, 2, :]),
                             (logf_sample.rearrange("b e s h -> (b e s) h"), lf[0:NS, NB, :])):
                sp.dma_start(dst, src).then_inc(kv_out, 16)
            cs = conv_sample.rearrange("b e j c -> (b e) j c")
            sp.dma_start(cs[:, 0, :], state_conv.rearrange("b e j c -> (b e) j c")[:, 1, :]).then_inc(kv_out, 16)
            sp.dma_start(cs[:, 1, :], crow[0:NS, :]).then_inc(kv_out, 16)
            sp.dma_start(conv_prompt[0, 0], crow[NS:10, :]).then_inc(kv_out, 16)

            sp.dma_start(qstore, sNat[:, 0, :]).then_inc(q_stored, 16)
            sp.wait_ge(q_stored, 16)
            sp.wait_ge(kv_out, 16 * 9)
            sp.wait_ge(d_pe, 2)

            def load_pages(b):
                if b.c or b.L:
                    sp.wait_ge(k_used, b.times(8).v)
                sp.sem_inc(passed, 1)
                sp.dma_start(qbc[:, :], qstore[ds(b.v, 1), :].to_broadcast([P, 512])).then_inc(qbc_in, 16)
                for j in range(16):
                    cache = cache_k if j < 8 else cache_v
                    if j >= 8:
                        sp.wait_ge(k_used, b.times(8).plus(j - 7).v)
                    elif b.c or b.L:
                        sp.wait_ge(v_used, b.times(8).plus(j - 7).v)
                    sp.sem_inc(passed, 1)
                    for q in range(2):
                        page = sp.value_load(pt[0:1, ds(b.times(PAGES).plus(2 * (j % 8) + q).v, 1)],
                                             min_val=0, max_val=cache_k.shape[0] - 1)
                        sp.dma_start(pages[:, j % 8, q, :], cache[ds(page, 1), 0].rearrange("a p h d -> (a p) (h d)")
                                     ).then_inc(pages_in[j % 8], 16)
            load_pages(V(0))
            loop(sp, NS - 1, 1, lambda b: load_pages(b.plus(1)))

            sp.wait_ge(x_spilled, 16)
            sp.wait_ge(y_ready, KT)
            sp.dma_start(xT[:, :, :], xstore.rearrange("p (k n) -> p k n", k=KT)).then_inc(x_back, 16)
            for i in (6, 7):
                load_unit(V(U_OUT[0] + i), woe[:, :, i * P:(i + 1) * P])
            mlp_units(0)

            sp.wait_ge(gate_cleared, 1)
            sp.dma_start(gob[:, :], g_o.to_broadcast([P, DV])).then_inc(gate_loaded, 16)
            sp.dma_start(wgk[P - 16:P, :], w_gk[0]).then_inc(gate_loaded, 16)
            in_units(U_IN[1], wio, 0, 16)
            load_unit(V(U_IN[1] + 16), wio[:, :, O_IN - P:O_IN])
            in_units(U_IN[1] + 17, wio, 2048, 8)
            sp.wait_ge(x_spilled, 32)
            for h in range(NG):
                if h:
                    sp.wait_ge(s_dve, 10 * h)
                else:
                    all_read(sp, T_IN[1] + 25)
                sp.dma_start(sst[:, :, :], state_gla[:, 0, h].rearrange("b k v -> k b v")).then_inc(s_in, 16)
                sp.wait_ge(s_dve, 10 * h + 10)
                sp.dma_start(gla_sample[:, 0, h].rearrange("b k v -> k b v"), sout[:, :, :]).then_inc(gla_stored, 16)
            load_unit(V(U_OUT[1]), woo[:, :, 0:P])
            load_unit(V(U_OUT[1] + 1), woo[:, :, P:2 * P])
            sp.wait_ge(y_ready, 2 * KT)
            sp.dma_start(xT[:, :, :], xstore.rearrange("p (k n) -> p k n", k=KT)).then_inc(x_back, 16)
            in_units(U_OUT[1] + 2, woo, 256, 6)
            mlp_units(1)
            for b in range(NB):
                sp.wait_ge(y_kept, b + 1)
                sp.dma_start(y_prompt[0, b * P:(b + 1) * P, :], ynat[:, b, :]).then_inc(outs, 16)
            sp.wait_ge(y_kept, NB + 1)
            sp.dma_start(y_sample.rearrange("b s d -> (b s) d"), ysn[:, :]).then_inc(outs, 16)
            sp.wait_ge(outs, 16 * (NB + 1))
            sp.wait_ge(gla_stored, 16 * NG)

        used_at = {}
        for l in range(DEPTH):
            nn = 2 * l + 1
            for i in range(25):
                used_at[U_IN[l] + i] = T_IN[l] - nn + i + 1
            for i in range(8):
                used_at[U_OUT[l] + i] = T_OUT[l] - nn + i + 1
            nn += 1
            for j in range(2):
                used_at[U_MLP[l] + j] = T_MLP[l] - nn + j + 1
            for i in range(NPAIR):
                if i < NPAIR - 1:
                    for j in range(2):
                        used_at[U_MLP[l] + 2 + 4 * i + j] = T_MLP[l] - nn + 10 * i + 2 + j + 1
                last = i < NPAIR - 1
                for j in range(2):
                    used_at[U_MLP[l] + (4 if last else 2) + 4 * i + j] = T_MLP[l] - nn + 10 * i + (12 if last else 10)

        @block.gpsimd
        def _(pool):
            link = Link(pool, pool_link)

            def select(t, cmp, fill, base, pattern, mult):
                link(pool.affine_select(out=t, in_=t, compare_op=cmp, fill=fill, base=base, pattern=pattern,
                                        channel_multiplier=mult))

            for t, v in ((ident, 0.0), (ones, 1.0), (tri, 1.0), (trisuf, 1.0), (later, 1.0), (pairmask, 1.0),
                         (eye8, 0.0), (headrow, 0.0), (only8, 0.0), (identb, 0.0), (negb, 0.0), (eps, EPS)):
                link(pool.memset(t[tuple(slice(None) for _ in t.shape)], v))
            select(ident[:, :], ALU.not_equal, 1.0, 0, [[-1, P]], 1)
            select(identb[:, :], ALU.not_equal, 1.0, 0, [[-1, P]], 1)
            select(tri[:, :], ALU.is_ge, 0.0, 0, [[1, P]], -1)
            select(trisuf[:, :], ALU.is_ge, 0.0, -1, [[-1, P]], 1)
            select(later[:, :], ALU.is_ge, 0.0, -1, [[-1, P]], 1)
            select(later[:, :].rearrange("p (b g) -> p b g", g=PAGES), ALU.is_ge, 0.0, PAGES - 1,
                   [[PAGES, NS], [0, PAGES]], -1)
            select(pairmask[:, :], ALU.is_ge, 0.0, 0, [[1, P]], -1)
            select(pairmask[:, :].rearrange("p (c r) -> p c r", r=CHUNK), ALU.is_ge, 0.0, 0,
                   [[-CHUNK, 2], [0, CHUNK]], 1)
            select(eye8[:, :, :], ALU.not_equal, 1.0, 0, [[1, 8], [-1, 8]], 0)
            select(headrow[:, :, :], ALU.not_equal, 1.0, 0, [[-1, NH], [0, HD]], 1)
            select(only8[:, :], ALU.is_equal, NEG, 0, [[-1, 8]], 1)
            pool.affine_select(out=negb[:, :], in_=negb[:, :], compare_op=ALU.is_ge, fill=NEG, base=0,
                               pattern=[[-1, P]], channel_multiplier=1).then_inc(consts_made, 1)
            pool.wait_ge(small_loaded, 16 * SMALL)
            pool.indirect_dma_start(Lraw[:, :, :].rearrange("p s h -> p (s h)"), None,
                                    cache_logf.rearrange("a e s h -> (a e) (s h)"),
                                    bass.IndirectOffsetOnAxis(ap=idx[:, 0:1].bitcast(U32), axis=0)
                                    ).then_inc(lf_gathered, 16)

            def split(u, used=None):
                if used is None and u.c >= 4:
                    used = V(used_at[u.c - 4])
                if used is not None:
                    pool.wait_ge(acc_done, used.v)
                pool.wait_ge(w_loaded[u.par], u.half.times(16).plus(16).v)
                pool.sem_inc(passed, 1)
                link(pool.tensor_copy(whi[:, u.c % 4, :], stage[:, u.c % 2, :]))
                pool.tensor_tensor(wlo[:, u.c % 4, :], stage[:, u.c % 2, :], whi[:, u.c % 4, :].bitcast(F32),
                                   ALU.subtract).then_inc(w_split, 1)

            def in_split(base, first, n):
                loop(pool, n, 4, lambda i: split(i.plus(base + first), i.plus(used_at[base + first - 4])
                                                 if first >= 4 else None), link, 1)

            for l in range(DEPTH):
                for i in range(4):
                    split(V(U_IN[l] + i))
                in_split(U_IN[l], 4, 20)
                split(V(U_IN[l] + 24))
                for i in range(4):
                    split(V(U_OUT[l] + i))
                if l == 0:
                    pool.wait_ge(prep_dve, 6)

                    def head(h):
                        n = h.times(NP)
                        pool.wait_ge(a_p, n.plus(2).v)
                        if h.c or h.L:
                            pool.wait_ge(a_den, h.v)
                        pool.sem_inc(passed, 1)
                        link(pool.tensor_copy(Psum[:, :], PT[:, 0:SEQ]))
                        for j in range(1, NB):
                            pool.wait_ge(a_p, n.plus(2 + sum(1 for q in key_pieces if 1 <= q[0] <= j)).v)
                            o = Psum[:, j * P:SEQ]
                            add = pool.tensor_tensor(o, o, PT[:, key_at[j]:key_at[j] + SEQ - j * P], ALU.add)
                            if j < NB - 1:
                                link(add)
                        add.then_inc(a_sum, 1)
                        pool.wait_ge(a_sum, h.plus(1).v)

                    def pair(p):
                        if p.c or p.L:
                            pool.wait_ge(a_av, p.times(2).v)
                        pool.sem_inc(passed, 1)
                        pool.tensor_copy(Vp[:, :, :], Vn[:, :, ds(p.times(P).v, P)]).then_inc(vp_ready, 1)
                        for e in range(2):
                            head(p.times(2).plus(e))
                    loop(pool, NH // 2, 1, pair, link, 2 * (NB - 1), peel=1)
                for i in range(4, 8):
                    split(V(U_OUT[l] + i))
                for i in range(6):
                    split(V(U_MLP[l] + i))
                base, done = U_MLP[l], T_MLP[l] - 2 * l - 2

                def step(i):
                    for j in range(2):
                        split(i.times(4).plus(base + 2 + j), i.times(10).plus(done - 8 + j + 1))
                    for j in range(2):
                        split(i.times(4).plus(base + 4 + j), i.times(10).plus(done + 2))
                loop(pool, NPAIR - 2, 1, lambda i: step(i.plus(1)), link, 4)
                for j in range(2):
                    split(V(U_MLP[l] + 62 + j))

        @block.tensor
        def _(pe):
            def turn(out, in_):
                k = in_.shape[0]
                return pe.transpose(out, in_, ident[0:k, 0:k])

            def acc_wait(t):
                if t.c >= 2 or t.L:
                    pe.wait_ge(acc_free[t.par], t.half.v)

            def product(t, parts):
                acc_wait(t)
                n = len(parts)
                for k, (wh, wl, xh, xl) in enumerate(parts):
                    for q, (w, x) in enumerate(((wh, xh), (wh, xl), (wl, xh))):
                        for c in range(3):
                            last = pe.matmul(ps[:, 3 * t.par + c, 0:CH], w, x[:, c * CH:(c + 1) * CH],
                                             start=(k == 0 and q == 0), stop=(k == n - 1 and q == 2))
                last.then_inc(acc_done, 1)

            def gemm(u, t):
                pe.wait_ge(w_split, u.plus(1).v)
                s = u.c % 4
                product(t, [(whi[:, s, k * P:(k + 1) * P], wlo[:, s, k * P:(k + 1) * P], hh[:, k, :], hl[:, k, :])
                            for k in range(KT)])

            def gemm_pair(u, t, ready, n):
                pe.wait_ge(w_split, u.plus(2).v)
                acc_wait(t)
                acc_wait(t.plus(1))
                for k in range(KT):
                    pe.wait_ge(ready, KT * n + k + 1)
                    for j in range(2):
                        s = (u.c + j) % 4
                        wh, wl = whi[:, s, k * P:(k + 1) * P], wlo[:, s, k * P:(k + 1) * P]
                        for q, (w, x) in enumerate(((wh, hh), (wh, hl), (wl, hh))):
                            for c in range(3):
                                last = pe.matmul(ps[:, 3 * ((t.c + j) % 2) + c, 0:CH], w, x[:, k, c * CH:(c + 1) * CH],
                                                 start=(k == 0 and q == 0), stop=(k == KT - 1 and q == 2))
                        if k == KT - 1:
                            last.then_inc(acc_done, 1)

            def norm(n):
                t = V(T_NORM[n])
                acc_wait(t)
                pe.wait_ge(sq_added, (KT - 1) * (n + 1))
                for c in range(3):
                    last = pe.matmul(ps[:, 3 * t.par + c, 0:CH], ones[:, :], sqsum[:, c * CH:(c + 1) * CH],
                                     start=True, stop=True)
                last.then_inc(sq_summed, 1)

            def to_tokens(i):
                pe.wait_ge(tmp_full, i.plus(1).v)
                if i.c or i.L:
                    pe.wait_ge(nat_kept, i.v)
                for b in range(NB):
                    last = turn(ps[:, 6 + b // 4, (b % 4) * P:(b % 4 + 1) * P],
                                tmp[:, i.c % 2, NS + b * P:NS + (b + 1) * P])
                last.then_inc(nat_done, 1)

            def mlp(l):
                u0, t0 = U_MLP[l], T_MLP[l]

                def up(i, u, t):
                    for j in range(2):
                        gemm(u.plus(j), t.plus(j))

                def down(i, u, t):
                    pe.wait_ge(w_split, u.plus(2).v)
                    pe.wait_ge(hid_ready, i.times(2).plus(2 * NPAIR * l + 2).v)
                    for f in range(KT):
                        product(t.plus(f), [(whi[:, (u.c + j) % 4, f * P:(f + 1) * P],
                                             wlo[:, (u.c + j) % 4, f * P:(f + 1) * P],
                                             hid[0][:, i.c % 2, j, :], hid[1][:, i.c % 2, j, :]) for j in range(2)])

                def step(i):
                    up(i.plus(1), i.times(4).plus(u0 + 2), i.times(10).plus(t0 + 2))
                    down(i, i.times(4).plus(u0 + 4), i.times(10).plus(t0 + 4))
                gemm_pair(V(u0), V(t0), h_ready, 2 * l + 1)
                loop(pe, NPAIR - 1, 2, step, peel=1)
                down(V(NPAIR - 1), V(u0 + 62), V(t0 + 152))

            def out_proj(l):
                gemm_pair(V(U_OUT[l]), V(T_OUT[l]), y_ready, l)
                for i in range(2, KT):
                    gemm(V(U_OUT[l] + i), V(T_OUT[l] + i))

            pe.wait_ge(consts_made, 1)
            pe.wait_ge(small_loaded, 16 * SMALL)
            turn(ps[:, 0, 0:P], vec1[:, :])
            turn(ps[:, 0, P:P + 16], vec2[:, :])
            for c in range(4):
                turn(ps[:, 0, 256 + 16 * c:272 + 16 * c], sconv[:, c * P:(c + 1) * P])
            for k in range(KT):
                last = turn(ps[:, 1, NS * k:NS * k + NS], xs[:, k * P:(k + 1) * P])
            last.then_inc(setup_pe, 1)
            pe.wait_ge(setup_dve, 2)
            for k in range(KT):
                last = turn(ps[:, 1, P + NC * k:P + NC * (k + 1)], c9[:, k * P:(k + 1) * P])
            last.then_inc(setup_pe, 1)
            pe.wait_ge(x_loaded, 16 * NB)
            for k in range(KT):
                if k >= 2:
                    pe.wait_ge(xt_kept, k - 1)
                for b in range(NB):
                    last = turn(ps[:, 2 + 2 * (k % 2) + b // 4, (b % 4) * P:(b % 4 + 1) * P],
                                xin[:, b, k * P:(k + 1) * P])
                last.then_inc(xt_done, 1)
            pe.wait_ge(setup_dve, 3)

            def modulation_turned(i):
                pe.wait_ge(mod_rows, i.plus(1).v)
                if i.c >= 2 or i.L:
                    pe.wait_ge(ada_kept, i.plus(-1).v)
                pe.sem_inc(passed, 1)
                for f in range(4):
                    last = turn(ps[:, 4 + i.c % 2, NC * f:NC * (f + 1)], modrow[:, i.c % 2, f * P:(f + 1) * P])
                last.then_inc(mod_turned, 1)

            def modulation(i):
                pe.wait_ge(ada_loaded[i.c % 4], V(i.c // 4, i.g, i.L // 4).times(16).plus(16).v)
                if i.c >= 2 or i.L:
                    pe.wait_ge(mod_rows, i.plus(-1).v)
                for k in range(KT):
                    last = pe.matmul(ps[0:NC, 6 + i.c % 2, :], scT[:, k, :], ada[:, i.c % 4, k, :],
                                     start=(k == 0), stop=(k == KT - 1))
                last.then_inc(ada_done, 1)
                if i.c or i.L:
                    modulation_turned(i.plus(-1))
            pe.wait_ge(xt_kept, KT)
            loop(pe, 24, 4, modulation, peel=4)
            modulation_turned(V(23))

            norm(0)
            gemm_pair(V(U_IN[0]), V(T_IN[0]), h_ready, 0)
            to_tokens(V(0))

            def natural(i):
                gemm(i.plus(U_IN[0] + 1), i.plus(T_IN[0] + 1))
                to_tokens(i)
            loop(pe, 10, 4, lambda i: natural(i.plus(1)), peel=2)
            gemm(V(U_IN[0] + 12), V(T_IN[0] + 12))
            to_tokens(V(11))
            loop(pe, 12, 4, lambda i: gemm(i.plus(U_IN[0] + 13), i.plus(T_IN[0] + 13)))
            to_tokens(V(12))
            all_read(pe, T_IN[0] + 25)
            for i in range(12):
                turn(ps[0:NS, i // 4, (i % 4) * P:(i % 4 + 1) * P], sF[:, i, :])
            turn(ps[0:NS, 3, 0:P], sF[:, 12, :])
            for c in range(4):
                last = turn(ps[0:10, 4, c * P:(c + 1) * P], uOut[:, c, :])
            last.then_inc(prep_pe, 1)
            pe.wait_ge(prep_dve, 5)
            for b in range(NB):
                for j in range(b):
                    pe.matmul(ps[:, 5, NH * b:NH * (b + 1)], ones[:, :], lf[:, j, :], start=(j == 0), stop=False)
                last = pe.matmul(ps[:, 5, NH * b:NH * (b + 1)], tri[:, :], lf[:, b, :], start=(b == 0), stop=True)
            last.then_inc(prep_pe, 1)

            pe.wait_ge(lf_gathered, 16)
            pe.wait_ge(prep_dve, 6)
            for h in range(NH):
                last = turn(ps[:, 2 + h // 4, (h % 4) * P:(h % 4 + 1) * P], Lraw[:, :, h])
            last.then_inc(d_pe, 1)
            pe.wait_ge(d_dve, 1)
            for h in range(NH):
                o = ps[:, 6 + h // 4, (h % 4) * P:(h % 4 + 1) * P]
                pe.matmul(o, trisuf[:, :], LT[:, h, :], start=True, stop=False)
                pe.matmul(o, TB[:, h, :], later[:, :], start=False, stop=False)
                last = pe.matmul(o.rearrange("p (b g) -> p b g", g=PAGES), LN[:, h, :],
                                 ident[0:NS, 0:NS].unsqueeze(2).to_broadcast([NS, NS, PAGES]), start=False, stop=True)
            last.then_inc(d_pe, 1)
            pe.wait_ge(d_dve, 2)

            def sequence_peaks(b):
                pe.wait_ge(d_dve, b.times(6).plus(2 + 1).v)
                pe.sem_inc(passed, 1)
                turn(ps[0:8, 7, 0:P], mx8[:, :]).then_inc(d_pe, 1)

            def sequence_peak(b):
                pe.wait_ge(d_dve, b.times(6).plus(2 + 2).v)
                pe.sem_inc(passed, 1)
                pe.matmul(ps[:, 7, 128:136], ones[0:8, :], small[0:8, 8:16], start=True, stop=True).then_inc(d_pe, 1)

            def sequence_values(b, j):
                if j == 0:
                    pe.wait_ge(d_act, b.plus(1).v)
                pe.wait_ge(pages_in[j], b.times(64).plus(64).v)
                pe.sem_inc(passed, 1)
                for q in range(2):
                    last = pe.matmul(ps[0:8, 6, :], PBx[:, 2 * j + q, :], pages[:, j, q, :],
                                     start=(j == 0 and q == 0), stop=False)
                last.then_inc(v_used, 1)

            def sequence_sum(b):
                pe.matmul(ps[0:8, 6, :], PBx[0:NS, PAGES, :], sNat[:, 2, :], start=False, stop=True)
                pe.wait_ge(d_dve, b.times(6).plus(2 + 4).v)
                pe.sem_inc(passed, 1)
                pe.matmul(ps[0:8, 7, 144:145], small[:, 16:24], ones[:, 0:1], start=True, stop=True).then_inc(d_pe, 1)

            def sequence_out(b):
                pe.wait_ge(d_dve, b.times(6).plus(2 + 5).v)
                pe.sem_inc(passed, 1)
                for c in range(4):
                    last = pe.matmul(ps[:, 7, 152 + c:153 + c], omask[:, c * P:(c + 1) * P], ones[0:8, 0:1],
                                     start=True, stop=True)
                last.then_inc(d_pe, 1)

            def head(h, odd):
                n = h.times(NP)
                first = not (h.c or h.L)
                rows = slice(HD * odd, HD * (odd + 1))
                pe.wait_ge(a_built, h.plus(1).v)
                if not first:
                    pe.wait_ge(a_lnd, h.v)
                pe.sem_inc(passed, 1)
                for b in range(NB):
                    last = turn(ps[0:HD + 2, b // 4, (b % 4) * P:(b % 4 + 1) * P], KA[:, b, :])
                last.then_inc(a_turned, 1)
                if not first:
                    pe.wait_ge(a_p, n.v)
                    pe.sem_inc(passed, 1)
                for b in range(NB):
                    last = turn(ps[0:HD + 2, 4 + b // 4, (b % 4) * P:(b % 4 + 1) * P], QA[:, b, :])
                last.then_inc(a_turned, 1)
                pe.wait_ge(a_q, h.plus(1).v)
                pe.wait_ge(a_k, h.plus(1).v)
                for p, (i, c, lo, w) in enumerate(query_pieces):
                    if p >= 2:
                        pe.wait_ge(a_max, n.plus(p - 1).v)
                    pe.sem_inc(passed, 1)
                    diag = lo + w == (i + 1) * P
                    o = ps[:, 4 + p % 2, 0:w]
                    last = pe.matmul(o, qT[:, i * P:(i + 1) * P], kT[:, lo:lo + w], start=True, stop=not diag)
                    if diag:
                        last = pe.matmul(o[:, w - P:w], identb[:, :], negb[:, :], start=False, stop=True)
                    last.then_inc(a_s, 1)
                    if not first and 2 <= p < 10:
                        sequence_values(h.plus(-1), p - 2)
                if not first:
                    sequence_sum(h.plus(-1))
                pe.wait_ge(a_shift, h.plus(1).v)
                pe.sem_inc(passed, 1)
                for b in range(NB):
                    last = turn(ps[0:HD + 2, b // 4, (b % 4) * P:(b % 4 + 1) * P], QA[:, b, :])
                last.then_inc(a_again, 1)
                if not first:
                    sequence_out(h.plus(-1))
                pe.wait_ge(a_q2, h.plus(1).v)

                def scores(p):
                    j, c, lo, w = key_pieces[p]
                    if p >= 2:
                        pe.wait_ge(a_p, n.plus(p - 1).v)
                    pe.sem_inc(passed, 1)
                    diag = lo == j * P
                    o = ps[:, 4 + p % 2, 0:w]
                    last = pe.matmul(o, kT[:, j * P:(j + 1) * P], qT[:, lo:lo + w], start=True, stop=not diag)
                    if diag:
                        last = pe.matmul(o[:, 0:P], negb[:, :], identb[:, :], start=False, stop=True)
                    last.then_inc(a_st, 1)

                scores(0)
                pe.wait_ge(vp_ready, h.half.plus(1).v if h.L else h.c // 2 + 1)
                if not odd and not first:
                    pe.wait_ge(a_pair, h.half.v)
                for p, (j, c, lo, w) in enumerate(key_pieces):
                    if p + 1 < NP:
                        scores(p + 1)
                    pe.wait_ge(a_p, n.plus(p + 1).v)
                    pe.sem_inc(passed, 1)
                    last = pe.matmul(ps[rows, 2 + c, lo - 512 * c:512], Vp[:, j, rows],
                                     PT[:, key_at[j] + lo - j * P:key_at[j] + lo - j * P + w],
                                     start=(j == 0), stop=(j == 4 * c + 3))
                last.then_inc(a_av, 1)
                sequence_peaks(h)
                pe.wait_ge(a_sum, h.plus(1).v)
                pe.sem_inc(passed, 1)
                for c in range(2):
                    last = pe.matmul(ps[rows, c, :], ones[:, 0:HD], Psum[:, 512 * c:512 * (c + 1)], start=True, stop=True)
                last.then_inc(a_den, 1)
                sequence_peak(h)

            def pair(p):
                for e in range(2):
                    head(p.times(2).plus(e), e)
            loop(pe, NH // 2, 1, pair, peel=1)
            for j in range(8):
                sequence_values(V(NS - 1), j)
            sequence_sum(V(NS - 1))
            sequence_out(V(NS - 1))
            out_proj(0)
            norm(1)
            mlp(0)

            norm(2)
            gemm_pair(V(U_IN[1]), V(T_IN[1]), h_ready, 2)
            loop(pe, 6, 4, lambda i: gemm(i.plus(U_IN[1] + 2), i.plus(T_IN[1] + 2)), peel=2)
            gemm(V(U_IN[1] + 8), V(T_IN[1] + 8))

            def values(i):
                gemm(i.plus(U_IN[1] + 9), i.plus(T_IN[1] + 9))
                to_tokens(i.plus(13))
            loop(pe, 8, 4, values)

            def gla_head(h):
                pe.wait_ge(g_dve, h.times(6).plus(1).v)
                for c in range(3):
                    last = pe.matmul(ps[:, c, 0:CH], wgh[:, :], tmp[:, 1, c * CH:(c + 1) * CH], start=True, stop=True)
                last.then_inc(g_pe, 1)
                pe.wait_ge(g_dve, h.times(6).plus(6).v)
                n = h.times(NB)
                first = not (h.c or h.L)

                def scores(b):
                    cols = slice(NS + b * P, NS + (b + 1) * P)
                    pe.matmul(ps[:, 0, 0:P], ke[:, cols], qe[:, cols], start=True, stop=True).then_inc(gb_a, 1)
                    turn(ps[:, 1, 0:P], bcum[:, cols]).then_inc(gb_a, 1)

                def turned(b):
                    m = n.plus(b)
                    pe.wait_ge(gb_out, m.plus(1).v)
                    if b or not first:
                        pe.wait_ge(g_trk, m.v)
                    pe.sem_inc(passed, 1)
                    for e in range(2):
                        last = turn(ps[:, 6, e * P:(e + 1) * P],
                                    tmp[:, 0, DV * (b % 2) + e * P:DV * (b % 2) + (e + 1) * P])
                    last.then_inc(g_tr, 1)

                scores(0)
                for b in range(NB):
                    m = n.plus(b)
                    pe.wait_ge(gb_scores, m.plus(1).v)
                    pe.wait_ge(gb_kd, m.plus(1).v)
                    pe.sem_inc(passed, 1)
                    if b + 1 < NB:
                        scores(b + 1)
                    v = Vo[:, b, ds(h.times(DV).v, DV)]
                    if b >= 2 or not first:
                        pe.wait_ge(gb_out, m.plus(-1).v)
                    O = ps[:, 2 + b % 2, 0:DV]
                    pe.matmul(O, aT[:, b % 2, :], v, start=True, stop=False, skip_group_check=True)
                    state = h.times(2 * NB + 1).plus(2 * b + 1)
                    pe.matmul(ps[:, 4, 0:DV], kdn[:, b % 2, 0, :], v, start=True, stop=True).then_inc(gb_kv, 1)
                    pe.wait_ge(gb_state, state.v)
                    pe.matmul(ps[:, 5, 0:DV], kdn[:, b % 2, 1, :], v, start=True, stop=True).then_inc(gb_kv, 1)
                    for c in range(2):
                        half = slice(CHUNK * c, CHUNK * (c + 1))
                        if c:
                            if b:
                                turned(b - 1)
                            pe.wait_ge(gb_state, state.plus(1).v)
                        pe.matmul(O[half, :], qe[:, NS + b * P + CHUNK * c:NS + b * P + CHUNK * (c + 1)], S[:, :],
                                  start=False, stop=(c == 1), skip_group_check=True).then_inc(gb_inter, 1)
                turned(NB - 1)
            all_read(pe, T_IN[1] + 17)
            loop(pe, NG, 1, gla_head, peel=1)
            loop(pe, 8, 4, lambda i: gemm(i.plus(U_IN[1] + 17), i.plus(T_IN[1] + 17)))

            all_read(pe, T_IN[1] + 25)
            for i in range(12):
                last = turn(ps[0:NS, i // 4, (i % 4) * P:(i % 4 + 1) * P], qks[:, 4 + i, :] if i < 4 else vs_f[:, i - 4, :])
            last.then_inc(s_pe, 1)
            for h in range(NG):
                pe.wait_ge(s_dve, 1 + 10 * h + 1)
                for b in range(NS):
                    def outer(b):
                        pe.matmul(ps[:, 3 + b % 2, 0:DV], kmask[:, b, :], kvnat[:, 512 + h * DV:512 + (h + 1) * DV],
                                  start=True, stop=True).then_inc(s_pe, 1)
                    if b == 0:
                        outer(0)
                        outer(1)
                    pe.wait_ge(s_dve, 1 + 10 * h + 1 + b + 1)
                    pe.matmul(ps[0:NS, 5, 0:DV], qmask[:, b, :], sout[:, b, :], start=(b == 0), stop=(b == NS - 1)
                              ).then_inc(s_out, 1)
                    if b + 2 < NS:
                        outer(b + 2)
            pe.wait_ge(s_dve, 42)
            for k in range(KT):
                last = turn(ps[:, 6, NS * k:NS * (k + 1)], osn[:, k * P:(k + 1) * P])
            last.then_inc(s_pe, 1)
            out_proj(1)
            norm(3)
            mlp(1)
            all_read(pe, T_MLP[1] + 160)
            for b in range(NB + 1):
                if b >= 2:
                    pe.wait_ge(y_kept, b - 1)
                for k in range(KT):
                    if b < NB:
                        last = turn(ps[:, 2 * (b % 2) + k // 4, (k % 4) * P:(k % 4 + 1) * P],
                                    xT[:, k, NS + b * P:NS + (b + 1) * P])
                    else:
                        last = turn(ps[0:NS, 2 * (b % 2) + k // 4, (k % 4) * P:(k % 4 + 1) * P], xT[:, k, 0:NS])
                last.then_inc(y_turned, 1)

        @block.scalar
        def _(act):
            link = Link(act, act_link)

            def rsqrt(out, in_, n, sem, read=None, read_count=None):
                if read is None:
                    link(act.activation(out, in_, ACT.Ln, bias=eps[0:out.shape[0], 0:1], scale=1.0 / n))
                else:
                    act.activation(out, in_, ACT.Ln, bias=eps[0:out.shape[0], 0:1], scale=1.0 / n).then_inc(read, 1)
                    act.wait_ge(read, read_count)
                act.activation(out, out, ACT.Exp, scale=-0.5).then_inc(sem, 1)

            def norm(n, last_tiles=None):
                l, w = n // 2, n % 2
                for k in range(KT):
                    if last_tiles is not None:
                        t = V(last_tiles + k)
                        act.wait_ge(acc_free[t.par], t.half.plus(1).v)
                    if k >= 3:
                        act.wait_ge(sq_added, (KT - 1) * n + k - 2)
                    act.activation(tmp[:, k % 2, :] if k else sqsum[:, :], xT[:, k, :], ACT.Square).then_inc(sq_ready, 1)
                t = V(T_NORM[n])
                act.wait_ge(sq_summed, n + 1)
                rsqrt(thirds(rstd[:, :]), acc(t.par), D, rstd_ready, acc_free[t.par], t.half.plus(1).v)
                for k in range(KT):
                    act.wait_ge(norm_scaled, KT * n + k + 1)
                    link(act.activation(tmp[:, k % 2, NS:T], tmp[:, k % 2, NS:T], ACT.Identity,
                                        bias=modT[:, l, 24 * w + k, NS:NC], scale=gain[:, n, k, NS:NC]))
                    act.wait_ge(norm_affine, KT * n + k + 1)
                    act.activation(hh[:, k, :], tmp[:, k % 2, :], ACT.Copy).then_inc(norm_hi, 1)

            def token_tile(i, t, nn, keep):
                act.wait_ge(acc_done, done(t, nn))
                if i.c >= 2 or i.L:
                    act.wait_ge(nat_done, i.plus(-1).v)
                act.activation(thirds(tmp[:, i.c % 2, :]), acc(t.par), ACT.Copy).then_inc(tmp_full, 1)
                act.activation(keep, ps[:, 3 * t.par, 0:NS], ACT.Copy).then_inc(acc_free[t.par], 1)

            def mlp(l):
                t0, nn = T_MLP[l], 2 * l + 2

                def up(i, t):
                    for j in range(2):
                        q = i.times(2).plus(2 * NPAIR * l + j)
                        act.wait_ge(acc_done, done(t.plus(j), nn))
                        if q.c >= 2 or q.L:
                            act.wait_ge(hid_ready, q.plus(-1).v)
                        tt = t.plus(j)
                        act.activation(thirds(tmp[:, j, :]), acc(tt.par), ACT.Relu).then_inc(acc_free[tt.par], 1)
                        act.wait_ge(hid_squared, q.plus(1).v)
                        act.activation(hid[0][:, i.c % 2, j, :], tmp[:, j, :], ACT.Copy).then_inc(hid_hi_ready, 1)
                up(V(0), V(t0))
                loop(act, NPAIR - 1, 2, lambda i: up(i.plus(1), i.times(10).plus(t0 + 2)), peel=1)

            act.wait_ge(small_loaded, 16 * SMALL)
            act.activation(c9e[:, :], c9[:, :], ACT.Exp, scale=-1.0).then_inc(silu_pos, 1)
            for k in range(KT):
                act.wait_ge(xt_done, k + 1)
                act.activation(xT[:, k, NS:T].rearrange("p (a n) -> p a n", a=2),
                               ps[:, 2 + 2 * (k % 2):4 + 2 * (k % 2), :], ACT.Copy).then_inc(xt_kept, 1)
            act.wait_ge(xt_kept, KT)

            def modulation(i):
                act.wait_ge(ada_done, i.plus(1).v)
                if i.c >= 2 or i.L:
                    act.wait_ge(mod_turned, i.plus(-1).v)
                act.activation(modrow[:, i.c % 2, :], ps[0:NC, 6 + i.c % 2, :], ACT.Copy).then_inc(mod_rows, 1)
            loop(act, 24, 2, modulation, peel=2)
            act.wait_ge(setup_dve, 4)
            norm(0)

            def residual_out(l):
                act.wait_ge(h_ready, KT * (2 * l + 1))
                act.dma_start(xstore.rearrange("p (k n) -> p k n", k=KT), xT[:, :, :]).then_inc(x_spilled, 16)
            residual_out(0)
            loop(act, 12, 2, lambda i: token_tile(i, i.plus(T_IN[0]), 1, sF[:, ds(i.v, 1), :].rearrange("p a n -> p (a n)")), peel=2)

            def conv(c):
                t = c.times(3).plus(T_IN[0] + 12)
                act.wait_ge(acc_done, done(t, 1))
                if c.c < 2 and not c.L:
                    act.wait_ge(nat_done, 12)
                else:
                    u = c.times(3).plus(T_IN[0] + 12 - 6 + 1)
                    act.wait_ge(acc_free[u.par], u.half.plus(1).v)
                act.activation(thirds(tmp[:, c.c % 2, :]), acc(t.par), ACT.Copy).then_inc(acc_free[t.par], 1)
            loop(act, 4, 2, conv, peel=2)
            all_read(act, T_IN[0] + 12 + 3 * 3 + 2)
            token_tile(V(12), V(T_IN[0] + 24), 1, sF[:, 12, :])
            act.wait_ge(nat_kept, 13)
            for j in range(2):
                last = act.activation(sqs[:, j], QK[:, j], ACT.Square)
            last.then_inc(prep_act, 1)
            act.wait_ge(prep_dve, 1)
            act.activation(sq8[:, :, :], sNat[:, 0:2, :], ACT.Square).then_inc(prep_act, 1)
            act.wait_ge(prep_dve, 3)
            link(act.activation(lft[:, :, :], lft[:, :, :], ACT.Exp))
            act.activation(lft[:, :, :], lft[:, :, :], ACT.Ln, bias=1.0).then_inc(prep_act, 1)
            act.wait_ge(prep_dve, 4)
            rsqrt(rsq[:, :], rsq[:, :], HD, prep_act)

            def sequence(b):
                act.wait_ge(d_dve, b.times(6).plus(2 + 3).v)
                act.activation(PBx[:, :, :], PBx[:, :, :], ACT.Exp).then_inc(d_act, 1)

            def head(h, odd):
                n = h.times(NP)
                first = not (h.c or h.L)
                rows = slice(HD * odd, HD * (odd + 1))
                if not first:
                    sequence(h.plus(-1))
                act.wait_ge(a_turned, h.times(2).plus(2).v)
                act.activation(qT[:, :].rearrange("p (a n) -> p a n", a=2), ps[0:HD + 2, 4:6, :], ACT.Copy).then_inc(a_q, 1)
                act.wait_ge(a_again, h.plus(1).v)
                act.activation(qT[HD:HD + 2, :].rearrange("p (a n) -> p a n", a=2), ps[HD:HD + 2, 0:2, :], ACT.Copy
                               ).then_inc(a_q2, 1)
                if not first:
                    act.wait_ge(a_av, h.v)
                    act.wait_ge(a_sum, h.v)
                for p, (j, c, lo, w) in enumerate(key_pieces):
                    act.wait_ge(a_st, n.plus(p + 1).v)
                    o = key_at[j] + lo - j * P
                    act.activation(PT[:, o:o + w], ps[:, 4 + p % 2, 0:w], ACT.Exp).then_inc(a_p, 1)
                act.wait_ge(a_den, h.plus(1).v)
                if not odd and not first:
                    act.wait_ge(a_pair, h.half.v)
                act.activation(rden[rows, :].rearrange("p (a n) -> p a n", a=2), ps[rows, 0:2, :], ACT.Ln).then_inc(a_lnd, 1)

            def pair(p):
                for e in range(2):
                    head(p.times(2).plus(e), e)
                act.wait_ge(a_lnd, p.times(2).plus(2).v)
                act.activation(rden[:, :], rden[:, :], ACT.Exp, scale=-1.0).then_inc(a_rden, 1)
            loop(act, NH // 2, 1, pair, peel=1)
            sequence(V(NS - 1))
            act.wait_ge(a_pair, NH // 2)
            act.wait_ge(d_dve, 2 + 6 * NS)
            for k in range(4):
                act.activation(hh[:, k, :], ya[:, k, :], ACT.Copy).then_inc(y_hi, 1)
            act.activation(hh[:, 4:8, 0:NS], ysam[:, :, :], ACT.Copy).then_inc(y_hi, 1)
            for c in range(4):
                act.activation(hh[:, 4 + c, NS:T].rearrange("p (b n) -> p b n", n=P), QK[:, 0, :, c * P:(c + 1) * P],
                               ACT.Copy).then_inc(y_hi, 1)
            norm(1, T_OUT[0])
            mlp(0)

            norm(2, T_MLP[0] + 152)
            residual_out(1)

            def query_or_key(i, k):
                t = i.plus(T_IN[1] + 4 * k)
                act.wait_ge(acc_done, done(t, 3))
                if not k and not i.c and not i.L:
                    act.wait_ge(x_spilled, 32)
                act.activation(qk1[:, ds(i.times(2).plus(k).v, 1), :].rearrange("p o (c n) -> p (o c) n", c=3),
                               acc(t.par), ACT.Copy).then_inc(acc_free[t.par], 1)
            for k in range(2):
                loop(act, 4, 2, lambda i: query_or_key(i, k), peel=2 if k == 0 else 0)
            loop(act, 8, 2, lambda i: token_tile(i.plus(13), i.plus(T_IN[1] + 8), 3,
                                                 vs_f[:, ds(i.v, 1), :].rearrange("p a n -> p (a n)")))
            t = V(T_IN[1] + 16)
            act.wait_ge(acc_done, done(t, 3))
            act.wait_ge(nat_done, 21)
            act.activation(thirds(tmp[:, 1, :]), acc(t.par), ACT.Copy).then_inc(acc_free[t.par], 1)

            def gla_head(h):
                g = h.times(6)
                act.wait_ge(g_dve, g.plus(2).v)
                link(act.activation(tmp[:, 0, :], tmp[:, 0, :], ACT.Exp))
                act.activation(tmp[:, 0, :], tmp[:, 0, :], ACT.Ln, bias=1.0).then_inc(g_act, 1)
                act.wait_ge(g_dve, g.plus(3).v)
                act.activation(dec[:, :], bcum[:, NS:T].rearrange("p (c r) -> p c r", r=CHUNK)[:, :, CHUNK - 1], ACT.Exp,
                               scale=1.0 / TAU)
                act.activation(tmp[:, 0, NS:T], bcum[:, NS:T], ACT.Exp, scale=1.0 / TAU).then_inc(g_act, 1)
                act.wait_ge(g_dve, g.plus(4).v)
                act.activation(tmp[:, 0, NS:T], bcum[:, NS:T], ACT.Exp, scale=-1.0 / TAU).then_inc(g_act, 1)
                act.wait_ge(g_dve, g.plus(5).v)
                act.activation(tmp[:, 0, NS:T], tmp[:, 0, NS:T], ACT.Exp, scale=1.0 / TAU).then_inc(g_act, 1)
                first = not (h.c or h.L)

                def keys(b):
                    m = h.times(NB).plus(b)
                    act.wait_ge(gb_a, m.times(2).plus(2).v)
                    if b >= 2 or not first:
                        act.wait_ge(gb_kv, m.times(2).plus(-2).v)
                    act.activation(kdn[0:CHUNK, b % 2, 0, :], ps[0:CHUNK, 1, 0:P], ACT.Copy)
                    act.activation(kdn[CHUNK:P, b % 2, 1, :], ps[CHUNK:P, 1, 0:P], ACT.Copy).then_inc(gb_kd, 1)

                def kept(b):
                    act.wait_ge(g_tr, h.times(NB).plus(b + 1).v)
                    act.activation(qk1[:, ds(h.times(2).v, 2), NS + b * P:NS + (b + 1) * P],
                                   ps[:, 6, 0:2 * P].rearrange("p (e n) -> p e n", e=2), ACT.Copy).then_inc(g_trk, 1)

                keys(0)
                for b in range(NB):
                    m = h.times(NB).plus(b)
                    if b + 1 < NB:
                        keys(b + 1)
                    if b:
                        kept(b - 1)
                    act.wait_ge(gb_inter, m.times(2).plus(2).v)
                    if b >= 2 or not first:
                        act.wait_ge(gb_out, m.plus(-1).v)
                    link(act.activation(tmp[:, 0, 2 * DV:3 * DV], ps[:, 2 + b % 2, 0:DV], ACT.Square,
                                        accum_out=ss1[:, b % 2, 0:1]))
                    rsqrt(ss1[:, b % 2, 1:2], ss1[:, b % 2, 0:1], DV, gb_rs)
                kept(NB - 1)
                act.wait_ge(gb_state, h.times(2 * NB + 1).plus(2 * NB + 1).v)
                act.dma_start(gla_prompt[0, 0, ds(h.v, 1)].rearrange("o k v -> (o k) v"), S[:, :]).then_inc(g_stored, 16)
            loop(act, NG, 1, gla_head, link, 1 + 2 * NB, peel=1)

            def gate(f):
                t = f.plus(T_IN[1] + 17)
                act.wait_ge(acc_done, done(t, 3))
                if f.c >= 2 or f.L:
                    act.wait_ge(r_done, f.plus(-1).v)
                r = tmp[:, f.c % 2, :]
                link(act.activation(thirds(r), acc(t.par), ACT.Exp, scale=-1.0))
                link(act.activation(r, r, ACT.Ln, bias=1.0))
                act.activation(r, r, ACT.Exp, scale=-1.0).then_inc(r_exp, 1)
            act.wait_ge(g_stored, 16 * NG)
            loop(act, KT, 2, gate, link, 2, peel=2)
            act.activation(dec_s[:, :, :], dec_s[:, :, :], ACT.Exp, scale=1.0 / TAU).then_inc(s_act, 1)
            act.wait_ge(s_ss, 1)
            rsqrt(ss8[:, :], ss8[:, :], DV, s_act)
            act.wait_ge(y_s, 1)
            act.wait_ge(r_done, KT)
            act.wait_ge(gla_stored, 16 * NG)
            for k in range(KT):
                act.activation(hh[:, k, :], qk1[:, k, :], ACT.Copy).then_inc(y_hi, 1)
            norm(3, T_OUT[1])
            mlp(1)
            act.wait_ge(g_stored, 16 * NG)

        @block.vector
        def _(dve):
            link = Link(dve, dve_link)
            tt, stt = dve.tensor_tensor, dve.scalar_tensor_tensor

            def add_square(n, k):
                dve.wait_ge(sq_ready, KT * n + k + 1)
                tt(sqsum[:, :], sqsum[:, :], tmp[:, k % 2, :], ALU.add).then_inc(sq_added, 1)
                dve.wait_ge(sq_added, (KT - 1) * n + k)

            def norm(n):
                l, w = n // 2, n % 2
                for k in range(1 if n == 0 else KT - 1, KT):
                    add_square(n, k)
                dve.wait_ge(rstd_ready, n + 1)

                def low(k):
                    dve.wait_ge(norm_hi, KT * n + k + 1)
                    tt(hl[:, k, :], tmp[:, k % 2, :], hh[:, k, :].bitcast(F32), ALU.subtract).then_inc(h_ready, 1)
                for k in range(KT):
                    if k >= 2:
                        dve.wait_ge(h_ready, KT * n + k - 1)
                    tt(tmp[:, k % 2, :], xT[:, k, :], rstd[:, :], ALU.mult).then_inc(norm_scaled, 1)
                    dve.wait_ge(norm_scaled, KT * n + k + 1)
                    link(tt(tmp[:, k % 2, 0:NS], tmp[:, k % 2, 0:NS], gain[:, n, k, 0:NS], ALU.mult))
                    tt(tmp[:, k % 2, 0:NS], tmp[:, k % 2, 0:NS], modT[:, l, 24 * w + k, 0:NS], ALU.add
                       ).then_inc(norm_affine, 1)
                    if k:
                        low(k - 1)
                low(KT - 1)

            def token_tile(i, dst):
                dve.wait_ge(nat_done, i.plus(1).v)
                dve.tensor_copy(dst, ps[:, 6:8, :].rearrange("p a (b n) -> p (a b) n", n=P)).then_inc(nat_kept, 1)

            def residual(t, nn, f, l, comp):
                dve.wait_ge(acc_done, done(t, nn))
                m = KT * comp + f
                s = 3 * t.par
                link(tt(t8[:, :], ps[:, s, 0:NS], modT[:, l, m, 0:NS], ALU.mult))
                tt(xT[:, f, 0:NS], xT[:, f, 0:NS], t8[:, :], ALU.add)
                stt(out=xT[:, f, NS:CH], in0=ps[:, s, NS:CH], scalar=modT[:, l, m, NS:NC], in1=xT[:, f, NS:CH],
                    op0=ALU.mult, op1=ALU.add)
                x2 = xT[:, f, CH:T].rearrange("p (c n) -> p c n", c=2)
                stt(out=x2, in0=ps[:, s + 1:s + 3, 0:CH], scalar=modT[:, l, m, NS:NC], in1=x2,
                    op0=ALU.mult, op1=ALU.add).then_inc(acc_free[t.par], 1)
                dve.wait_ge(acc_free[t.par], t.half.plus(1).v)

            def out_proj(l):
                dve.wait_ge(x_back, 16 * (l + 1))
                for f in range(KT):
                    residual(V(T_OUT[l] + f), 2 * l + 1, f, l, 2)
                    if f >= 2:
                        add_square(2 * l + 1, f - 1)

            def mlp(l):
                t0, nn = T_MLP[l], 2 * l + 2

                def up(i, t):
                    for j in range(2):
                        q = i.times(2).plus(2 * NPAIR * l + j)
                        tj = t.plus(j)
                        dve.wait_ge(acc_free[tj.par], tj.half.plus(1).v)
                        tt(tmp[:, j, :], tmp[:, j, :], tmp[:, j, :], ALU.mult).then_inc(hid_squared, 1)
                        dve.wait_ge(hid_hi_ready, q.plus(1).v)
                        tt(hid[1][:, i.c % 2, j, :], tmp[:, j, :], hid[0][:, i.c % 2, j, :].bitcast(F32), ALU.subtract
                           ).then_inc(hid_ready, 1)

                def down(i, t, last=False):
                    for f in range(KT):
                        residual(t.plus(f), nn, f, l, 5)
                        if last and f >= 2:
                            add_square(2, f - 1)

                def step(i):
                    up(i.plus(1), i.times(10).plus(t0 + 2))
                    down(i, i.times(10).plus(t0 + 4))
                up(V(0), V(t0))
                loop(dve, NPAIR - 1, 2, step, link, KT, peel=1)
                down(V(NPAIR - 1), V(t0 + 152), last=l < DEPTH - 1)

            dve.wait_ge(consts_made, 1)
            dve.wait_ge(setup_pe, 1)
            dve.tensor_copy(vecT[:, :], ps[:, 0, 0:144])
            dve.tensor_copy(prevT[:, :, :], ps[:, 0, 256:320].rearrange("p (c n) -> p c n", c=4))
            dve.tensor_copy(xT[:, :, 0:NS], ps[:, 1, 0:NS * KT].rearrange("p (k n) -> p k n", k=KT)).then_inc(setup_dve, 1)
            link(dve.tensor_scalar(gqb[:, :], gqb[:, :], HD ** -0.5, None, ALU.mult))
            dve.wait_ge(silu_pos, 1)
            link(dve.tensor_scalar(c9e[:, :], c9e[:, :], 1.0, None, ALU.add))
            link(dve.reciprocal(c9e[:, :], c9e[:, :]))
            tt(c9[:, :], c9[:, :], c9e[:, :], ALU.mult).then_inc(setup_dve, 1)
            dve.wait_ge(setup_pe, 2)
            dve.tensor_copy(scT[:, :, :], ps[:, 1, P:P + NC * KT].rearrange("p (k n) -> p k n", k=KT)).then_inc(setup_dve, 1)
            modA = modT[:, :, :, :].rearrange("p l n c -> p (l n) c")

            def modulation(i):
                dve.wait_ge(mod_turned, i.plus(1).v)
                n = i.times(4).v
                tt(modA[:, ds(n, 4), :], ps[:, 4 + i.c % 2, 0:4 * NC].rearrange("p (f c) -> p f c", f=4),
                   vecT[:, ds(n, 4)].unsqueeze(2).to_broadcast([P, 4, NC]), ALU.add).then_inc(ada_kept, 1)
            loop(dve, 24, 2, modulation)
            dve.wait_ge(ada_kept, 24)
            for n in range(4):
                l, w = n // 2, n % 2
                last = stt(out=gain[:, n, :, :], in0=modT[:, l, 24 * w + 8:24 * w + 16, :], scalar=1.0,
                           in1=vecT[:, 96 + 16 * w + 8 * l:104 + 16 * w + 8 * l].unsqueeze(2).to_broadcast([P, KT, NC]),
                           op0=ALU.add, op1=ALU.mult)
            last.then_inc(setup_dve, 1)
            dve.wait_ge(setup_dve, 4)
            norm(0)

            dve.wait_ge(x_spilled, 16)
            for j in range(2):
                loop(dve, 4, 2, lambda i: token_tile(i.plus(4 * j), QK[:, j, :, ds(i.times(P).v, P)]))
            loop(dve, 4, 2, lambda i: token_tile(i.plus(8), Vn[:, :, ds(i.times(P).v, P)]))

            def conv(c):
                t = c.times(3).plus(T_IN[0] + 12)
                m = c.c % 2
                dve.wait_ge(acc_free[t.par], t.half.plus(1).v)
                t = t.plus(1)
                dve.wait_ge(acc_done, done(t, 1))
                s = 3 * t.par
                tt(U[:, 0:NS], ps[:, s, 0:NS], tmp[:, m, 0:NS], ALU.mult)
                tt(U[:, NS + 2:CH + 2], ps[:, s, NS:CH], tmp[:, m, NS:CH], ALU.mult)
                tt(U[:, CH + 2:T + 2].rearrange("p (c n) -> p c n", c=2), ps[:, s + 1:s + 3, 0:CH],
                   tmp[:, m, CH:T].rearrange("p (c n) -> p c n", c=2), ALU.mult).then_inc(acc_free[t.par], 1)
                dve.wait_ge(acc_free[t.par], t.half.plus(1).v)
                w = [vecT[:, ds(c.plus(P + 4 * j).v, 1)] for j in range(3)]
                y = ya[:, ds(c.v, 1), :].rearrange("p o n -> p (o n)")
                link(dve.tensor_scalar(y[:, NS:T], U[:, NS + 2:T + 2], w[2], None, ALU.mult))
                link(stt(out=y[:, NS:T], in0=U[:, NS + 1:T + 1], scalar=w[1], in1=y[:, NS:T], op0=ALU.mult, op1=ALU.add))
                link(stt(out=y[:, NS:T], in0=U[:, NS:T], scalar=w[0], in1=y[:, NS:T], op0=ALU.mult, op1=ALU.add))
                prev = prevT[:, ds(c.v, 1), :].rearrange("p o (b j) -> p (o b) j", j=2)
                link(dve.tensor_scalar(y[:, 0:NS], U[:, 0:NS], w[2], None, ALU.mult))
                for j in (1, 0):
                    link(stt(out=y[:, 0:NS], in0=prev[:, :, j], scalar=w[j], in1=y[:, 0:NS], op0=ALU.mult, op1=ALU.add))
                dve.tensor_copy(uOut[:, ds(c.v, 1), 0:NS].rearrange("p o n -> p (o n)"), U[:, 0:NS])
                dve.tensor_copy(uOut[:, ds(c.v, 1), NS:10].rearrange("p o n -> p (o n)"), U[:, T:T + 2])
                t = t.plus(1)
                dve.wait_ge(acc_done, done(t, 1))
                tt(thirds(y), thirds(y), acc(t.par), ALU.mult).then_inc(acc_free[t.par], 1)
                dve.wait_ge(acc_free[t.par], t.half.plus(1).v)
            dve.wait_ge(setup_pe, 2)
            link(dve.memset(U[:, NS:NS + 2], 0.0))
            loop(dve, 4, 2, conv, link, 6)

            link(dve.memset(lf[:, :, :], 0.0))
            link(dve.memset(rsq[:, :], 1.0))
            dve.wait_ge(nat_done, 13)
            tt(lf[:, 0:NB, :], ps[:, 6:8, :].rearrange("p a (b n) -> p (a b) n", n=P)[:, :, P - NH:P],
               bfb[:, :].unsqueeze(1).to_broadcast([P, NB, NH]), ALU.add).then_inc(nat_kept, 1)
            dve.wait_ge(prep_pe, 1)
            dve.tensor_copy(sNat[:, :, :], ps[0:NS, 0:3, :]).then_inc(prep_dve, 1)
            tt(lf[0:NS, NB, :], ps[0:NS, 3, P - NH:P], bfb[0:NS, :], ALU.add)
            dve.tensor_copy(crow[:, :], ps[0:10, 4, :]).then_inc(prep_dve, 1)
            dve.wait_ge(prep_dve, 2)
            stt(out=lft[:, :, :], in0=lf[:, :, :], scalar=-1.0, in1=lf[:, :, :], op0=ALU.mult, op1=ALU.min
                ).then_inc(prep_dve, 1)
            dve.wait_ge(prep_act, 1)
            groups = "p j b (h d) -> p (j b h) d"
            dve.tensor_reduce(rsq[:, 0:2 * NB * NH], sqs[:, :, :, :].rearrange(groups, d=HD), X, ALU.add)
            dve.wait_ge(prep_act, 2)
            dve.tensor_reduce(rsq[0:NS, 2 * NB * NH:], sq8[:, :, :].rearrange("p j (h d) -> p (j h) d", d=HD), X, ALU.add
                              ).then_inc(prep_dve, 1)
            dve.wait_ge(prep_act, 3)
            stt(out=lf[:, :, :], in0=lf[:, :, :], scalar=0.0, in1=lft[:, :, :], op0=ALU.min, op1=ALU.subtract
                ).then_inc(prep_dve, 1)
            dve.wait_ge(prep_act, 4)
            rs = rsq[:, 0:2 * NB * NH].rearrange("p (j g) -> p j g", j=2)
            rs8 = rsq[0:NS, 2 * NB * NH:].rearrange("p (j g) -> p j g", j=2)
            for j, g in ((0, gqb), (1, gkb)):
                q = QK[:, j].rearrange("p b (h d) -> p (b h) d", d=HD)
                s = sNat[:, j, :].rearrange("p (h d) -> p h d", d=HD)
                link(tt(q, q, rs[:, j, :].unsqueeze(2).to_broadcast([P, NB * NH, HD]), ALU.mult))
                link(tt(q, q, g[:, :].unsqueeze(1).to_broadcast([P, NB * NH, HD]), ALU.mult))
                link(tt(s, s, rs8[:, j, :].unsqueeze(2).to_broadcast([NS, NH, HD]), ALU.mult))
                link(tt(s, s, g[0:NS, :].unsqueeze(1).to_broadcast([NS, NH, HD]), ALU.mult))
            tt(sq8[:, 0, :], sNat[:, 0, :], sNat[:, 1, :], ALU.mult).then_inc(prep_dve, 1)
            dve.wait_ge(prep_dve, 6)
            dve.tensor_reduce(snew[:, :], sq8[:, 0, :].rearrange("p (h d) -> p h d", d=HD), X, ALU.add)
            dve.wait_ge(prep_pe, 2)
            link(dve.tensor_copy(fcum[:, :, :], ps[:, 5, 0:NB * NH].rearrange("p (b h) -> p b h", h=NH)))
            dve.memset(QA[:, :, HD + 1:HD + 2], 1.0)
            dve.memset(KA[:, :, HD:HD + 1], 1.0)

            dve.wait_ge(d_pe, 1)
            dve.tensor_copy(LT[:, :, :], ps[:, 2:4, :].rearrange("p a (h n) -> p (a h) n", n=P))
            link(dve.tensor_reduce(ptot[:, :], Lraw[:, :, :].rearrange("p s h -> p h s"), X, ALU.add))
            tt(TB[:, :, :], ptot[:, :].unsqueeze(2).to_broadcast([P, NH, P]),
               ones[:, :].unsqueeze(1).to_broadcast([P, NH, P]), ALU.mult)
            tt(LN[:, :, :], lf[0:NS, NB, :].unsqueeze(2).to_broadcast([NS, NH, P]),
               ones[0:NS, :].unsqueeze(1).to_broadcast([NS, NH, P]), ALU.mult).then_inc(d_dve, 1)
            dve.wait_ge(d_pe, 2)
            link(dve.memset(sc[:, PAGES, :], NEG))
            link(dve.memset(peaks[:, :, :], NEG))
            dve.tensor_copy(Lsuf[:, :, :], ps[:, 6:8, :].rearrange("p a (h n) -> p (a h) n", n=P)).then_inc(d_dve, 1)

            dve.wait_ge(kv_out, 16 * 9)

            def sequence_scores(b):
                dve.wait_ge(qbc_in, b.times(16).plus(16).v)
                for j in range(8):
                    dve.wait_ge(pages_in[j], b.times(64).plus(32).v)
                    kk = pages[:, j, :, :]
                    link(tt(kk, kk, qbc[:, :].unsqueeze(1).to_broadcast([P, 2, 512]), ALU.mult))
                    dve.tensor_reduce(sc[:, 2 * j:2 * j + 2, :], kk.rearrange("p g (h d) -> p g h d", d=HD), X, ALU.add
                                      ).then_inc(k_used, 1)
                dve.wait_ge(k_used, b.times(8).plus(8).v)
                s16 = sc[:, 0:PAGES, :]
                tt(s16, s16, Lsuf[:, :, ds(b.times(PAGES).v, PAGES)].rearrange("p h g -> p g h"), ALU.add)
                link(dve.tensor_scalar(sc[0:NS, PAGES, :], snew[:, :], only8[:, ds(b.v, 1)], None, ALU.add))
                dve.tensor_reduce(mx8[:, :], sc[:, :, :].rearrange("p g h -> p h g"), X, ALU.max).then_inc(d_dve, 1)
                dve.wait_ge(d_pe, b.times(4).plus(2 + 1).v)
                link(dve.tensor_reduce(small[0:8, 0:1], ps[0:8, 7, 0:P], X, ALU.max))
                dve.tensor_scalar(small[0:8, 8:16], ident[0:8, 0:8], small[0:8, 0:1], None, ALU.mult).then_inc(d_dve, 1)
                dve.wait_ge(d_pe, b.times(4).plus(2 + 2).v)
                tt(PBx[:, :, :], sc[:, :, :], ps[:, 7, 128:136].unsqueeze(1).to_broadcast([P, PAGES + 1, NH]), ALU.subtract
                   ).then_inc(d_dve, 1)
                dve.wait_ge(d_dve, b.times(6).plus(2 + 3).v)

            def sequence_sums(b):
                dve.wait_ge(d_act, b.plus(1).v)
                dve.tensor_reduce(small[:, 16:24], PBx[:, :, :].rearrange("p g h -> p h g"), X, ALU.add).then_inc(d_dve, 1)
                dve.wait_ge(d_dve, b.times(6).plus(2 + 4).v)

            def sequence_scaled(b):
                dve.wait_ge(d_pe, b.times(4).plus(2 + 3).v)
                link(dve.reciprocal(small[0:8, 1:2], ps[0:8, 7, 144:145]))
                stt(out=omask, in0=ps[0:8, 6, :], scalar=small[0:8, 1:2],
                    in1=headrow[:, :, :].rearrange("p h d -> p (h d)"), op0=ALU.mult, op1=ALU.mult).then_inc(d_dve, 1)

            def sequence_out(b):
                dve.wait_ge(d_pe, b.times(4).plus(2 + 4).v)
                dve.tensor_copy(ysam[:, :, ds(b.v, 1)].rearrange("p c o -> p (c o)"), ps[:, 7, 152:156]).then_inc(d_dve, 1)
                dve.wait_ge(d_dve, b.times(6).plus(2 + 6).v)

            def head(h):
                n = h.times(NP)
                first = not (h.c or h.L)
                if not first:
                    dve.wait_ge(a_again, h.v)
                dve.tensor_copy(KA[:, :, 0:HD], QK[:, 1, :, ds(h.times(HD).v, HD)])
                dve.tensor_scalar(KA[:, :, HD + 1:HD + 2], fcum[:, :, ds(h.v, 1)], -1.0, None, ALU.mult)
                dve.tensor_copy(QA[:, :, 0:HD], QK[:, 0, :, ds(h.times(HD).v, HD)])
                dve.tensor_copy(QA[:, :, HD:HD + 1], fcum[:, :, ds(h.v, 1)]).then_inc(a_built, 1)
                dve.wait_ge(a_turned, h.times(2).plus(1).v)
                dve.tensor_copy(kT[:, :].rearrange("p (a n) -> p a n", a=2), ps[0:HD + 2, 0:2, :]).then_inc(a_k, 1)
                for p, (i, c, lo, w) in enumerate(query_pieces):
                    dve.wait_ge(a_s, n.plus(p + 1).v)
                    dve.tensor_reduce(peaks[:, i, c:c + 1], ps[:, 4 + p % 2, 0:w], X, ALU.max).then_inc(a_max, 1)
                    if p == 1 and not first:
                        sequence_sums(h.plus(-1))
                dve.wait_ge(a_max, n.plus(NP).v)
                link(dve.tensor_reduce(peak[:, :], peaks[:, :, :], X, ALU.max))
                tt(QA[:, :, HD], fcum[:, :, ds(h.v, 1)].rearrange("p b o -> p (b o)"), peak[:, :], ALU.subtract
                   ).then_inc(a_shift, 1)
                if not first:
                    sequence_scaled(h.plus(-1))
                    sequence_out(h.plus(-1))
                sequence_scores(h)

            def pair(p):
                for e in range(2):
                    head(p.times(2).plus(e))
                dve.wait_ge(a_rden, p.plus(1).v)
                dve.wait_ge(a_built, p.times(2).plus(2).v)
                tt(QK[:, 0, :, ds(p.times(P).v, P)], ps[:, 2:4, :].rearrange("p a (b n) -> p (a b) n", n=P),
                   rden[:, :].rearrange("p (b n) -> p b n", n=P), ALU.mult).then_inc(a_pair, 1)
            loop(dve, NH // 2, 1, pair, link, 24, peel=1)
            sequence_sums(V(NS - 1))
            sequence_scaled(V(NS - 1))
            sequence_out(V(NS - 1))
            for k in range(4):
                dve.wait_ge(y_hi, k + 1)
                tt(hl[:, k, :], ya[:, k, :], hh[:, k, :].bitcast(F32), ALU.subtract).then_inc(y_ready, 1)
            dve.wait_ge(y_hi, 5)
            tt(hl[:, 4:8, 0:NS], ysam[:, :, :], hh[:, 4:8, 0:NS].bitcast(F32), ALU.subtract)
            for c in range(4):
                dve.wait_ge(y_hi, 6 + c)
                cols = "p (b n) -> p b n"
                tt(hl[:, 4 + c, NS:T].rearrange(cols, n=P), QK[:, 0, :, c * P:(c + 1) * P],
                   hh[:, 4 + c, NS:T].rearrange(cols, n=P).bitcast(F32), ALU.subtract).then_inc(y_ready, 1)
            out_proj(0)
            norm(1)
            mlp(0)

            dve.memset(kdn[:, :, :, :], 0.0)
            dve.memset(wgk[:, :], 0.0).then_inc(gate_cleared, 1)
            link(dve.memset(scanm[:, :], 1.0))
            link(dve.memset(scanm[:, :].rearrange("p (c r) -> p c r", r=CHUNK)[:, :, 0:1], 0.0))
            norm(2)
            loop(dve, 8, 2, lambda i: token_tile(i.plus(13), Vo[:, :, ds(i.times(P).v, P)]))

            def gla_head(h):
                g = h.times(6)
                hc = h.v
                z = ke
                if h.c or h.L:
                    dve.wait_ge(g_stored, h.times(16).v)
                    dve.wait_ge(g_tr, h.times(NB).v)
                dve.tensor_copy(wgh[:, :], wgk[:, ds(h.times(DK).v, DK)]).then_inc(g_dve, 1)
                dve.wait_ge(g_pe, h.plus(1).v)
                link(dve.tensor_scalar(thirds(z[:, :]), ps[:, 0:3, 0:CH], vecT[:, ds(h.plus(140).v, 1)], None, ALU.add))
                stt(out=tmp[:, 0, :], in0=z[:, :], scalar=-1.0, in1=z[:, :], op0=ALU.mult, op1=ALU.min).then_inc(g_dve, 1)
                dve.wait_ge(g_act, h.times(4).plus(1).v)
                link(stt(out=z[:, :], in0=z[:, :], scalar=0.0, in1=tmp[:, 0, :], op0=ALU.min, op1=ALU.subtract))
                dve.tensor_copy(dec_s[:, ds(hc, 1), :].rearrange("p o n -> p (o n)"), z[:, 0:NS])
                dve.tensor_tensor_scan(bcum[:, NS:T], scanm[:, :], z[:, NS:T], 0.0, ALU.mult, ALU.add).then_inc(g_dve, 1)
                qh = qk1[:, ds(h.times(2).v, 1), :].rearrange("p o n -> p (o n)")
                kh = qk1[:, ds(h.times(2).plus(1).v, 1), :].rearrange("p o n -> p (o n)")
                dve.wait_ge(g_act, h.times(4).plus(2).v)
                stt(out=qe[:, NS:T], in0=qh[:, NS:T], scalar=DK ** -0.5, in1=tmp[:, 0, NS:T], op0=ALU.mult, op1=ALU.mult
                    ).then_inc(g_dve, 1)
                dve.wait_ge(g_act, h.times(4).plus(3).v)
                link(tt(ke[:, NS:T], kh[:, NS:T], tmp[:, 0, NS:T], ALU.mult))
                bc = bcum[:, NS:T].rearrange("p (c r) -> p c r", r=CHUNK)
                tt(tmp[:, 0, NS:T].rearrange("p (c r) -> p c r", r=CHUNK),
                   bc[:, :, CHUNK - 1:CHUNK].to_broadcast([P, SEQ // CHUNK, CHUNK]), bc, ALU.subtract).then_inc(g_dve, 1)
                dve.tensor_copy(qks[:, ds(hc, 1), :].rearrange("p o n -> p (o n)"), qh[:, 0:NS])
                dve.tensor_copy(qks[:, ds(h.plus(4).v, 1), :].rearrange("p o n -> p (o n)"), kh[:, 0:NS])
                dve.wait_ge(g_act, h.times(4).plus(4).v)
                tt(bcum[:, NS:T], kh[:, NS:T], tmp[:, 0, NS:T], ALU.mult).then_inc(g_dve, 1)
                dve.wait_ge(g_dve, g.plus(6).v)
                dve.memset(S[:, :], 0.0).then_inc(gb_state, 1)
                def masked(b):
                    m = h.times(NB).plus(b)
                    dve.wait_ge(gb_a, m.times(2).plus(1).v)
                    if b >= 2:
                        dve.wait_ge(gb_kv, m.times(2).plus(-2).v)
                    tt(aT[:, b % 2, :], ps[:, 0, 0:P], pairmask[:, :], ALU.mult).then_inc(gb_scores, 1)

                def scaled(b):
                    m = h.times(NB).plus(b)
                    dve.wait_ge(gb_rs, m.plus(1).v)
                    if b >= 2:
                        dve.wait_ge(g_tr, m.plus(-1).v)
                    stt(out=tmp[:, 0, DV * (b % 2):DV * (b % 2 + 1)], in0=ps[:, 2 + b % 2, 0:DV],
                        scalar=ss1[:, b % 2, 1:2], in1=gob[:, :], op0=ALU.mult, op1=ALU.mult).then_inc(gb_out, 1)

                masked(0)
                for b in range(NB):
                    m = h.times(NB).plus(b)
                    if b + 1 < NB:
                        masked(b + 1)
                    if b:
                        scaled(b - 1)
                    for c in range(2):
                        dve.wait_ge(gb_kv, m.times(2).plus(c + 1).v)
                        dve.wait_ge(gb_inter, m.times(2).plus(c + 1).v)
                        dve.wait_ge(gb_state, h.times(2 * NB + 1).plus(2 * b + c + 1).v)
                        stt(out=S[:, :], in0=S[:, :], scalar=dec[:, 2 * b + c:2 * b + c + 1], in1=ps[:, 4 + c, 0:DV],
                            op0=ALU.mult, op1=ALU.add).then_inc(gb_state, 1)
                scaled(NB - 1)
            dve.wait_ge(gate_loaded, 32)
            loop(dve, NG, 1, gla_head, link, 3, peel=1)

            def gate(f):
                t = f.plus(T_IN[1] + 17)
                r = tmp[:, f.c % 2, :]
                dve.wait_ge(r_exp, f.plus(1).v)
                tt(thirds(r), thirds(r), acc(t.par), ALU.mult).then_inc(acc_free[t.par], 1)
                dve.wait_ge(acc_free[t.par], t.half.plus(1).v)
                dve.tensor_copy(rs_f[:, ds(f.v, 1), :].rearrange("p o n -> p (o n)"), r[:, 0:NS])
                o = qk1[:, ds(f.v, 1), NS:T].rearrange("p o n -> p (o n)")
                tt(o, o, r[:, NS:T], ALU.mult).then_inc(r_done, 1)
            dve.wait_ge(g_trk, NG * NB)
            loop(dve, KT, 2, gate)

            dve.wait_ge(s_pe, 1)
            dve.tensor_copy(kvnat[:, :], ps[0:NS, 0:3, :].rearrange("p a n -> p (a n)")).then_inc(s_dve, 1)
            dve.wait_ge(s_dve, 1)
            dve.wait_ge(s_act, 1)
            for h in range(NG):
                base = 1 + 10 * h
                tt(kmask[:, :, :], kvnat[:, h * DK:(h + 1) * DK].unsqueeze(1).to_broadcast([NS, NS, DK]),
                   ident[0:NS, 0:NS].unsqueeze(2).to_broadcast([NS, NS, DK]), ALU.mult)
                stt(out=qmask[:, :, :], in0=qks[:, h, :].unsqueeze(1).to_broadcast([P, NS, NS]), scalar=DK ** -0.5,
                    in1=eye8[:, :, :], op0=ALU.mult, op1=ALU.mult).then_inc(s_dve, 1)
                dve.wait_ge(s_in, 16 * (h + 1))
                if h:
                    dve.wait_ge(gla_stored, 16 * h)
                for b in range(NS):
                    dve.wait_ge(s_pe, 1 + 8 * h + b + 1)
                    stt(out=sout[:, b, :], in0=sst[:, b, :], scalar=dec_s[:, h, b:b + 1], in1=ps[:, 3 + b % 2, 0:DV],
                        op0=ALU.mult, op1=ALU.add).then_inc(s_dve, 1)
                dve.wait_ge(s_out, 8 * (h + 1))
                dve.tensor_copy(osn[:, h * DV:(h + 1) * DV], ps[0:NS, 5, 0:DV]).then_inc(s_dve, 1)
            dve.wait_ge(s_dve, 41)
            sq = kmask[:, :, :].rearrange("p a n -> p (a n)")
            link(tt(sq, osn[:, :], osn[:, :], ALU.mult))
            dve.tensor_reduce(ss8[:, :], sq.rearrange("p (h v) -> p h v", v=DV), X, ALU.add).then_inc(s_ss, 1)
            dve.wait_ge(s_act, 2)
            o3 = osn[:, :].rearrange("p (h v) -> p h v", v=DV)
            link(tt(o3, o3, ss8[:, :].unsqueeze(2).to_broadcast([NS, NG, DV]), ALU.mult))
            tt(o3, o3, gob[0:NS, :].unsqueeze(1).to_broadcast([NS, NG, DV]), ALU.mult).then_inc(s_dve, 1)
            dve.wait_ge(s_pe, 34)
            tt(qk1[:, :, 0:NS], ps[:, 6, 0:NS * KT].rearrange("p (k n) -> p k n", k=KT), rs_f[:, :, :], ALU.mult
               ).then_inc(y_s, 1)
            for k in range(KT):
                dve.wait_ge(y_hi, KT + 1 + k + 1)
                tt(hl[:, k, :], qk1[:, k, :], hh[:, k, :].bitcast(F32), ALU.subtract).then_inc(y_ready, 1)
            out_proj(1)
            norm(3)
            mlp(1)
            for b in range(NB + 1):
                dve.wait_ge(y_turned, b + 1)
                n = P if b < NB else NS
                dst = ynat[:, b, :] if b < NB else ysn[:, :]
                dve.tensor_copy(dst.rearrange("p (a n) -> p a n", a=2), ps[0:n, 2 * (b % 2):2 * (b % 2) + 2, :]
                                ).then_inc(y_kept, 1)


_INS = ["x_prompt", "x_sample", "c_prompt", "c_sample", "cache_k", "cache_v", "cache_logf", "page_table", "state_conv",
        "state_gla", "g_mix", "g_ffn", "w_ada", "b_ada", "w_in_even", "b_f", "g_q", "g_k", "w_conv", "w_out_even",
        "w_in_odd", "w_gk", "b_gk", "g_o", "w_out_odd", "w_ff1", "w_ff2"]
_OUTS = [(1, 1024, 1024), (8, 1, 1024), (1, 1, 1024, 8, 64), (1, 1, 1024, 8, 64), (1, 1, 1024, 8),
         (8, 1, 1, 8, 64), (8, 1, 1, 8, 64), (8, 1, 1, 8), (1, 1, 2, 512), (8, 1, 2, 512),
         (1, 1, 4, 128, 256), (8, 1, 4, 128, 256)]


def kernel(**inputs):
    import numpy as _np
    import concourse.bacc as _bacc
    from concourse import mybir as _mybir
    from concourse.bass_utils import run_bass_kernel_spmd as _run

    nc = _bacc.Bacc("TRN2", target_bir_lowering=False, num_devices=1)
    arrays, args = {}, []
    for name in _INS:
        a = _np.ascontiguousarray(inputs[name])
        arrays[f"in_{name}_dram"] = a
        args.append(nc.dram_tensor(f"in_{name}_dram", a.shape, _mybir.dt.from_np(a.dtype), kind="ExternalInput").ap())
    for i, shape in enumerate(_OUTS):
        args.append(nc.dram_tensor(f"out_{i}_dram", shape, _mybir.dt.float32, kind="ExternalOutput").ap())
    build(nc, *args)
    r = _run(nc, [arrays], core_ids=[0])
    return tuple(r.results[0][f"out_{i}_dram"] for i in range(len(_OUTS)))
```

```python
from contextlib import ExitStack

import concourse.bass as bass
from concourse import mybir

F32 = mybir.dt.float32
F32R = mybir.dt.float32r
BF16 = mybir.dt.bfloat16
I32 = mybir.dt.int32
U32 = mybir.dt.uint32
ALU = mybir.AluOpType
ACT = mybir.ActivationFunctionType
X = mybir.AxisListType.X
ds = bass.ds

P = 128
D = 1024
KT = D // P
SEQ = 1024
NB = SEQ // P
NS = 8
T = NS + SEQ
CH = T // 3
NC = NS + 1
DEPTH = 2
NH, HD = 8, 64
PAGES, PS = 16, 128
NG, DK, DV = 4, 128, 256
CHUNK = 64
TAU = 16.0
NPAIR = 4096 // 256
EPS = 1e-6
NEG = -1e30


class V:

    def __init__(self, c, g=0, L=0):
        self.c, self.g, self.L = c, g, L
        self.v = c + g * L if L else c

    def plus(self, n):
        return V(self.c + n, self.g, self.L)

    def times(self, m):
        return V(self.c * m, self.g, self.L * m)

    @property
    def half(self):
        assert self.L % 2 == 0
        return V(self.c // 2, self.g, self.L // 2)

    @property
    def par(self):
        assert self.L % 2 == 0
        return self.c % 2


class Link:

    def __init__(self, eng, sem):
        self.eng, self.sem, self.n = eng, sem, V(0)

    def __call__(self, ins):
        self.n = self.n.plus(1)
        ins.then_inc(self.sem, 1)
        self.eng.wait_ge(self.sem, self.n.v)


def loop(eng, n, per, body, link=None, links=0, peel=0):
    for j in range(peel):
        body(V(j))
    n -= peel
    inner, body = body, lambda i: inner(i.plus(peel))
    full = n // per
    start = link.n if link else None
    if full > 1:
        with eng.Fori(0, full) as g:
            if link:
                link.n = V(start.c, g, per * links)
            for j in range(per):
                body(V(j, g, per))
            if link:
                assert link.n.c == start.c + per * links, (link.n.c - start.c, per)
        if link:
            link.n = V(start.c + full * per * links)
        done = full * per
    else:
        done = 0
    for j in range(done, n):
        body(V(j))


def build(nc, x_prompt, x_sample, c_prompt, c_sample, cache_k, cache_v, cache_logf, page_table, state_conv,
          state_gla, g_mix, g_ffn, w_ada, b_ada, w_in_even, b_f, g_q, g_k, w_conv, w_out_even, w_in_odd, w_gk,
          b_gk, g_o, w_out_odd, w_ff1, w_ff2,
          y_prompt, y_sample, k_prompt, v_prompt, logf_prompt, k_sample, v_sample, logf_sample, conv_prompt,
          conv_sample, gla_prompt, gla_sample):
    with ExitStack() as ctx:
        slab_start = (nc.sbuf_base + 31) // 32 * 32

        def at(name, shape, dt, offset):
            return nc.alloc_sbuf_tensor_at(name, shape, dt, offset=offset)

        def size(shape, dt):
            n = 2 if dt == BF16 else 4
            for s in shape[1:]:
                n *= s
            return (n + 31) // 32 * 32

        TILE = T * 4
        A0 = slab_start
        B0 = A0 + KT * TILE
        C0 = B0 + KT * TILE
        F0 = C0 + KT * TILE
        W0 = F0 + KT * TILE
        top = [W0]

        def put(name, shape, dt=F32):
            o = top[0]
            top[0] += size(shape, dt)
            return at(name, shape, dt, o)

        stage = put("stage", [P, 2, D])
        whi = put("whi", [P, 4, D], F32R)
        wlo = put("wlo", [P, 4, D], F32R)
        TMP0 = top[0]
        tmp = put("tmp", [P, 2, T])
        ident = put("ident", [P, P])
        ones = put("ones", [P, P])
        pairmask = put("pairmask", [P, P])
        eye8 = put("eye8", [P, 8, 8])
        vecT = put("vecT", [P, 144])
        modT = put("modT", [P, DEPTH, 48, NC])
        gain = put("gain", [P, 2 * DEPTH, KT, NC])
        eps = put("eps", [P, 1])
        t8 = put("t8", [P, NS])
        lay = top[0]
        tri = put("tri", [P, P])
        trisuf = put("trisuf", [P, P])
        later = put("later", [P, P])
        identb = put("identb", [P, P], BF16)
        negb = put("negb", [P, P], BF16)
        headrow = put("headrow", [8, NH, HD])
        gqb = put("gqb", [P, HD])
        gkb = put("gkb", [P, HD])
        bfb = put("bfb", [P, NH])
        sF = put("sF", [P, 13, NS])
        sNat = put("sNat", [NS, 3, 512])
        lf = put("lf", [P, NB + 1, NH])
        lft = put("lft", [P, NB + 1, NH])
        fcum = put("fcum", [P, NB, NH])
        prevT = put("prevT", [P, 4, 16])
        uOut = put("uOut", [P, 4, 10])
        rsq = put("rsq", [P, 2, 2 * NB])
        rsq8 = put("rsq8", [NS, 16])
        only8 = put("only8", [8, 8])
        snew = put("snew", [8, 8])
        peaks = put("peaks", [P, NB, 2])
        peak = put("peak", [P, NB])
        ysam = put("ysam", [P, 4, NS])
        U = at("U", [P, T + 2], F32, top[0])
        QA = put("QA", [P, NB, HD + 2])
        KA = put("KA", [P, NB, HD + 2])
        Lraw = at("Lraw", [P, PS, NH], F32, top[0])
        sqs = at("sqs", [P, NB, P], F32, top[0])
        Lsuf = put("Lsuf", [P, NH, P])
        sc = put("sc", [P, PAGES + 1, NH])
        PBx = put("PBx", [P, PAGES + 1, NH])
        idx = put("idx", [P, 1], I32)
        pt = put("pt", [1, P], I32)
        assert top[0] <= nc.sbuf_usable_end, top[0] - nc.sbuf_usable_end
        top[0] = lay
        gob = put("gob", [P, DV])
        wgk = put("wgk", [P, NG * DK])
        bcum = put("bcum", [P, T])
        qe = put("qe", [P, T])
        ke = put("ke", [P, T])
        scanm = put("scanm", [P, SEQ])
        S = tmp[:, 0, 3 * DV:4 * DV]
        kdn = put("kdn", [P, 2, 2, P])
        aT = put("aT", [P, 2, P])
        wgh = put("wgh", [P, P])
        dec = put("dec", [P, 16])
        dec_s = put("dec_s", [P, NG, NS])
        zs = put("zs", [P, NG, NS])
        vs_f = put("vs_f", [P, 8, NS])
        ss1 = put("ss1", [P, 2, 2])
        ss8 = put("ss8", [NS, NG])
        assert top[0] <= nc.sbuf_usable_end, top[0] - nc.sbuf_usable_end

        xT = at("xT", [P, KT, T], F32, A0)
        hh = at("hh", [P, KT, T], F32R, B0)
        hl = at("hl", [P, KT, T], F32R, C0)
        hid = [at(n, [P, 2, 2, T], F32R, F0 + i * 4 * TILE) for i, n in enumerate(("hid_hi", "hid_lo"))]
        ada = at("ada", [P, 4, KT, 512], F32, B0)
        xin = at("xin", [P, NB, D], F32, F0)
        vec1 = at("vec1", [P, P], F32, W0)
        vec2 = at("vec2", [16, P], F32, W0 + 512)
        c9 = at("c9", [NC, D], F32, W0 + 1024)
        c9e = at("c9e", [NC, D], F32, W0 + 1024 + 4096)
        xs = at("xs", [NS, D], F32, W0 + 1024 + 8192)
        sconv = at("sconv", [16, 512], F32, W0 + 1024 + 12288)
        scT = at("scT", [P, KT, NC], F32, W0 + 20480)
        modrow = at("modrow", [P, 512], F32, W0 + 20480 + 512)
        rstd = at("rstd", [P, T], F32, F0)
        sqsum = at("sqsum", [P, T], F32, F0 + TILE)
        qstore = nc.dram_tensor("qstore", (NS, 512), F32, kind="Internal").ap()
        rstore = nc.dram_tensor("rstore", (P, KT * T), F32, kind="Internal").ap()
        bstore = nc.dram_tensor("bstore", (P, NG * SEQ), F32, kind="Internal").ap()
        xstore = nc.dram_tensor("xstore", (P, KT * T), F32, kind="Internal").ap()
        QK = at("QK", [P, 2, NB, NH * HD], F32, A0)
        Vn = at("Vn", [P, NB, NH * HD], F32, F0)
        ya = at("ya", [P, 4, T], F32, F0 + 16384)
        sq8 = at("sq8", [NS, 2, 512], F32, C0)
        crow = at("crow", [10, 512], F32, C0 + 8192)
        qT = at("qT", [HD + 2, SEQ], F32, B0)
        kT = at("kT", [HD + 2, SEQ], F32, B0 + 4096)
        PT = at("PT", [P, NB * (NB + 1) // 2 * P], F32, B0 + 8192)
        rden = at("rden", [P, SEQ], F32, B0 + 26624)
        qbc = at("qbc", [P, 512], F32, B0 + 30720)
        mx8 = at("mx8", [P, 8], F32, B0 + 32768)
        small = at("small", [P, 32], F32, B0 + 32768 + 32)
        Vp = at("Vp", [P, NB, P], F32, TMP0)
        Psum = at("Psum", [P, SEQ], F32, TMP0 + 4096)
        omask = sNat[:, 1, :]
        LT = at("LT", [P, NH, P], F32, B0)
        TB = at("TB", [P, NH, P], F32, B0 + 4096)
        LN = at("LN", [8, NH, P], F32, B0 + 8192)
        ptot = at("ptot", [P, NH], F32, B0 + 12288)
        pages = at("pages", [P, 8, 2, 512], F32, C0)
        qk1 = at("qk1", [P, KT, T], F32, A0)
        Vo = at("Vo", [P, NB, D], F32, F0)
        draw = tmp[:, 1, NS:T]
        rT = at("rT", [P, KT, T], F32, B0)
        sst = at("sst", [P, NS, DV], F32, C0)
        sout = at("sout", [P, NS, DV], F32, C0 + 8192)
        kmask = at("kmask", [NS, NS, P], F32, C0 + 16384)
        qmask = at("qmask", [P, NS, NS], F32, C0 + 20480)
        kvnat = at("kvnat", [NS, NG * DK + D], F32, C0 + 20736)
        osn = at("osn", [NS, D], F32, C0 + 26880)
        ynat = at("ynat", [P, NB, D], F32, F0)
        ysn = at("ysn", [NS, D], F32, B0)

        ps = ctx.enter_context(nc.psum_tensor("ps", [P, 8, 512], F32))

        def acc(par):
            return ps[:, 3 * par:3 * par + 3, 0:CH]

        def thirds(ap):
            return ap.rearrange("p (c n) -> p c n", c=3)

        def sem(name):
            return ctx.enter_context(nc.semaphore(name))

        consts_made = sem("consts_made")
        small_loaded = sem("small_loaded")
        x_loaded = sem("x_loaded")
        ada_loaded = [sem(f"ada_loaded{i}") for i in range(4)]
        w_loaded = [sem(f"w_loaded{i}") for i in range(2)]
        w_split = sem("w_split")
        acc_done = sem("acc_done")
        acc_free = [sem("acc_free0"), sem("acc_free1")]
        passed = sem("passed")
        pool_link = sem("pool_link")
        dve_link = sem("dve_link")
        act_link = sem("act_link")
        setup_pe = sem("setup_pe")
        setup_dve = sem("setup_dve")
        silu_pos = sem("silu_pos")
        ada_done = sem("ada_done")
        mod_rows = sem("mod_rows")
        mod_turned = sem("mod_turned")
        ada_kept = sem("ada_kept")
        xt_done = sem("xt_done")
        xt_kept = sem("xt_kept")
        sq_ready = sem("sq_ready")
        sq_added = sem("sq_added")
        sq_summed = sem("sq_summed")
        rstd_ready = sem("rstd_ready")
        norm_scaled = sem("norm_scaled")
        norm_affine = sem("norm_affine")
        norm_hi = sem("norm_hi")
        h_ready = sem("h_ready")
        x_spilled = sem("x_spilled")
        x_back = sem("x_back")
        tmp_full = sem("tmp_full")
        nat_done = sem("nat_done")
        nat_kept = sem("nat_kept")
        hid_squared = sem("hid_squared")
        hid_hi_ready = sem("hid_hi_ready")
        hid_ready = sem("hid_ready")
        qk_summed = sem("qk_summed")
        qk_rs = sem("qk_rs")
        qk_scaled = sem("qk_scaled")
        prep_pe = sem("prep_pe")
        prep_act = sem("prep_act")
        prep_dve = sem("prep_dve")
        kv_out = sem("kv_out")
        outs = sem("outs")
        a_built = sem("a_built")
        a_turned = sem("a_turned")
        a_q = sem("a_q")
        a_k = sem("a_k")
        a_s = sem("a_s")
        a_max = sem("a_max")
        a_shift = sem("a_shift")
        a_again = sem("a_again")
        a_q2 = sem("a_q2")
        a_st = sem("a_st")
        a_p = sem("a_p")
        a_av = sem("a_av")
        a_sum = sem("a_sum")
        a_den = sem("a_den")
        a_lnd = sem("a_lnd")
        a_rden = sem("a_rden")
        a_pair = sem("a_pair")
        vp_ready = sem("vp_ready")
        q_stored = sem("q_stored")
        qbc_in = sem("qbc_in")
        lf_gathered = sem("lf_gathered")
        pages_in = [sem(f"pages_in{i}") for i in range(8)]
        k_used = sem("k_used")
        v_used = sem("v_used")
        d_pe = sem("d_pe")
        d_act = sem("d_act")
        d_dve = sem("d_dve")
        y_hi = sem("y_hi")
        y_ready = sem("y_ready")
        g_act = sem("g_act")
        g_dve = sem("g_dve")
        g_diff = sem("g_diff")
        gb_a = sem("gb_a")
        gb_scores = sem("gb_scores")
        gb_kd = sem("gb_kd")
        gb_state = sem("gb_state")
        gb_inter = sem("gb_inter")
        gb_kv = sem("gb_kv")
        gb_rs = sem("gb_rs")
        gb_out = sem("gb_out")
        g_stored = sem("g_stored")
        gate_cleared = sem("gate_cleared")
        gate_loaded = sem("gate_loaded")
        r_exp = sem("r_exp")
        r_stored = [sem("r_stored0"), sem("r_stored1")]
        r_in = sem("r_in")
        w_copied = sem("w_copied")
        z_summed = sem("z_summed")
        z_folded = sem("z_folded")
        z_logs = sem("z_logs")
        z_scanned = sem("z_scanned")
        z_stored = sem("z_stored")
        zs_summed = sem("zs_summed")
        zs_folded = sem("zs_folded")
        zs_logs = sem("zs_logs")
        zs_ready = sem("zs_ready")
        dec_s_ready = sem("dec_s_ready")
        b_in = sem("b_in")
        b_used = sem("b_used")
        s_in = sem("s_in")
        s_turned = sem("s_turned")
        s_kv = sem("s_kv")
        s_masks = sem("s_masks")
        s_outer = sem("s_outer")
        s_new = sem("s_new")
        s_out = sem("s_out")
        s_added = sem("s_added")
        s_squares = sem("s_squares")
        s_rs = sem("s_rs")
        s_scaled = sem("s_scaled")
        gla_stored = sem("gla_stored")
        y_s = sem("y_s")
        g_tr = sem("g_tr")
        g_trk = sem("g_trk")
        y_turned = sem("y_turned")
        y_kept = sem("y_kept")

        block = ctx.enter_context(nc.Block())

        wie = w_in_even[0].rearrange("(k p) n -> p k n", p=P)
        woe = w_out_even[0].rearrange("(k p) n -> p k n", p=P)
        wio = w_in_odd[0].rearrange("(k p) n -> p k n", p=P)
        woo = w_out_odd[0].rearrange("(k p) n -> p k n", p=P)
        E_IN, O_IN = w_in_even.shape[2], w_in_odd.shape[2]

        U_IN, U_OUT, U_MLP = [0, 97], [25, 122], [33, 130]
        T_NORM, T_IN, T_OUT, T_MLP = [0, 34, 195, 229], [1, 196], [26, 221], [35, 230]
        SMALL = 14

        query_pieces = [(i, c, 512 * c, min((i + 1) * P, 512 * (c + 1)) - 512 * c)
                        for i in range(NB) for c in range(2) if 512 * c < (i + 1) * P]
        key_pieces = [(j, c, max(512 * c, j * P), 512 * (c + 1) - max(512 * c, j * P))
                      for j in range(NB) for c in range(2) if 512 * (c + 1) > j * P]
        NP = len(key_pieces)
        key_at = [sum(SEQ - m * P for m in range(j)) for j in range(NB)]

        def all_read(eng, t):
            eng.wait_ge(acc_free[0], (t + 1) // 2)
            eng.wait_ge(acc_free[1], t // 2)

        def done(t, nn):
            return t.plus(1 - nn).v

        @block.sync
        def _(sp):
            def small_load(dst, src):
                sp.dma_start(dst, src).then_inc(small_loaded, 16)

            small_load(vec1[0:96, :], b_ada.rearrange("l (n p) -> (l n) p", p=P))
            small_load(vec1[96:112, :], g_mix.rearrange("l (n p) -> (l n) p", p=P))
            small_load(vec1[112:128, :], g_ffn.rearrange("l (n p) -> (l n) p", p=P))
            small_load(vec2[0:12, :], w_conv[0].rearrange("j (c p) -> (j c) p", p=P))
            small_load(vec2[12:16, :], b_gk.rearrange("o (c p) -> (o c) p", p=P))
            small_load(c9[0:NS, :], c_sample)
            small_load(c9[NS:NC, :], c_prompt)
            small_load(xs[:, :], x_sample.rearrange("b s d -> (b s) d"))
            small_load(sconv[:, :], state_conv.rearrange("b e j c -> (b e j) c"))
            small_load(gqb[:, :], g_q.to_broadcast([P, HD]))
            small_load(gkb[:, :], g_k.to_broadcast([P, HD]))
            small_load(bfb[:, :], b_f.to_broadcast([P, NH]))
            small_load(idx[:, :], page_table.rearrange("b (p o) -> (b p) o", o=1))
            small_load(pt[:, :], page_table.rearrange("(o b) p -> o (b p)", o=1))
            for b in range(NB):
                sp.dma_start(xin[:, b, :], x_prompt[0, b * P:(b + 1) * P, :]).then_inc(x_loaded, 16)

            def load_ada(i, l):
                if l or i.c >= 4 or i.L:
                    sp.wait_ge(ada_done, i.plus(12 * l - 3).v)
                sp.dma_start(ada[:, i.c % 4, :, :],
                             w_ada[l].rearrange("(k p) n -> p k n", p=P)[:, :, ds(i.times(512).v, 512)]
                             ).then_inc(ada_loaded[i.c % 4], 16)

            for l in range(DEPTH):
                loop(sp, 12, 4, lambda i: load_ada(i, l), peel=4)

            def load_unit(u, src):
                if u.c >= 2 or u.L:
                    sp.wait_ge(w_split, u.plus(-1).v)
                sp.sem_inc(passed, 1)
                dst = stage[:, u.c % 2, :]
                if len(src.shape) == 3:
                    dst = dst.rearrange("p (k n) -> p k n", n=P)
                sp.dma_start(dst, src).then_inc(w_loaded[u.par], 16)

            def in_units(base, w, col, n, per=4):
                loop(sp, n, per, lambda i: load_unit(i.plus(base), w[:, :, ds(i.times(P).plus(col).v, P)]), peel=2)

            def mlp_units(l):
                base = U_MLP[l]
                w1 = w_ff1[l].rearrange("(k p) n -> p k n", p=P)
                w2 = w_ff2[l].rearrange("(r p) n -> p r n", p=P)

                def up(i, u):
                    for j in range(2):
                        load_unit(u.plus(j), w1[:, :, ds(i.times(256).plus(128 * j).v, P)])

                def down(i, u):
                    for j in range(2):
                        load_unit(u.plus(j), w2[:, ds(i.times(2).plus(j).v, 1), :].rearrange("p r n -> p (r n)"))

                def step(i):
                    up(i.plus(1), i.times(4).plus(base + 2))
                    down(i, i.times(4).plus(base + 4))

                up(V(0), V(base))
                loop(sp, NPAIR - 1, 1, step)
                down(V(NPAIR - 1), V(base + 62))

            sp.wait_ge(setup_dve, 3)
            in_units(U_IN[0], wie, 1536, 12)

            def conv_units(c):
                for j, col in enumerate((512, 1024, 0)):
                    load_unit(c.times(3).plus(U_IN[0] + 12 + j), wie[:, :, ds(c.times(P).plus(col).v, P)])
            loop(sp, 4, 2, conv_units)
            load_unit(V(U_IN[0] + 24), wie[:, :, E_IN - P:E_IN])
            for i in range(6):
                load_unit(V(U_OUT[0] + i), woe[:, :, i * P:(i + 1) * P])
            sp.wait_ge(prep_dve, 6)
            tok = "(b p) h d -> p b (h d)"
            for dst, src in ((k_prompt[0, 0].rearrange(tok, p=P), QK[:, 1]), (v_prompt[0, 0].rearrange(tok, p=P), Vn[:, :, :]),
                             (logf_prompt[0, 0].rearrange("(b p) h -> p b h", p=P), lf[:, 0:NB, :]),
                             (k_sample.rearrange("b e s h d -> (b e s) (h d)"), sNat[:, 1, :]),
                             (v_sample.rearrange("b e s h d -> (b e s) (h d)"), sNat[:, 2, :]),
                             (logf_sample.rearrange("b e s h -> (b e s) h"), lf[0:NS, NB, :])):
                sp.dma_start(dst, src).then_inc(kv_out, 16)
            cs = conv_sample.rearrange("b e j c -> (b e) j c")
            sp.dma_start(cs[:, 0, :], state_conv.rearrange("b e j c -> (b e) j c")[:, 1, :]).then_inc(kv_out, 16)
            sp.dma_start(cs[:, 1, :], crow[0:NS, :]).then_inc(kv_out, 16)
            sp.dma_start(conv_prompt[0, 0], crow[NS:10, :]).then_inc(kv_out, 16)

            sp.dma_start(qstore, sNat[:, 0, :]).then_inc(q_stored, 16)
            sp.wait_ge(q_stored, 16)
            sp.wait_ge(kv_out, 16 * 9)
            sp.wait_ge(d_pe, 2)

            def load_pages(b):
                if b.c or b.L:
                    sp.wait_ge(k_used, b.times(8).v)
                sp.sem_inc(passed, 1)
                sp.dma_start(qbc[:, :], qstore[ds(b.v, 1), :].to_broadcast([P, 512])).then_inc(qbc_in, 16)
                for j in range(16):
                    cache = cache_k if j < 8 else cache_v
                    if j >= 8:
                        sp.wait_ge(k_used, b.times(8).plus(j - 7).v)
                    elif b.c or b.L:
                        sp.wait_ge(v_used, b.times(8).plus(j - 7).v)
                    sp.sem_inc(passed, 1)
                    for q in range(2):
                        page = sp.value_load(pt[0:1, ds(b.times(PAGES).plus(2 * (j % 8) + q).v, 1)],
                                             min_val=0, max_val=cache_k.shape[0] - 1)
                        sp.dma_start(pages[:, j % 8, q, :], cache[ds(page, 1), 0].rearrange("a p h d -> (a p) (h d)")
                                     ).then_inc(pages_in[j % 8], 16)
            load_pages(V(0))
            loop(sp, NS - 1, 1, lambda b: load_pages(b.plus(1)))

            sp.wait_ge(x_spilled, 16)
            sp.wait_ge(y_ready, KT)
            sp.dma_start(xT[:, :, :], xstore.rearrange("p (k n) -> p k n", k=KT)).then_inc(x_back, 16)
            for i in (6, 7):
                load_unit(V(U_OUT[0] + i), woe[:, :, i * P:(i + 1) * P])
            mlp_units(0)

            in_units(U_IN[1], wio, 0, 16)
            sp.wait_ge(gate_cleared, 1)
            sp.dma_start(gob[:, :], g_o.to_broadcast([P, DV])).then_inc(gate_loaded, 16)
            sp.dma_start(wgk[P - 16:P, :], w_gk[0]).then_inc(gate_loaded, 16)
            load_unit(V(U_IN[1] + 16), wio[:, :, O_IN - P:O_IN])
            in_units(U_IN[1] + 17, wio, 2048, 8)
            for i in range(6):
                load_unit(V(U_OUT[1] + i), woo[:, :, i * P:(i + 1) * P])
            all_read(sp, T_IN[1] + 25)
            sp.wait_ge(z_stored, 16 * NG)
            sp.wait_ge(zs_summed, 1)
            for h in range(NG):
                if h:
                    sp.wait_ge(b_used, 2 * h)
                sp.dma_start(draw, bstore[:, h * SEQ:(h + 1) * SEQ]).then_inc(b_in, 16)
                if h:
                    sp.wait_ge(s_new, NS * h)
                sp.dma_start(sst[:, :, :], state_gla[:, 0, h].rearrange("b k v -> k b v")).then_inc(s_in, 16)
                if h == 0:
                    for i in range(2):
                        sp.wait_ge(r_stored[i], 16 * KT // 2)
                    sp.dma_start(rT[:, :, :], rstore.rearrange("p (k n) -> p k n", k=KT)).then_inc(r_in, 16)
                sp.wait_ge(s_new, NS * (h + 1))
                sp.dma_start(gla_sample[:, 0, h].rearrange("b k v -> k b v"), sout[:, :, :]).then_inc(gla_stored, 16)
            sp.wait_ge(x_spilled, 32)
            sp.wait_ge(y_ready, 2 * KT)
            sp.dma_start(xT[:, :, :], xstore.rearrange("p (k n) -> p k n", k=KT)).then_inc(x_back, 16)
            for i in (6, 7):
                load_unit(V(U_OUT[1] + i), woo[:, :, i * P:(i + 1) * P])
            mlp_units(1)
            for b in range(NB):
                sp.wait_ge(y_kept, b + 1)
                sp.dma_start(y_prompt[0, b * P:(b + 1) * P, :], ynat[:, b, :]).then_inc(outs, 16)
            sp.wait_ge(y_kept, NB + 1)
            sp.dma_start(y_sample.rearrange("b s d -> (b s) d"), ysn[:, :]).then_inc(outs, 16)
            sp.wait_ge(outs, 16 * (NB + 1))
            sp.wait_ge(gla_stored, 16 * NG)

        used_at = {}
        for l in range(DEPTH):
            nn = 2 * l + 1
            for i in range(25):
                used_at[U_IN[l] + i] = T_IN[l] - nn + i + 1
            for i in range(8):
                used_at[U_OUT[l] + i] = T_OUT[l] - nn + i + 1
            nn += 1
            for j in range(2):
                used_at[U_MLP[l] + j] = T_MLP[l] - nn + j + 1
            for i in range(NPAIR):
                if i < NPAIR - 1:
                    for j in range(2):
                        used_at[U_MLP[l] + 2 + 4 * i + j] = T_MLP[l] - nn + 10 * i + 2 + j + 1
                last = i < NPAIR - 1
                for j in range(2):
                    used_at[U_MLP[l] + (4 if last else 2) + 4 * i + j] = T_MLP[l] - nn + 10 * i + (12 if last else 10)

        @block.gpsimd
        def _(pool):
            link = Link(pool, pool_link)

            def select(t, cmp, fill, base, pattern, mult):
                link(pool.affine_select(out=t, in_=t, compare_op=cmp, fill=fill, base=base, pattern=pattern,
                                        channel_multiplier=mult))

            for t, v in ((ident, 0.0), (ones, 1.0), (tri, 1.0), (trisuf, 1.0), (later, 1.0), (pairmask, 1.0),
                         (eye8, 0.0), (headrow, 0.0), (only8, 0.0), (identb, 0.0), (negb, 0.0), (eps, EPS)):
                link(pool.memset(t[tuple(slice(None) for _ in t.shape)], v))
            select(ident[:, :], ALU.not_equal, 1.0, 0, [[-1, P]], 1)
            select(identb[:, :], ALU.not_equal, 1.0, 0, [[-1, P]], 1)
            select(tri[:, :], ALU.is_ge, 0.0, 0, [[1, P]], -1)
            select(trisuf[:, :], ALU.is_ge, 0.0, -1, [[-1, P]], 1)
            select(later[:, :], ALU.is_ge, 0.0, -1, [[-1, P]], 1)
            select(later[:, :].rearrange("p (b g) -> p b g", g=PAGES), ALU.is_ge, 0.0, PAGES - 1,
                   [[PAGES, NS], [0, PAGES]], -1)
            select(pairmask[:, :], ALU.is_ge, 0.0, 0, [[1, P]], -1)
            select(pairmask[:, :].rearrange("p (c r) -> p c r", r=CHUNK), ALU.is_ge, 0.0, 0,
                   [[-CHUNK, 2], [0, CHUNK]], 1)
            select(eye8[:, :, :], ALU.not_equal, 1.0, 0, [[1, 8], [-1, 8]], 0)
            select(headrow[:, :, :], ALU.not_equal, 1.0, 0, [[-1, NH], [0, HD]], 1)
            select(only8[:, :], ALU.is_equal, NEG, 0, [[-1, 8]], 1)
            pool.affine_select(out=negb[:, :], in_=negb[:, :], compare_op=ALU.is_ge, fill=NEG, base=0,
                               pattern=[[-1, P]], channel_multiplier=1).then_inc(consts_made, 1)
            def split(u, used=None):
                if used is None and u.c >= 4:
                    used = V(used_at[u.c - 4])
                if used is not None:
                    pool.wait_ge(acc_done, used.v)
                pool.wait_ge(w_loaded[u.par], u.half.times(16).plus(16).v)
                pool.sem_inc(passed, 1)
                link(pool.tensor_copy(whi[:, u.c % 4, :], stage[:, u.c % 2, :]))
                pool.tensor_tensor(wlo[:, u.c % 4, :], stage[:, u.c % 2, :], whi[:, u.c % 4, :].bitcast(F32),
                                   ALU.subtract).then_inc(w_split, 1)

            def in_split(base, first, n):
                loop(pool, n, 4, lambda i: split(i.plus(base + first), i.plus(used_at[base + first - 4])
                                                 if first >= 4 else None), link, 1)

            pool.wait_ge(setup_dve, 3)
            for l in range(DEPTH):
                for i in range(4):
                    if l == 0 and i == 3:
                        pool.wait_ge(setup_dve, 4)
                    split(V(U_IN[l] + i))
                in_split(U_IN[l], 4, 20)
                split(V(U_IN[l] + 24))
                for i in range(4):
                    split(V(U_OUT[l] + i))
                if l == 0:
                    pool.wait_ge(qk_scaled, 2 * NB)
                    pool.indirect_dma_start(Lraw[:, :, :].rearrange("p s h -> p (s h)"), None,
                                            cache_logf.rearrange("a e s h -> (a e) (s h)"),
                                            bass.IndirectOffsetOnAxis(ap=idx[:, 0:1].bitcast(U32), axis=0)
                                            ).then_inc(lf_gathered, 16)
                    pool.wait_ge(prep_dve, 6)

                    def head(h):
                        n = h.times(NP)
                        pool.wait_ge(a_p, n.plus(2).v)
                        if h.c or h.L:
                            pool.wait_ge(a_den, h.v)
                        pool.sem_inc(passed, 1)
                        link(pool.tensor_copy(Psum[:, :], PT[:, 0:SEQ]))
                        for j in range(1, NB):
                            pool.wait_ge(a_p, n.plus(2 + sum(1 for q in key_pieces if 1 <= q[0] <= j)).v)
                            o = Psum[:, j * P:SEQ]
                            add = pool.tensor_tensor(o, o, PT[:, key_at[j]:key_at[j] + SEQ - j * P], ALU.add)
                            if j < NB - 1:
                                link(add)
                        add.then_inc(a_sum, 1)
                        pool.wait_ge(a_sum, h.plus(1).v)

                    def pair(p):
                        if p.c or p.L:
                            pool.wait_ge(a_av, p.times(2).v)
                        pool.sem_inc(passed, 1)
                        pool.tensor_copy(Vp[:, :, :], Vn[:, :, ds(p.times(P).v, P)]).then_inc(vp_ready, 1)
                        for e in range(2):
                            head(p.times(2).plus(e))
                    loop(pool, NH // 2, 1, pair, link, 2 * (NB - 1), peel=1)
                for i in range(4, 8):
                    split(V(U_OUT[l] + i))
                for i in range(6):
                    split(V(U_MLP[l] + i))
                base, done = U_MLP[l], T_MLP[l] - 2 * l - 2

                def step(i):
                    for j in range(2):
                        split(i.times(4).plus(base + 2 + j), i.times(10).plus(done - 8 + j + 1))
                    for j in range(2):
                        split(i.times(4).plus(base + 4 + j), i.times(10).plus(done + 2))
                loop(pool, NPAIR - 2, 1, lambda i: step(i.plus(1)), link, 4)
                for j in range(2):
                    split(V(U_MLP[l] + 62 + j))

        @block.tensor
        def _(pe):
            def turn(out, in_):
                k = in_.shape[0]
                return pe.transpose(out, in_, ident[0:k, 0:k])

            def acc_wait(t):
                if t.c >= 2 or t.L:
                    pe.wait_ge(acc_free[t.par], t.half.v)

            def product(t, parts):
                acc_wait(t)
                n = len(parts)
                for k, (wh, wl, xh, xl) in enumerate(parts):
                    for q, (w, x) in enumerate(((wh, xh), (wh, xl), (wl, xh))):
                        for c in range(3):
                            last = pe.matmul(ps[:, 3 * t.par + c, 0:CH], w, x[:, c * CH:(c + 1) * CH],
                                             start=(k == 0 and q == 0), stop=(k == n - 1 and q == 2))
                last.then_inc(acc_done, 1)

            def gemm(u, t):
                pe.wait_ge(w_split, u.plus(1).v)
                s = u.c % 4
                product(t, [(whi[:, s, k * P:(k + 1) * P], wlo[:, s, k * P:(k + 1) * P], hh[:, k, :], hl[:, k, :])
                            for k in range(KT)])

            def gemm_pair(u, t, ready, n):
                pe.wait_ge(w_split, u.plus(2).v)
                acc_wait(t)
                acc_wait(t.plus(1))
                for k in range(KT):
                    pe.wait_ge(ready, KT * n + k + 1)
                    for j in range(2):
                        s = (u.c + j) % 4
                        wh, wl = whi[:, s, k * P:(k + 1) * P], wlo[:, s, k * P:(k + 1) * P]
                        for q, (w, x) in enumerate(((wh, hh), (wh, hl), (wl, hh))):
                            for c in range(3):
                                last = pe.matmul(ps[:, 3 * ((t.c + j) % 2) + c, 0:CH], w, x[:, k, c * CH:(c + 1) * CH],
                                                 start=(k == 0 and q == 0), stop=(k == KT - 1 and q == 2))
                        if k == KT - 1:
                            last.then_inc(acc_done, 1)

            def norm(n):
                t = V(T_NORM[n])
                acc_wait(t)
                pe.wait_ge(sq_added, (KT - 1) * (n + 1))
                for c in range(3):
                    last = pe.matmul(ps[:, 3 * t.par + c, 0:CH], ones[:, :], sqsum[:, c * CH:(c + 1) * CH],
                                     start=True, stop=True)
                last.then_inc(sq_summed, 1)

            def to_tokens(i):
                pe.wait_ge(tmp_full, i.plus(1).v)
                if i.c or i.L:
                    pe.wait_ge(nat_kept, i.v)
                for b in range(NB):
                    last = turn(ps[:, 6 + b // 4, (b % 4) * P:(b % 4 + 1) * P],
                                tmp[:, i.c % 2, NS + b * P:NS + (b + 1) * P])
                last.then_inc(nat_done, 1)

            def mlp(l):
                u0, t0 = U_MLP[l], T_MLP[l]

                def up(i, u, t):
                    for j in range(2):
                        gemm(u.plus(j), t.plus(j))

                def down(i, u, t):
                    pe.wait_ge(w_split, u.plus(2).v)
                    pe.wait_ge(hid_ready, i.times(2).plus(2 * NPAIR * l + 2).v)
                    for f in range(KT):
                        product(t.plus(f), [(whi[:, (u.c + j) % 4, f * P:(f + 1) * P],
                                             wlo[:, (u.c + j) % 4, f * P:(f + 1) * P],
                                             hid[0][:, i.c % 2, j, :], hid[1][:, i.c % 2, j, :]) for j in range(2)])

                def step(i):
                    up(i.plus(1), i.times(4).plus(u0 + 2), i.times(10).plus(t0 + 2))
                    down(i, i.times(4).plus(u0 + 4), i.times(10).plus(t0 + 4))
                gemm_pair(V(u0), V(t0), h_ready, 2 * l + 1)
                loop(pe, NPAIR - 1, 2, step, peel=1)
                down(V(NPAIR - 1), V(u0 + 62), V(t0 + 152))

            def out_proj(l):
                gemm_pair(V(U_OUT[l]), V(T_OUT[l]), y_ready, l)
                for i in range(2, KT):
                    gemm(V(U_OUT[l] + i), V(T_OUT[l] + i))

            pe.wait_ge(consts_made, 1)
            pe.wait_ge(small_loaded, 16 * SMALL)
            turn(ps[:, 0, 0:P], vec1[:, :])
            turn(ps[:, 0, P:P + 16], vec2[:, :])
            for c in range(4):
                turn(ps[:, 0, 256 + 16 * c:272 + 16 * c], sconv[:, c * P:(c + 1) * P])
            for k in range(KT):
                last = turn(ps[:, 1, NS * k:NS * k + NS], xs[:, k * P:(k + 1) * P])
            last.then_inc(setup_pe, 1)
            pe.wait_ge(setup_dve, 2)
            for k in range(KT):
                last = turn(ps[:, 1, P + NC * k:P + NC * (k + 1)], c9[:, k * P:(k + 1) * P])
            last.then_inc(setup_pe, 1)
            pe.wait_ge(x_loaded, 16 * NB)
            for k in range(KT):
                if k >= 2:
                    pe.wait_ge(xt_kept, k - 1)
                for b in range(NB):
                    last = turn(ps[:, 2 + 2 * (k % 2) + b // 4, (b % 4) * P:(b % 4 + 1) * P],
                                xin[:, b, k * P:(k + 1) * P])
                last.then_inc(xt_done, 1)
            pe.wait_ge(setup_dve, 3)

            def modulation_turned(g):
                pe.wait_ge(mod_rows, g.times(4).plus(4).v)
                if g.c or g.L:
                    pe.wait_ge(ada_kept, g.v)
                pe.sem_inc(passed, 1)
                for f in range(4):
                    last = turn(ps[:, 4, f * P:(f + 1) * P], modrow[:, f * P:(f + 1) * P])
                last.then_inc(mod_turned, 1)

            def modulation(g):
                for j in range(4):
                    i = g.times(4).plus(j)
                    pe.wait_ge(ada_loaded[j], g.times(16).plus(16).v)
                    if j >= 2 or g.c or g.L:
                        pe.wait_ge(mod_rows, i.plus(-1).v)
                    pe.sem_inc(passed, 1)
                    for k in range(KT):
                        last = pe.matmul(ps[32 * j:32 * j + NC, 6 + j % 2, :], scT[:, k, :], ada[:, j, k, :],
                                         start=(k == 0), stop=(k == KT - 1))
                    last.then_inc(ada_done, 1)
                    if j == 0 and (g.c or g.L):
                        modulation_turned(g.plus(-1))
            pe.wait_ge(xt_kept, KT)
            modulation(V(0))
            norm(0)
            loop(pe, 5, 1, lambda g: modulation(g.plus(1)))
            modulation_turned(V(5))

            gemm_pair(V(U_IN[0]), V(T_IN[0]), h_ready, 0)
            to_tokens(V(0))

            def natural(i):
                gemm(i.plus(U_IN[0] + 1), i.plus(T_IN[0] + 1))
                to_tokens(i)
            loop(pe, 10, 4, lambda i: natural(i.plus(1)), peel=2)
            gemm(V(U_IN[0] + 12), V(T_IN[0] + 12))
            to_tokens(V(11))
            loop(pe, 12, 4, lambda i: gemm(i.plus(U_IN[0] + 13), i.plus(T_IN[0] + 13)))
            to_tokens(V(12))
            all_read(pe, T_IN[0] + 25)
            for i in range(12):
                turn(ps[0:NS, i // 4, (i % 4) * P:(i % 4 + 1) * P], sF[:, i, :])
            turn(ps[0:NS, 3, 0:P], sF[:, 12, :])
            for c in range(4):
                last = turn(ps[0:10, 4, c * P:(c + 1) * P], uOut[:, c, :])
            last.then_inc(prep_pe, 1)
            pe.wait_ge(prep_dve, 5)
            for b in range(NB):
                for j in range(b):
                    pe.matmul(ps[:, 5, NH * b:NH * (b + 1)], ones[:, :], lf[:, j, :], start=(j == 0), stop=False)
                last = pe.matmul(ps[:, 5, NH * b:NH * (b + 1)], tri[:, :], lf[:, b, :], start=(b == 0), stop=True)
            last.then_inc(prep_pe, 1)

            pe.wait_ge(lf_gathered, 16)
            pe.wait_ge(prep_dve, 6)
            for h in range(NH):
                last = turn(ps[:, 2 + h // 4, (h % 4) * P:(h % 4 + 1) * P], Lraw[:, :, h])
            last.then_inc(d_pe, 1)
            pe.wait_ge(d_dve, 1)
            for h in range(NH):
                o = ps[:, 6 + h // 4, (h % 4) * P:(h % 4 + 1) * P]
                pe.matmul(o, trisuf[:, :], LT[:, h, :], start=True, stop=False)
                pe.matmul(o, TB[:, h, :], later[:, :], start=False, stop=False)
                last = pe.matmul(o.rearrange("p (b g) -> p b g", g=PAGES), LN[:, h, :],
                                 ident[0:NS, 0:NS].unsqueeze(2).to_broadcast([NS, NS, PAGES]), start=False, stop=True)
            last.then_inc(d_pe, 1)
            pe.wait_ge(d_dve, 2)

            def sequence_peaks(b):
                pe.wait_ge(d_dve, b.times(6).plus(2 + 1).v)
                pe.sem_inc(passed, 1)
                turn(ps[0:8, 7, 0:P], mx8[:, :]).then_inc(d_pe, 1)

            def sequence_peak(b):
                pe.wait_ge(d_dve, b.times(6).plus(2 + 2).v)
                pe.sem_inc(passed, 1)
                pe.matmul(ps[:, 7, 128:136], ones[0:8, :], small[0:8, 8:16], start=True, stop=True).then_inc(d_pe, 1)

            def sequence_values(b, j):
                if j == 0:
                    pe.wait_ge(d_act, b.plus(1).v)
                pe.wait_ge(pages_in[j], b.times(64).plus(64).v)
                pe.sem_inc(passed, 1)
                for q in range(2):
                    last = pe.matmul(ps[0:8, 6, :], PBx[:, 2 * j + q, :], pages[:, j, q, :],
                                     start=(j == 0 and q == 0), stop=False)
                last.then_inc(v_used, 1)

            def sequence_sum(b):
                pe.matmul(ps[0:8, 6, :], PBx[0:NS, PAGES, :], sNat[:, 2, :], start=False, stop=True)
                pe.wait_ge(d_dve, b.times(6).plus(2 + 4).v)
                pe.sem_inc(passed, 1)
                pe.matmul(ps[0:8, 7, 144:145], small[:, 16:24], ones[:, 0:1], start=True, stop=True).then_inc(d_pe, 1)

            def sequence_out(b):
                pe.wait_ge(d_dve, b.times(6).plus(2 + 5).v)
                pe.sem_inc(passed, 1)
                for c in range(4):
                    last = pe.matmul(ps[:, 7, 152 + c:153 + c], omask[:, c * P:(c + 1) * P], ones[0:8, 0:1],
                                     start=True, stop=True)
                last.then_inc(d_pe, 1)

            def head(h, odd):
                n = h.times(NP)
                first = not (h.c or h.L)
                rows = slice(HD * odd, HD * (odd + 1))
                pe.wait_ge(a_built, h.plus(1).v)
                if not first:
                    pe.wait_ge(a_lnd, h.v)
                pe.sem_inc(passed, 1)
                for b in range(NB):
                    last = turn(ps[0:HD + 2, b // 4, (b % 4) * P:(b % 4 + 1) * P], KA[:, b, :])
                last.then_inc(a_turned, 1)
                if not first:
                    pe.wait_ge(a_p, n.v)
                    pe.sem_inc(passed, 1)
                for b in range(NB):
                    last = turn(ps[0:HD + 2, 4 + b // 4, (b % 4) * P:(b % 4 + 1) * P], QA[:, b, :])
                last.then_inc(a_turned, 1)
                pe.wait_ge(a_q, h.plus(1).v)
                pe.wait_ge(a_k, h.plus(1).v)
                for p, (i, c, lo, w) in enumerate(query_pieces):
                    if p >= 2:
                        pe.wait_ge(a_max, n.plus(p - 1).v)
                    pe.sem_inc(passed, 1)
                    diag = lo + w == (i + 1) * P
                    o = ps[:, 4 + p % 2, 0:w]
                    last = pe.matmul(o, qT[:, i * P:(i + 1) * P], kT[:, lo:lo + w], start=True, stop=not diag)
                    if diag:
                        last = pe.matmul(o[:, w - P:w], identb[:, :], negb[:, :], start=False, stop=True)
                    last.then_inc(a_s, 1)
                    if not first and 2 <= p < 10:
                        sequence_values(h.plus(-1), p - 2)
                if not first:
                    sequence_sum(h.plus(-1))
                pe.wait_ge(a_shift, h.plus(1).v)
                pe.sem_inc(passed, 1)
                for b in range(NB):
                    last = turn(ps[0:HD + 2, b // 4, (b % 4) * P:(b % 4 + 1) * P], QA[:, b, :])
                last.then_inc(a_again, 1)
                if not first:
                    sequence_out(h.plus(-1))
                pe.wait_ge(a_q2, h.plus(1).v)

                def scores(p):
                    j, c, lo, w = key_pieces[p]
                    if p >= 2:
                        pe.wait_ge(a_p, n.plus(p - 1).v)
                    pe.sem_inc(passed, 1)
                    diag = lo == j * P
                    o = ps[:, 4 + p % 2, 0:w]
                    last = pe.matmul(o, kT[:, j * P:(j + 1) * P], qT[:, lo:lo + w], start=True, stop=not diag)
                    if diag:
                        last = pe.matmul(o[:, 0:P], negb[:, :], identb[:, :], start=False, stop=True)
                    last.then_inc(a_st, 1)

                scores(0)
                pe.wait_ge(vp_ready, h.half.plus(1).v if h.L else h.c // 2 + 1)
                if not odd and not first:
                    pe.wait_ge(a_pair, h.half.v)
                for p, (j, c, lo, w) in enumerate(key_pieces):
                    if p + 1 < NP:
                        scores(p + 1)
                    pe.wait_ge(a_p, n.plus(p + 1).v)
                    pe.sem_inc(passed, 1)
                    last = pe.matmul(ps[rows, 2 + c, lo - 512 * c:512], Vp[:, j, rows],
                                     PT[:, key_at[j] + lo - j * P:key_at[j] + lo - j * P + w],
                                     start=(j == 0), stop=(j == 4 * c + 3))
                last.then_inc(a_av, 1)
                sequence_peaks(h)
                pe.wait_ge(a_sum, h.plus(1).v)
                pe.sem_inc(passed, 1)
                for c in range(2):
                    last = pe.matmul(ps[rows, c, :], ones[:, 0:HD], Psum[:, 512 * c:512 * (c + 1)], start=True, stop=True)
                last.then_inc(a_den, 1)
                sequence_peak(h)

            def pair(p):
                for e in range(2):
                    head(p.times(2).plus(e), e)
            loop(pe, NH // 2, 1, pair, peel=1)
            for j in range(8):
                sequence_values(V(NS - 1), j)
            sequence_sum(V(NS - 1))
            sequence_out(V(NS - 1))
            out_proj(0)
            norm(1)
            mlp(0)

            norm(2)
            gemm_pair(V(U_IN[1]), V(T_IN[1]), h_ready, 2)
            loop(pe, 6, 4, lambda i: gemm(i.plus(U_IN[1] + 2), i.plus(T_IN[1] + 2)), peel=2)
            gemm(V(U_IN[1] + 8), V(T_IN[1] + 8))

            def values(i):
                gemm(i.plus(U_IN[1] + 9), i.plus(T_IN[1] + 9))
                to_tokens(i.plus(13))
            loop(pe, 8, 4, values)


            def two_tiles(h):
                for j in range(2):
                    gemm(h.times(2).plus(U_IN[1] + 17 + j), h.times(2).plus(T_IN[1] + 17 + j))
                pe.wait_ge(w_copied, h.plus(1).v)
                pe.sem_inc(passed, 1)
                for c in range(2):
                    last = pe.matmul(ps[:, 6 + c, :], wgh[:, :], tmp[:, 1, NS + 512 * c:NS + 512 * (c + 1)],
                                     start=True, stop=True)
                last.then_inc(z_summed, 1)
            loop(pe, NG, 2, two_tiles)

            all_read(pe, T_IN[1] + 25)
            for i in range(12):
                last = turn(ps[0:NS, i // 4, (i % 4) * P:(i % 4 + 1) * P],
                            qk1[:, 2 * i + 1, 0:NS] if i < 4 else vs_f[:, i - 4, :])
            last.then_inc(s_turned, 1)
            for h in range(NG):
                last = pe.matmul(ps[:, 3, NS * h:NS * (h + 1)], wgk[:, h * DK:(h + 1) * DK], tmp[:, 1, 0:NS],
                                 start=True, stop=True)
            last.then_inc(zs_summed, 1)
            pe.wait_ge(s_kv, 1)
            pe.wait_ge(zs_folded, 1)

            def gla_head(h):
                pe.wait_ge(g_dve, h.plus(1).v)
                pe.sem_inc(passed, 1)
                n = h.times(NB)
                first = not (h.c or h.L)

                def scores(b):
                    cols = slice(NS + b * P, NS + (b + 1) * P)
                    pe.matmul(ps[:, 0, 0:P], ke[:, cols], qe[:, cols], start=True, stop=True).then_inc(gb_a, 1)
                    turn(ps[:, 1, 0:P], bcum[:, cols]).then_inc(gb_a, 1)

                def turned(b):
                    m = n.plus(b)
                    pe.wait_ge(gb_out, m.plus(1).v)
                    if b or not first:
                        pe.wait_ge(g_trk, m.v)
                    pe.sem_inc(passed, 1)
                    for e in range(2):
                        last = turn(ps[:, 6, e * P:(e + 1) * P],
                                    tmp[:, 0, DV * (b % 2) + e * P:DV * (b % 2) + (e + 1) * P])
                    last.then_inc(g_tr, 1)

                scores(0)
                for b in range(NB):
                    m = n.plus(b)
                    pe.wait_ge(gb_scores, m.plus(1).v)
                    pe.wait_ge(gb_kd, m.plus(1).v)
                    pe.sem_inc(passed, 1)
                    if b + 1 < NB:
                        scores(b + 1)
                    if b == 0:
                        pe.wait_ge(s_masks, h.plus(1).v)
                    if b or not first:
                        pe.wait_ge(s_added, h.times(NS).plus(b).v)
                    pe.sem_inc(passed, 1)
                    pe.matmul(ps[:, 7, 0:DV], kmask[:, b, :], kvnat[:, ds(h.times(DV).plus(NG * DK).v, DV)],
                              start=True, stop=True).then_inc(s_outer, 1)
                    v = Vo[:, b, ds(h.times(DV).v, DV)]
                    if b >= 2 or not first:
                        pe.wait_ge(gb_out, m.plus(-1).v)
                    O = ps[:, 2 + b % 2, 0:DV]
                    pe.matmul(O, aT[:, b % 2, :], v, start=True, stop=False, skip_group_check=True)
                    state = h.times(2 * NB + 1).plus(2 * b + 1)
                    pe.matmul(ps[:, 4, 0:DV], kdn[:, b % 2, 0, :], v, start=True, stop=True).then_inc(gb_kv, 1)
                    pe.wait_ge(gb_state, state.v)
                    pe.matmul(ps[:, 5, 0:DV], kdn[:, b % 2, 1, :], v, start=True, stop=True).then_inc(gb_kv, 1)
                    for c in range(2):
                        half = slice(CHUNK * c, CHUNK * (c + 1))
                        if c:
                            if b:
                                turned(b - 1)
                            pe.wait_ge(gb_state, state.plus(1).v)
                        pe.matmul(O[half, :], qe[:, NS + b * P + CHUNK * c:NS + b * P + CHUNK * (c + 1)], S[:, :],
                                  start=False, stop=(c == 1), skip_group_check=True).then_inc(gb_inter, 1)
                    pe.wait_ge(s_new, h.times(NS).plus(b + 1).v)
                    pe.sem_inc(passed, 1)
                    pe.matmul(ps[0:NS, 7, DV:2 * DV], qmask[:, b, :], sout[:, b, :], start=True, stop=True
                              ).then_inc(s_out, 1)
                turned(NB - 1)
            loop(pe, NG, 1, gla_head, peel=1)
            pe.wait_ge(s_scaled, 1)
            for k in range(KT):
                last = turn(ps[:, 6, NS * k:NS * (k + 1)], osn[:, k * P:(k + 1) * P])
            last.then_inc(s_turned, 1)
            out_proj(1)
            norm(3)
            mlp(1)
            all_read(pe, T_MLP[1] + 160)
            for b in range(NB + 1):
                if b >= 2:
                    pe.wait_ge(y_kept, b - 1)
                for k in range(KT):
                    if b < NB:
                        last = turn(ps[:, 2 * (b % 2) + k // 4, (k % 4) * P:(k % 4 + 1) * P],
                                    xT[:, k, NS + b * P:NS + (b + 1) * P])
                    else:
                        last = turn(ps[0:NS, 2 * (b % 2) + k // 4, (k % 4) * P:(k % 4 + 1) * P], xT[:, k, 0:NS])
                last.then_inc(y_turned, 1)

        @block.scalar
        def _(act):
            link = Link(act, act_link)

            def rsqrt(out, in_, n, sem, read=None, read_count=None):
                if read is None:
                    link(act.activation(out, in_, ACT.Ln, bias=eps[0:out.shape[0], 0:1], scale=1.0 / n))
                else:
                    act.activation(out, in_, ACT.Ln, bias=eps[0:out.shape[0], 0:1], scale=1.0 / n).then_inc(read, 1)
                    act.wait_ge(read, read_count)
                act.activation(out, out, ACT.Exp, scale=-0.5).then_inc(sem, 1)

            def squares(n, last_tiles=None):
                for k in range(KT):
                    if last_tiles is not None:
                        t = V(last_tiles + k)
                        act.wait_ge(acc_free[t.par], t.half.plus(1).v)
                    if k >= 3:
                        act.wait_ge(sq_added, (KT - 1) * n + k - 2)
                    act.activation(tmp[:, k % 2, :] if k else sqsum[:, :], xT[:, k, :], ACT.Square).then_inc(sq_ready, 1)

            def one_over_rms(n):
                t = V(T_NORM[n])
                act.wait_ge(sq_summed, n + 1)
                rsqrt(thirds(rstd[:, :]), acc(t.par), D, rstd_ready, acc_free[t.par], t.half.plus(1).v)

            def modulated(n):
                l, w = n // 2, n % 2
                for k in range(KT):
                    act.wait_ge(norm_scaled, KT * n + k + 1)
                    link(act.activation(tmp[:, k % 2, NS:T], tmp[:, k % 2, NS:T], ACT.Identity,
                                        bias=modT[:, l, 24 * w + k, NS:NC], scale=gain[:, n, k, NS:NC]))
                    act.wait_ge(norm_affine, KT * n + k + 1)
                    act.activation(hh[:, k, :], tmp[:, k % 2, :], ACT.Copy).then_inc(norm_hi, 1)

            def residual_out():
                act.dma_start(xstore.rearrange("p (k n) -> p k n", k=KT), xT[:, :, :]).then_inc(x_spilled, 16)

            def norm(n, last_tiles):
                squares(n, last_tiles)
                if n == 2:
                    residual_out()
                one_over_rms(n)
                modulated(n)

            def token_tile(i, t, nn, keep):
                act.wait_ge(acc_done, done(t, nn))
                if i.c >= 2 or i.L:
                    act.wait_ge(nat_done, i.plus(-1).v)
                act.activation(thirds(tmp[:, i.c % 2, :]), acc(t.par), ACT.Copy).then_inc(tmp_full, 1)
                act.activation(keep, ps[:, 3 * t.par, 0:NS], ACT.Copy).then_inc(acc_free[t.par], 1)

            def mlp(l):
                t0, nn = T_MLP[l], 2 * l + 2

                def up(i, t):
                    for j in range(2):
                        q = i.times(2).plus(2 * NPAIR * l + j)
                        act.wait_ge(acc_done, done(t.plus(j), nn))
                        if q.c >= 2 or q.L:
                            act.wait_ge(hid_ready, q.plus(-1).v)
                        tt = t.plus(j)
                        act.activation(thirds(tmp[:, j, :]), acc(tt.par), ACT.Relu).then_inc(acc_free[tt.par], 1)
                        act.wait_ge(hid_squared, q.plus(1).v)
                        act.activation(hid[0][:, i.c % 2, j, :], tmp[:, j, :], ACT.Copy).then_inc(hid_hi_ready, 1)
                up(V(0), V(t0))
                loop(act, NPAIR - 1, 2, lambda i: up(i.plus(1), i.times(10).plus(t0 + 2)), peel=1)

            act.wait_ge(small_loaded, 16 * SMALL)
            act.activation(c9e[:, :], c9[:, :], ACT.Exp, scale=-1.0).then_inc(silu_pos, 1)
            for k in range(KT):
                act.wait_ge(xt_done, k + 1)
                act.activation(xT[:, k, NS:T].rearrange("p (a n) -> p a n", a=2),
                               ps[:, 2 + 2 * (k % 2):4 + 2 * (k % 2), :], ACT.Copy).then_inc(xt_kept, 1)
            act.wait_ge(xt_kept, KT)

            def modulation(g):
                if g.c or g.L:
                    act.wait_ge(mod_turned, g.v)
                for j in range(4):
                    act.wait_ge(ada_done, g.times(4).plus(j + 1).v)
                    act.activation(modrow[32 * j:32 * j + NC, :], ps[32 * j:32 * j + NC, 6 + j % 2, :], ACT.Copy
                                   ).then_inc(mod_rows, 1)
            act.wait_ge(setup_dve, 1)
            squares(0)
            modulation(V(0))
            one_over_rms(0)
            loop(act, 5, 1, lambda g: modulation(g.plus(1)))
            residual_out()
            act.wait_ge(setup_dve, 4)
            modulated(0)

            loop(act, 12, 2, lambda i: token_tile(i, i.plus(T_IN[0]), 1, sF[:, ds(i.v, 1), :].rearrange("p a n -> p (a n)")), peel=2)

            def conv(c):
                t = c.times(3).plus(T_IN[0] + 12)
                act.wait_ge(acc_done, done(t, 1))
                if c.c < 2 and not c.L:
                    act.wait_ge(nat_done, 12)
                else:
                    u = c.times(3).plus(T_IN[0] + 12 - 6 + 1)
                    act.wait_ge(acc_free[u.par], u.half.plus(1).v)
                act.activation(thirds(tmp[:, c.c % 2, :]), acc(t.par), ACT.Copy).then_inc(acc_free[t.par], 1)
                for j in range(2):
                    act.wait_ge(qk_summed, c.times(2).plus(j + 1).v)
                    rsqrt(rsq[:, j, :], rsq[:, j, :], HD, qk_rs)
            loop(act, 4, 2, conv, link, 2, peel=2)
            all_read(act, T_IN[0] + 12 + 3 * 3 + 2)
            token_tile(V(12), V(T_IN[0] + 24), 1, sF[:, 12, :])
            act.wait_ge(prep_dve, 1)
            act.activation(sq8[:, :, :], sNat[:, 0:2, :], ACT.Square).then_inc(prep_act, 1)
            act.wait_ge(prep_dve, 3)
            link(act.activation(lft[:, :, :], lft[:, :, :], ACT.Exp))
            act.activation(lft[:, :, :], lft[:, :, :], ACT.Ln, bias=1.0).then_inc(prep_act, 1)
            act.wait_ge(prep_dve, 4)
            rsqrt(rsq8[:, :], rsq8[:, :], HD, prep_act)

            def sequence(b):
                act.wait_ge(d_dve, b.times(6).plus(2 + 3).v)
                act.activation(PBx[:, :, :], PBx[:, :, :], ACT.Exp).then_inc(d_act, 1)

            def head(h, odd):
                n = h.times(NP)
                first = not (h.c or h.L)
                rows = slice(HD * odd, HD * (odd + 1))
                if not first:
                    sequence(h.plus(-1))
                act.wait_ge(a_turned, h.times(2).plus(2).v)
                act.activation(qT[:, :].rearrange("p (a n) -> p a n", a=2), ps[0:HD + 2, 4:6, :], ACT.Copy).then_inc(a_q, 1)
                act.wait_ge(a_again, h.plus(1).v)
                act.activation(qT[HD:HD + 2, :].rearrange("p (a n) -> p a n", a=2), ps[HD:HD + 2, 0:2, :], ACT.Copy
                               ).then_inc(a_q2, 1)
                if not first:
                    act.wait_ge(a_av, h.v)
                    act.wait_ge(a_sum, h.v)
                for p, (j, c, lo, w) in enumerate(key_pieces):
                    act.wait_ge(a_st, n.plus(p + 1).v)
                    o = key_at[j] + lo - j * P
                    act.activation(PT[:, o:o + w], ps[:, 4 + p % 2, 0:w], ACT.Exp).then_inc(a_p, 1)
                act.wait_ge(a_den, h.plus(1).v)
                if not odd and not first:
                    act.wait_ge(a_pair, h.half.v)
                act.activation(rden[rows, :].rearrange("p (a n) -> p a n", a=2), ps[rows, 0:2, :], ACT.Ln).then_inc(a_lnd, 1)

            def pair(p):
                for e in range(2):
                    head(p.times(2).plus(e), e)
                act.wait_ge(a_lnd, p.times(2).plus(2).v)
                act.activation(rden[:, :], rden[:, :], ACT.Exp, scale=-1.0).then_inc(a_rden, 1)
            loop(act, NH // 2, 1, pair, peel=1)
            sequence(V(NS - 1))
            act.wait_ge(a_pair, NH // 2)
            act.wait_ge(d_dve, 2 + 6 * NS)
            for k in range(4):
                act.activation(hh[:, k, :], ya[:, k, :], ACT.Copy).then_inc(y_hi, 1)
            act.activation(hh[:, 4:8, 0:NS], ysam[:, :, :], ACT.Copy).then_inc(y_hi, 1)
            for c in range(4):
                act.activation(hh[:, 4 + c, NS:T].rearrange("p (b n) -> p b n", n=P), QK[:, 0, :, c * P:(c + 1) * P],
                               ACT.Copy).then_inc(y_hi, 1)
            norm(1, T_OUT[0])
            mlp(0)

            norm(2, T_MLP[0] + 152)

            def query_or_key(i, k):
                t = i.plus(T_IN[1] + 4 * k)
                act.wait_ge(acc_done, done(t, 3))
                if not k and not i.c and not i.L:
                    act.wait_ge(x_spilled, 32)
                act.activation(qk1[:, ds(i.times(2).plus(k).v, 1), :].rearrange("p o (c n) -> p (o c) n", c=3),
                               acc(t.par), ACT.Copy).then_inc(acc_free[t.par], 1)
            for k in range(2):
                loop(act, 4, 2, lambda i: query_or_key(i, k), peel=2 if k == 0 else 0)
            loop(act, 8, 2, lambda i: token_tile(i.plus(13), i.plus(T_IN[1] + 8), 3,
                                                 vs_f[:, ds(i.v, 1), :].rearrange("p a n -> p (a n)")))
            t = V(T_IN[1] + 16)
            act.wait_ge(acc_done, done(t, 3))
            act.wait_ge(nat_done, 21)
            act.activation(thirds(tmp[:, 1, :]), acc(t.par), ACT.Copy).then_inc(acc_free[t.par], 1)

            def gate(f):
                t = f.plus(T_IN[1] + 17)
                act.wait_ge(acc_done, done(t, 3))
                if f.c >= 2 or f.L:
                    act.wait_ge(r_stored[f.par], f.half.times(16).v)
                r = (qe, ke)[f.c % 2][:, :]
                link(act.activation(thirds(r), acc(t.par), ACT.Exp, scale=-1.0))
                link(act.activation(r, r, ACT.Ln, bias=1.0))
                act.activation(r, r, ACT.Exp, scale=-1.0).then_inc(r_exp, 1)
                act.wait_ge(acc_free[t.par], t.half.plus(1).v)
                act.dma_start(rstore[:, ds(f.times(T).v, T)], r).then_inc(r_stored[f.par], 16)

            def two_tiles(h):
                for j in range(2):
                    gate(h.times(2).plus(j))
                act.wait_ge(z_folded, h.plus(1).v)
                r = tmp[:, 0, NS:T]
                link(act.activation(r, r, ACT.Exp))
                act.activation(r, r, ACT.Ln, bias=1.0).then_inc(z_logs, 1)
                act.wait_ge(z_scanned, h.plus(1).v)
                act.dma_start(bstore[:, ds(h.times(SEQ).v, SEQ)], r).then_inc(z_stored, 16)
            loop(act, NG, 1, two_tiles, link, 5, peel=1)
            act.wait_ge(zs_folded, 1)
            link(act.activation(dec_s[:, :, :], dec_s[:, :, :], ACT.Exp))
            act.activation(dec_s[:, :, :], dec_s[:, :, :], ACT.Ln, bias=1.0).then_inc(zs_logs, 1)
            act.wait_ge(zs_ready, 1)
            act.activation(dec_s[:, :, :], zs[:, :, :], ACT.Exp, scale=1.0 / TAU).then_inc(dec_s_ready, 1)

            def gla_head(h):
                act.wait_ge(b_in, h.times(16).plus(16).v)
                if h.c or h.L:
                    act.wait_ge(g_tr, h.times(NB).v)
                act.sem_inc(passed, 1)
                act.activation(qe[:, NS:T], draw, ACT.Exp, scale=1.0 / TAU).then_inc(g_act, 1)
                act.activation(dec[:, :], draw.rearrange("p (c r) -> p c r", r=CHUNK)[:, :, CHUNK - 1], ACT.Exp,
                               scale=1.0 / TAU)
                act.activation(ke[:, NS:T], draw, ACT.Exp, scale=-1.0 / TAU).then_inc(b_used, 1)
                act.wait_ge(g_diff, h.plus(1).v)
                act.activation(bcum[:, NS:T], bcum[:, NS:T], ACT.Exp, scale=1.0 / TAU).then_inc(g_act, 1)
                first = not (h.c or h.L)

                def keys(b):
                    m = h.times(NB).plus(b)
                    act.wait_ge(gb_a, m.times(2).plus(2).v)
                    if b >= 2 or not first:
                        act.wait_ge(gb_kv, m.times(2).plus(-2).v)
                    act.activation(kdn[0:CHUNK, b % 2, 0, :], ps[0:CHUNK, 1, 0:P], ACT.Copy)
                    act.activation(kdn[CHUNK:P, b % 2, 1, :], ps[CHUNK:P, 1, 0:P], ACT.Copy).then_inc(gb_kd, 1)

                keys(0)
                for b in range(NB):
                    m = h.times(NB).plus(b)
                    if b + 1 < NB:
                        keys(b + 1)
                    act.wait_ge(gb_inter, m.times(2).plus(2).v)
                    if b >= 2 or not first:
                        act.wait_ge(gb_out, m.plus(-1).v)
                    link(act.activation(tmp[:, 0, 2 * DV:3 * DV], ps[:, 2 + b % 2, 0:DV], ACT.Square,
                                        accum_out=ss1[:, b % 2, 0:1]))
                    act.activation(ss1[:, b % 2, 1:2], ss1[:, b % 2, 0:1], ACT.Sqrt, bias=eps[:, 0:1], scale=1.0 / DV
                                   ).then_inc(gb_rs, 1)
                act.wait_ge(gb_state, h.times(2 * NB + 1).plus(2 * NB + 1).v)
                act.dma_start(gla_prompt[0, 0, ds(h.v, 1)].rearrange("o k v -> (o k) v"), S[:, :]).then_inc(g_stored, 16)
            loop(act, NG, 1, gla_head, link, NB, peel=1)

            act.wait_ge(s_squares, 1)
            rsqrt(ss8[:, :], ss8[:, :], DV, s_rs)
            act.wait_ge(y_s, 1)
            act.wait_ge(gla_stored, 16 * NG)
            act.wait_ge(g_stored, 16 * NG)
            for k in range(KT):
                act.activation(hh[:, k, :], qk1[:, k, :], ACT.Copy).then_inc(y_hi, 1)
            norm(3, T_OUT[1])
            mlp(1)

        @block.vector
        def _(dve):
            link = Link(dve, dve_link)
            tt, stt = dve.tensor_tensor, dve.scalar_tensor_tensor

            def add_square(n, k):
                dve.wait_ge(sq_ready, KT * n + k + 1)
                tt(sqsum[:, :], sqsum[:, :], tmp[:, k % 2, :], ALU.add).then_inc(sq_added, 1)
                dve.wait_ge(sq_added, (KT - 1) * n + k)

            def norm(n):
                l, w = n // 2, n % 2
                if n:
                    add_square(n, KT - 1)
                dve.wait_ge(rstd_ready, n + 1)

                def low(k):
                    dve.wait_ge(norm_hi, KT * n + k + 1)
                    tt(hl[:, k, :], tmp[:, k % 2, :], hh[:, k, :].bitcast(F32), ALU.subtract).then_inc(h_ready, 1)
                for k in range(KT):
                    if k >= 2:
                        dve.wait_ge(h_ready, KT * n + k - 1)
                    tt(tmp[:, k % 2, :], xT[:, k, :], rstd[:, :], ALU.mult).then_inc(norm_scaled, 1)
                    dve.wait_ge(norm_scaled, KT * n + k + 1)
                    link(tt(tmp[:, k % 2, 0:NS], tmp[:, k % 2, 0:NS], gain[:, n, k, 0:NS], ALU.mult))
                    tt(tmp[:, k % 2, 0:NS], tmp[:, k % 2, 0:NS], modT[:, l, 24 * w + k, 0:NS], ALU.add
                       ).then_inc(norm_affine, 1)
                    if k:
                        low(k - 1)
                low(KT - 1)

            def token_tile(i, dst):
                dve.wait_ge(nat_done, i.plus(1).v)
                dve.tensor_copy(dst, ps[:, 6:8, :].rearrange("p a (b n) -> p (a b) n", n=P)).then_inc(nat_kept, 1)

            def residual(t, nn, f, l, comp):
                dve.wait_ge(acc_done, done(t, nn))
                m = KT * comp + f
                s = 3 * t.par
                link(tt(t8[:, :], ps[:, s, 0:NS], modT[:, l, m, 0:NS], ALU.mult))
                tt(xT[:, f, 0:NS], xT[:, f, 0:NS], t8[:, :], ALU.add)
                stt(out=xT[:, f, NS:CH], in0=ps[:, s, NS:CH], scalar=modT[:, l, m, NS:NC], in1=xT[:, f, NS:CH],
                    op0=ALU.mult, op1=ALU.add)
                x2 = xT[:, f, CH:T].rearrange("p (c n) -> p c n", c=2)
                stt(out=x2, in0=ps[:, s + 1:s + 3, 0:CH], scalar=modT[:, l, m, NS:NC], in1=x2,
                    op0=ALU.mult, op1=ALU.add).then_inc(acc_free[t.par], 1)
                dve.wait_ge(acc_free[t.par], t.half.plus(1).v)

            def out_proj(l):
                dve.wait_ge(x_back, 16 * (l + 1))
                for f in range(KT):
                    residual(V(T_OUT[l] + f), 2 * l + 1, f, l, 2)
                    if f >= 2:
                        add_square(2 * l + 1, f - 1)

            def mlp(l):
                t0, nn = T_MLP[l], 2 * l + 2

                def square(i, t, j):
                    tj = t.plus(j)
                    dve.wait_ge(acc_free[tj.par], tj.half.plus(1).v)
                    tt(tmp[:, j, :], tmp[:, j, :], tmp[:, j, :], ALU.mult).then_inc(hid_squared, 1)

                def low(i, j):
                    q = i.times(2).plus(2 * NPAIR * l + j)
                    dve.wait_ge(hid_hi_ready, q.plus(1).v)
                    tt(hid[1][:, i.c % 2, j, :], tmp[:, j, :], hid[0][:, i.c % 2, j, :].bitcast(F32), ALU.subtract
                       ).then_inc(hid_ready, 1)

                def up(i, t):
                    square(i, t, 0)
                    low(i, 0)
                    square(i, t, 1)

                def down(i, t, last=False):
                    for f in range(KT):
                        residual(t.plus(f), nn, f, l, 5)
                        if f == 0 and not last:
                            low(i.plus(1), 1)
                        if last and l < DEPTH - 1 and f >= 2:
                            add_square(2, f - 1)

                def step(i):
                    up(i.plus(1), i.times(10).plus(t0 + 2))
                    down(i, i.times(10).plus(t0 + 4))
                up(V(0), V(t0))
                low(V(0), 1)
                loop(dve, NPAIR - 1, 2, step, link, KT, peel=1)
                down(V(NPAIR - 1), V(t0 + 152), last=True)

            dve.memset(modrow[:, :], 0.0)
            dve.wait_ge(consts_made, 1)
            dve.wait_ge(setup_pe, 1)
            dve.tensor_copy(vecT[:, :], ps[:, 0, 0:144])
            dve.tensor_copy(prevT[:, :, :], ps[:, 0, 256:320].rearrange("p (c n) -> p c n", c=4))
            dve.tensor_copy(xT[:, :, 0:NS], ps[:, 1, 0:NS * KT].rearrange("p (k n) -> p k n", k=KT)).then_inc(setup_dve, 1)
            link(dve.tensor_scalar(gqb[:, :], gqb[:, :], HD ** -0.5, None, ALU.mult))
            dve.wait_ge(silu_pos, 1)
            link(dve.tensor_scalar(c9e[:, :], c9e[:, :], 1.0, None, ALU.add))
            link(dve.reciprocal(c9e[:, :], c9e[:, :]))
            tt(c9[:, :], c9[:, :], c9e[:, :], ALU.mult).then_inc(setup_dve, 1)
            dve.wait_ge(setup_pe, 2)
            dve.tensor_copy(scT[:, :, :], ps[:, 1, P:P + NC * KT].rearrange("p (k n) -> p k n", k=KT)).then_inc(setup_dve, 1)
            modA = modT[:, :, :, :].rearrange("p l n c -> p (l n) c")

            def modulation(g):
                dve.wait_ge(mod_turned, g.plus(1).v)
                n = g.times(16).v
                tt(modA[:, ds(n, 16), :].rearrange("p (j f) c -> p j f c", f=4),
                   ps[:, 4, :].rearrange("p (f j r) -> p j f r", j=4, r=32)[:, :, :, 0:NC],
                   vecT[:, ds(n, 16)].rearrange("p (j f) -> p j f", f=4).unsqueeze(3).to_broadcast([P, 4, 4, NC]),
                   ALU.add).then_inc(ada_kept, 1)
            for k in range(1, KT):
                add_square(0, k)
            loop(dve, 6, 1, modulation)
            dve.wait_ge(ada_kept, 6)
            for n in range(4):
                l, w = n // 2, n % 2
                last = stt(out=gain[:, n, :, :], in0=modT[:, l, 24 * w + 8:24 * w + 16, :], scalar=1.0,
                           in1=vecT[:, 96 + 16 * w + 8 * l:104 + 16 * w + 8 * l].unsqueeze(2).to_broadcast([P, KT, NC]),
                           op0=ALU.add, op1=ALU.mult)
            last.then_inc(setup_dve, 1)
            dve.wait_ge(setup_dve, 4)
            norm(0)

            dve.wait_ge(x_spilled, 16)
            for j in range(2):
                loop(dve, 4, 2, lambda i: token_tile(i.plus(4 * j), QK[:, j, :, ds(i.times(P).v, P)]))
            loop(dve, 4, 2, lambda i: token_tile(i.plus(8), Vn[:, :, ds(i.times(P).v, P)]))

            def conv(c):
                t = c.times(3).plus(T_IN[0] + 12)
                m = c.c % 2
                dve.wait_ge(acc_free[t.par], t.half.plus(1).v)
                t = t.plus(1)
                dve.wait_ge(acc_done, done(t, 1))
                s = 3 * t.par
                tt(U[:, 0:NS], ps[:, s, 0:NS], tmp[:, m, 0:NS], ALU.mult)
                tt(U[:, NS + 2:CH + 2], ps[:, s, NS:CH], tmp[:, m, NS:CH], ALU.mult)
                tt(U[:, CH + 2:T + 2].rearrange("p (c n) -> p c n", c=2), ps[:, s + 1:s + 3, 0:CH],
                   tmp[:, m, CH:T].rearrange("p (c n) -> p c n", c=2), ALU.mult).then_inc(acc_free[t.par], 1)
                dve.wait_ge(acc_free[t.par], t.half.plus(1).v)
                w = [vecT[:, ds(c.plus(P + 4 * j).v, 1)] for j in range(3)]
                y = ya[:, ds(c.v, 1), :].rearrange("p o n -> p (o n)")
                link(dve.tensor_scalar(y[:, NS:T], U[:, NS + 2:T + 2], w[2], None, ALU.mult))
                link(stt(out=y[:, NS:T], in0=U[:, NS + 1:T + 1], scalar=w[1], in1=y[:, NS:T], op0=ALU.mult, op1=ALU.add))
                link(stt(out=y[:, NS:T], in0=U[:, NS:T], scalar=w[0], in1=y[:, NS:T], op0=ALU.mult, op1=ALU.add))
                prev = prevT[:, ds(c.v, 1), :].rearrange("p o (b j) -> p (o b) j", j=2)
                link(dve.tensor_scalar(y[:, 0:NS], U[:, 0:NS], w[2], None, ALU.mult))
                for j in (1, 0):
                    link(stt(out=y[:, 0:NS], in0=prev[:, :, j], scalar=w[j], in1=y[:, 0:NS], op0=ALU.mult, op1=ALU.add))
                dve.tensor_copy(uOut[:, ds(c.v, 1), 0:NS].rearrange("p o n -> p (o n)"), U[:, 0:NS])
                dve.tensor_copy(uOut[:, ds(c.v, 1), NS:10].rearrange("p o n -> p (o n)"), U[:, T:T + 2])
                t = t.plus(1)
                dve.wait_ge(acc_done, done(t, 1))
                tt(thirds(y), thirds(y), acc(t.par), ALU.mult).then_inc(acc_free[t.par], 1)
                dve.wait_ge(acc_free[t.par], t.half.plus(1).v)
                q = [QK[:, j, :, ds(c.times(P).v, P)] for j in range(2)]
                for j in range(2):
                    link(tt(sqs[:, :, :], q[j], q[j], ALU.mult))
                    dve.tensor_reduce(rsq[:, j, :], sqs[:, :, :].rearrange("p b (h d) -> p (b h) d", d=HD), X, ALU.add
                                      ).then_inc(qk_summed, 1)
                    dve.wait_ge(qk_summed, c.times(2).plus(j + 1).v)
                for j, g in ((0, gqb), (1, gkb)):
                    heads = q[j].rearrange("p b (h d) -> p b h d", d=HD)
                    dve.wait_ge(qk_rs, c.times(2).plus(j + 1).v)
                    link(tt(heads, heads, rsq[:, j, :].rearrange("p (b h) -> p b h", h=2).unsqueeze(3).to_broadcast([P, NB, 2, HD]),
                            ALU.mult))
                    for e in range(2):
                        last = tt(heads[:, :, e, :], heads[:, :, e, :], g[:, :].unsqueeze(1).to_broadcast([P, NB, HD]), ALU.mult)
                        last.then_inc(qk_scaled, 1)
            dve.wait_ge(setup_pe, 2)
            link(dve.memset(U[:, NS:NS + 2], 0.0))
            dve.wait_ge(nat_kept, 12)
            loop(dve, 4, 2, conv, link, 10)
            dve.wait_ge(qk_scaled, 2 * NB)

            link(dve.memset(lf[:, :, :], 0.0))
            dve.wait_ge(nat_done, 13)
            tt(lf[:, 0:NB, :], ps[:, 6:8, :].rearrange("p a (b n) -> p (a b) n", n=P)[:, :, P - NH:P],
               bfb[:, :].unsqueeze(1).to_broadcast([P, NB, NH]), ALU.add).then_inc(nat_kept, 1)
            dve.wait_ge(prep_pe, 1)
            dve.tensor_copy(sNat[:, :, :], ps[0:NS, 0:3, :]).then_inc(prep_dve, 1)
            tt(lf[0:NS, NB, :], ps[0:NS, 3, P - NH:P], bfb[0:NS, :], ALU.add)
            dve.tensor_copy(crow[:, :], ps[0:10, 4, :]).then_inc(prep_dve, 1)
            dve.wait_ge(prep_dve, 2)
            stt(out=lft[:, :, :], in0=lf[:, :, :], scalar=-1.0, in1=lf[:, :, :], op0=ALU.mult, op1=ALU.min
                ).then_inc(prep_dve, 1)
            dve.wait_ge(prep_act, 1)
            dve.tensor_reduce(rsq8[:, :], sq8[:, :, :].rearrange("p j (h d) -> p (j h) d", d=HD), X, ALU.add
                              ).then_inc(prep_dve, 1)
            dve.wait_ge(prep_act, 2)
            stt(out=lf[:, :, :], in0=lf[:, :, :], scalar=0.0, in1=lft[:, :, :], op0=ALU.min, op1=ALU.subtract
                ).then_inc(prep_dve, 1)
            dve.wait_ge(prep_act, 3)
            rs8 = rsq8[:, :].rearrange("p (j g) -> p j g", j=2)
            for j, g in ((0, gqb), (1, gkb)):
                s = sNat[:, j, :].rearrange("p (h d) -> p h d", d=HD)
                link(tt(s, s, rs8[:, j, :].unsqueeze(2).to_broadcast([NS, NH, HD]), ALU.mult))
                link(tt(s, s, g[0:NS, :].unsqueeze(1).to_broadcast([NS, NH, HD]), ALU.mult))
            tt(sq8[:, 0, :], sNat[:, 0, :], sNat[:, 1, :], ALU.mult).then_inc(prep_dve, 1)
            dve.wait_ge(prep_dve, 6)
            dve.tensor_reduce(snew[:, :], sq8[:, 0, :].rearrange("p (h d) -> p h d", d=HD), X, ALU.add)
            dve.wait_ge(prep_pe, 2)
            link(dve.tensor_copy(fcum[:, :, :], ps[:, 5, 0:NB * NH].rearrange("p (b h) -> p b h", h=NH)))
            dve.memset(QA[:, :, HD + 1:HD + 2], 1.0)
            dve.memset(KA[:, :, HD:HD + 1], 1.0)

            dve.wait_ge(d_pe, 1)
            dve.tensor_copy(LT[:, :, :], ps[:, 2:4, :].rearrange("p a (h n) -> p (a h) n", n=P))
            link(dve.tensor_reduce(ptot[:, :], Lraw[:, :, :].rearrange("p s h -> p h s"), X, ALU.add))
            tt(TB[:, :, :], ptot[:, :].unsqueeze(2).to_broadcast([P, NH, P]),
               ones[:, :].unsqueeze(1).to_broadcast([P, NH, P]), ALU.mult)
            tt(LN[:, :, :], lf[0:NS, NB, :].unsqueeze(2).to_broadcast([NS, NH, P]),
               ones[0:NS, :].unsqueeze(1).to_broadcast([NS, NH, P]), ALU.mult).then_inc(d_dve, 1)
            dve.wait_ge(d_pe, 2)
            link(dve.memset(sc[:, PAGES, :], NEG))
            link(dve.memset(peaks[:, :, :], NEG))
            dve.tensor_copy(Lsuf[:, :, :], ps[:, 6:8, :].rearrange("p a (h n) -> p (a h) n", n=P)).then_inc(d_dve, 1)

            dve.wait_ge(kv_out, 16 * 9)

            def sequence_scores(b):
                dve.wait_ge(qbc_in, b.times(16).plus(16).v)
                for j in range(8):
                    dve.wait_ge(pages_in[j], b.times(64).plus(32).v)
                    kk = pages[:, j, :, :]
                    link(tt(kk, kk, qbc[:, :].unsqueeze(1).to_broadcast([P, 2, 512]), ALU.mult))
                    dve.tensor_reduce(sc[:, 2 * j:2 * j + 2, :], kk.rearrange("p g (h d) -> p g h d", d=HD), X, ALU.add
                                      ).then_inc(k_used, 1)
                dve.wait_ge(k_used, b.times(8).plus(8).v)
                s16 = sc[:, 0:PAGES, :]
                tt(s16, s16, Lsuf[:, :, ds(b.times(PAGES).v, PAGES)].rearrange("p h g -> p g h"), ALU.add)
                link(dve.tensor_scalar(sc[0:NS, PAGES, :], snew[:, :], only8[:, ds(b.v, 1)], None, ALU.add))
                dve.tensor_reduce(mx8[:, :], sc[:, :, :].rearrange("p g h -> p h g"), X, ALU.max).then_inc(d_dve, 1)
                dve.wait_ge(d_pe, b.times(4).plus(2 + 1).v)
                link(dve.tensor_reduce(small[0:8, 0:1], ps[0:8, 7, 0:P], X, ALU.max))
                dve.tensor_scalar(small[0:8, 8:16], ident[0:8, 0:8], small[0:8, 0:1], None, ALU.mult).then_inc(d_dve, 1)
                dve.wait_ge(d_pe, b.times(4).plus(2 + 2).v)
                tt(PBx[:, :, :], sc[:, :, :], ps[:, 7, 128:136].unsqueeze(1).to_broadcast([P, PAGES + 1, NH]), ALU.subtract
                   ).then_inc(d_dve, 1)
                dve.wait_ge(d_dve, b.times(6).plus(2 + 3).v)

            def sequence_sums(b):
                dve.wait_ge(d_act, b.plus(1).v)
                dve.tensor_reduce(small[:, 16:24], PBx[:, :, :].rearrange("p g h -> p h g"), X, ALU.add).then_inc(d_dve, 1)
                dve.wait_ge(d_dve, b.times(6).plus(2 + 4).v)

            def sequence_scaled(b):
                dve.wait_ge(d_pe, b.times(4).plus(2 + 3).v)
                link(dve.reciprocal(small[0:8, 1:2], ps[0:8, 7, 144:145]))
                stt(out=omask, in0=ps[0:8, 6, :], scalar=small[0:8, 1:2],
                    in1=headrow[:, :, :].rearrange("p h d -> p (h d)"), op0=ALU.mult, op1=ALU.mult).then_inc(d_dve, 1)

            def sequence_out(b):
                dve.wait_ge(d_pe, b.times(4).plus(2 + 4).v)
                dve.tensor_copy(ysam[:, :, ds(b.v, 1)].rearrange("p c o -> p (c o)"), ps[:, 7, 152:156]).then_inc(d_dve, 1)
                dve.wait_ge(d_dve, b.times(6).plus(2 + 6).v)

            def head(h):
                n = h.times(NP)
                first = not (h.c or h.L)
                if not first:
                    dve.wait_ge(a_again, h.v)
                dve.tensor_copy(KA[:, :, 0:HD], QK[:, 1, :, ds(h.times(HD).v, HD)])
                dve.tensor_scalar(KA[:, :, HD + 1:HD + 2], fcum[:, :, ds(h.v, 1)], -1.0, None, ALU.mult)
                dve.tensor_copy(QA[:, :, 0:HD], QK[:, 0, :, ds(h.times(HD).v, HD)])
                dve.tensor_copy(QA[:, :, HD:HD + 1], fcum[:, :, ds(h.v, 1)]).then_inc(a_built, 1)
                dve.wait_ge(a_turned, h.times(2).plus(1).v)
                dve.tensor_copy(kT[:, :].rearrange("p (a n) -> p a n", a=2), ps[0:HD + 2, 0:2, :]).then_inc(a_k, 1)
                for p, (i, c, lo, w) in enumerate(query_pieces):
                    dve.wait_ge(a_s, n.plus(p + 1).v)
                    dve.tensor_reduce(peaks[:, i, c:c + 1], ps[:, 4 + p % 2, 0:w], X, ALU.max).then_inc(a_max, 1)
                    if p == 1 and not first:
                        sequence_sums(h.plus(-1))
                dve.wait_ge(a_max, n.plus(NP).v)
                link(dve.tensor_reduce(peak[:, :], peaks[:, :, :], X, ALU.max))
                tt(QA[:, :, HD], fcum[:, :, ds(h.v, 1)].rearrange("p b o -> p (b o)"), peak[:, :], ALU.subtract
                   ).then_inc(a_shift, 1)
                if not first:
                    sequence_scaled(h.plus(-1))
                    sequence_out(h.plus(-1))
                sequence_scores(h)

            def pair(p):
                for e in range(2):
                    head(p.times(2).plus(e))
                dve.wait_ge(a_rden, p.plus(1).v)
                dve.wait_ge(a_built, p.times(2).plus(2).v)
                tt(QK[:, 0, :, ds(p.times(P).v, P)], ps[:, 2:4, :].rearrange("p a (b n) -> p (a b) n", n=P),
                   rden[:, :].rearrange("p (b n) -> p b n", n=P), ALU.mult).then_inc(a_pair, 1)
            loop(dve, NH // 2, 1, pair, link, 24, peel=1)
            sequence_sums(V(NS - 1))
            sequence_scaled(V(NS - 1))
            sequence_out(V(NS - 1))
            for k in range(4):
                dve.wait_ge(y_hi, k + 1)
                tt(hl[:, k, :], ya[:, k, :], hh[:, k, :].bitcast(F32), ALU.subtract).then_inc(y_ready, 1)
            dve.wait_ge(y_hi, 5)
            tt(hl[:, 4:8, 0:NS], ysam[:, :, :], hh[:, 4:8, 0:NS].bitcast(F32), ALU.subtract)
            for c in range(4):
                dve.wait_ge(y_hi, 6 + c)
                cols = "p (b n) -> p b n"
                tt(hl[:, 4 + c, NS:T].rearrange(cols, n=P), QK[:, 0, :, c * P:(c + 1) * P],
                   hh[:, 4 + c, NS:T].rearrange(cols, n=P).bitcast(F32), ALU.subtract).then_inc(y_ready, 1)
            out_proj(0)
            norm(1)
            mlp(0)

            dve.memset(kdn[:, :, :, :], 0.0)
            dve.memset(wgk[:, :], 0.0).then_inc(gate_cleared, 1)
            link(dve.memset(scanm[:, :], 1.0))
            link(dve.memset(scanm[:, :].rearrange("p (c r) -> p c r", r=CHUNK)[:, :, 0:1], 0.0))
            norm(2)
            loop(dve, 8, 2, lambda i: token_tile(i.plus(13), Vo[:, :, ds(i.times(P).v, P)]))

            def gate(f):
                t = f.plus(T_IN[1] + 17)
                r = (qe, ke)[f.c % 2][:, :]
                dve.wait_ge(r_exp, f.plus(1).v)
                tt(thirds(r), thirds(r), acc(t.par), ALU.mult).then_inc(acc_free[t.par], 1)

            def two_tiles(h):
                if h.c or h.L:
                    dve.wait_ge(z_summed, h.v)
                dve.sem_inc(passed, 1)
                dve.tensor_copy(wgh[:, :], wgk[:, ds(h.times(DK).v, DK)]).then_inc(w_copied, 1)
                for j in range(2):
                    gate(h.times(2).plus(j))
                z = bcum[:, NS:T]
                dve.wait_ge(z_summed, h.plus(1).v)
                if h.c or h.L:
                    dve.wait_ge(z_stored, h.times(16).v)
                dve.sem_inc(passed, 1)
                link(dve.tensor_scalar(z.rearrange("p (a n) -> p a n", a=2), ps[:, 6:8, :], vecT[:, ds(h.plus(140).v, 1)],
                                       None, ALU.add))
                stt(out=tmp[:, 0, NS:T], in0=z, scalar=-1.0, in1=z, op0=ALU.mult, op1=ALU.min).then_inc(z_folded, 1)
                dve.wait_ge(z_logs, h.plus(1).v)
                link(stt(out=z, in0=z, scalar=0.0, in1=tmp[:, 0, NS:T], op0=ALU.min, op1=ALU.subtract))
                dve.tensor_tensor_scan(tmp[:, 0, NS:T], scanm[:, :], z, 0.0, ALU.mult, ALU.add).then_inc(z_scanned, 1)
                dve.wait_ge(z_scanned, h.plus(1).v)
            dve.wait_ge(gate_loaded, 32)
            loop(dve, NG, 1, two_tiles, link, 2, peel=1)
            all_read(dve, T_IN[1] + 25)
            dve.wait_ge(zs_summed, 1)
            for h in range(NG):
                last = dve.tensor_scalar(zs[:, h, :], ps[:, 3, NS * h:NS * (h + 1)], vecT[:, 140 + h:141 + h], None, ALU.add)
            link(last)
            stt(out=dec_s[:, :, :], in0=zs[:, :, :], scalar=-1.0, in1=zs[:, :, :], op0=ALU.mult, op1=ALU.min
                ).then_inc(zs_folded, 1)
            dve.wait_ge(zs_logs, 1)
            stt(out=zs[:, :, :], in0=zs[:, :, :], scalar=0.0, in1=dec_s[:, :, :], op0=ALU.min, op1=ALU.subtract
                ).then_inc(zs_ready, 1)
            dve.wait_ge(s_turned, 1)
            dve.tensor_copy(kvnat[:, :], ps[0:NS, 0:3, :].rearrange("p a n -> p (a n)")).then_inc(s_kv, 1)
            dve.wait_ge(s_kv, 1)
            link(dve.memset(osn[:, :], 0.0))
            for i in range(2):
                dve.wait_ge(r_stored[i], 16 * KT // 2)

            def gla_head(h):
                if h.c or h.L:
                    dve.wait_ge(g_stored, h.times(16).v)
                    dve.wait_ge(g_tr, h.times(NB).v)
                    dve.wait_ge(s_new, h.times(NS).v)
                    dve.wait_ge(gb_state, h.times(2 * NB + 1).v)
                dve.wait_ge(b_in, h.times(16).plus(16).v)
                dve.sem_inc(passed, 1)
                bc = draw.rearrange("p (c r) -> p c r", r=CHUNK)
                tt(bcum[:, NS:T].rearrange("p (c r) -> p c r", r=CHUNK),
                   bc[:, :, CHUNK - 1:CHUNK].to_broadcast([P, SEQ // CHUNK, CHUNK]), bc, ALU.subtract).then_inc(g_diff, 1)
                dve.wait_ge(g_diff, h.plus(1).v)
                dve.sem_inc(b_used, 1)
                qh = qk1[:, ds(h.times(2).v, 1), :].rearrange("p o n -> p (o n)")
                kh = qk1[:, ds(h.times(2).plus(1).v, 1), :].rearrange("p o n -> p (o n)")
                dve.memset(S[:, :], 0.0).then_inc(gb_state, 1)
                tt(kmask[:, :, :], kvnat[:, ds(h.times(DK).v, DK)].unsqueeze(1).to_broadcast([NS, NS, DK]),
                   ident[0:NS, 0:NS].unsqueeze(2).to_broadcast([NS, NS, DK]), ALU.mult)
                stt(out=qmask[:, :, :], in0=qh[:, 0:NS].unsqueeze(1).to_broadcast([P, NS, NS]), scalar=DK ** -0.5,
                    in1=eye8[:, :, :], op0=ALU.mult, op1=ALU.mult).then_inc(s_masks, 1)
                dve.wait_ge(g_act, h.times(2).plus(1).v)
                stt(out=qe[:, NS:T], in0=qh[:, NS:T], scalar=DK ** -0.5, in1=qe[:, NS:T], op0=ALU.mult, op1=ALU.mult)
                dve.wait_ge(g_act, h.times(2).plus(2).v)
                tt(ke[:, NS:T], kh[:, NS:T], ke[:, NS:T], ALU.mult)
                tt(bcum[:, NS:T], kh[:, NS:T], bcum[:, NS:T], ALU.mult).then_inc(g_dve, 1)
                def masked(b):
                    m = h.times(NB).plus(b)
                    dve.wait_ge(gb_a, m.times(2).plus(1).v)
                    if b >= 2:
                        dve.wait_ge(gb_kv, m.times(2).plus(-2).v)
                    tt(aT[:, b % 2, :], ps[:, 0, 0:P], pairmask[:, :], ALU.mult).then_inc(gb_scores, 1)

                def scaled(b):
                    m = h.times(NB).plus(b)
                    dve.wait_ge(gb_rs, m.plus(1).v)
                    if b >= 2:
                        dve.wait_ge(g_tr, m.plus(-1).v)
                    link(dve.reciprocal(ss1[:, b % 2, 1:2], ss1[:, b % 2, 1:2]))
                    stt(out=tmp[:, 0, DV * (b % 2):DV * (b % 2 + 1)], in0=ps[:, 2 + b % 2, 0:DV],
                        scalar=ss1[:, b % 2, 1:2], in1=gob[:, :], op0=ALU.mult, op1=ALU.mult).then_inc(gb_out, 1)

                def kept(b):
                    if b == 0 and not (h.c or h.L):
                        dve.wait_ge(r_in, 16)
                    dve.wait_ge(g_tr, h.times(NB).plus(b + 1).v)
                    o = (slice(None), ds(h.times(2).v, 2), slice(NS + b * P, NS + (b + 1) * P))
                    tt(qk1[o], ps[:, 6, 0:2 * P].rearrange("p (e n) -> p e n", e=2), rT[o], ALU.mult).then_inc(g_trk, 1)

                def sample_state(b):
                    n = h.times(NS).plus(b + 1)
                    dve.wait_ge(s_outer, n.v)
                    stt(out=sout[:, b, :], in0=sst[:, b, :], scalar=dec_s[:, ds(h.v, 1), b], in1=ps[:, 7, 0:DV],
                        op0=ALU.mult, op1=ALU.add).then_inc(s_new, 1)

                def sample_output(b):
                    n = h.times(NS).plus(b + 1)
                    dve.wait_ge(s_out, n.v)
                    o = osn[:, ds(h.times(DV).v, DV)]
                    tt(o, o, ps[0:NS, 7, DV:2 * DV], ALU.add).then_inc(s_added, 1)
                    dve.wait_ge(s_added, n.v)

                dve.wait_ge(s_in, h.times(16).plus(16).v)
                if h.c or h.L:
                    dve.wait_ge(gla_stored, h.times(16).v)
                masked(0)
                for b in range(NB):
                    m = h.times(NB).plus(b)
                    if b + 1 < NB:
                        masked(b + 1)
                    if b:
                        scaled(b - 1)
                    sample_state(b)
                    for c in range(2):
                        dve.wait_ge(gb_kv, m.times(2).plus(c + 1).v)
                        dve.wait_ge(gb_inter, m.times(2).plus(c + 1).v)
                        dve.wait_ge(gb_state, h.times(2 * NB + 1).plus(2 * b + c + 1).v)
                        stt(out=S[:, :], in0=S[:, :], scalar=dec[:, 2 * b + c:2 * b + c + 1], in1=ps[:, 4 + c, 0:DV],
                            op0=ALU.mult, op1=ALU.add).then_inc(gb_state, 1)
                    if b:
                        kept(b - 1)
                    sample_output(b)
                scaled(NB - 1)
                kept(NB - 1)
            dve.wait_ge(dec_s_ready, 1)
            loop(dve, NG, 1, gla_head, link, NB, peel=1)

            dve.wait_ge(g_trk, NG * NB)
            sq = kmask[:, :, :].rearrange("p a n -> p (a n)")
            link(tt(sq, osn[:, :], osn[:, :], ALU.mult))
            dve.tensor_reduce(ss8[:, :], sq.rearrange("p (h v) -> p h v", v=DV), X, ALU.add).then_inc(s_squares, 1)
            dve.wait_ge(s_rs, 1)
            o3 = osn[:, :].rearrange("p (h v) -> p h v", v=DV)
            link(tt(o3, o3, ss8[:, :].unsqueeze(2).to_broadcast([NS, NG, DV]), ALU.mult))
            tt(o3, o3, gob[0:NS, :].unsqueeze(1).to_broadcast([NS, NG, DV]), ALU.mult).then_inc(s_scaled, 1)
            dve.wait_ge(s_turned, 2)
            tt(qk1[:, :, 0:NS], ps[:, 6, 0:NS * KT].rearrange("p (k n) -> p k n", k=KT), rT[:, :, 0:NS], ALU.mult
               ).then_inc(y_s, 1)
            for k in range(KT):
                dve.wait_ge(y_hi, KT + 1 + k + 1)
                tt(hl[:, k, :], qk1[:, k, :], hh[:, k, :].bitcast(F32), ALU.subtract).then_inc(y_ready, 1)
            out_proj(1)
            norm(3)
            mlp(1)
            for b in range(NB + 1):
                dve.wait_ge(y_turned, b + 1)
                n = P if b < NB else NS
                dst = ynat[:, b, :] if b < NB else ysn[:, :]
                dve.tensor_copy(dst.rearrange("p (a n) -> p a n", a=2), ps[0:n, 2 * (b % 2):2 * (b % 2) + 2, :]
                                ).then_inc(y_kept, 1)


_INS = ["x_prompt", "x_sample", "c_prompt", "c_sample", "cache_k", "cache_v", "cache_logf", "page_table", "state_conv",
        "state_gla", "g_mix", "g_ffn", "w_ada", "b_ada", "w_in_even", "b_f", "g_q", "g_k", "w_conv", "w_out_even",
        "w_in_odd", "w_gk", "b_gk", "g_o", "w_out_odd", "w_ff1", "w_ff2"]
_OUTS = [(1, 1024, 1024), (8, 1, 1024), (1, 1, 1024, 8, 64), (1, 1, 1024, 8, 64), (1, 1, 1024, 8),
         (8, 1, 1, 8, 64), (8, 1, 1, 8, 64), (8, 1, 1, 8), (1, 1, 2, 512), (8, 1, 2, 512),
         (1, 1, 4, 128, 256), (8, 1, 4, 128, 256)]


def kernel(**inputs):
    import numpy as _np
    import concourse.bacc as _bacc
    from concourse import mybir as _mybir
    from concourse.bass_utils import run_bass_kernel_spmd as _run

    nc = _bacc.Bacc("TRN2", target_bir_lowering=False, num_devices=1)
    arrays, args = {}, []
    for name in _INS:
        a = _np.ascontiguousarray(inputs[name])
        arrays[f"in_{name}_dram"] = a
        args.append(nc.dram_tensor(f"in_{name}_dram", a.shape, _mybir.dt.from_np(a.dtype), kind="ExternalInput").ap())
    for i, shape in enumerate(_OUTS):
        args.append(nc.dram_tensor(f"out_{i}_dram", shape, _mybir.dt.float32, kind="ExternalOutput").ap())
    build(nc, *args)
    r = _run(nc, [arrays], core_ids=[0])
    return tuple(r.results[0][f"out_{i}_dram"] for i in range(len(_OUTS)))
```
